# Optimizing a Trainium2 kernel written in Bass

```python
import jax, jax.numpy as jnp
from jax import lax
import numpy as np

D_MODEL = 1024
BATCH = 1
SEQ = 512
DEPTH = 1

CTX_LEN = 256
GRID_W = 64
EXPAND = 2
D_INNER = EXPAND * D_MODEL
D_FOURIER = D_INNER // 4
FOURIER_GROUP = 64
N_FOURIER_GROUPS = D_FOURIER // FOURIER_GROUP
D_SSD = D_INNER - D_FOURIER
SSD_HEAD_DIM = 64
N_SSD_HEADS = D_SSD // SSD_HEAD_DIM
N_BC_GROUPS = 4
HEADS_PER_GROUP = N_SSD_HEADS // N_BC_GROUPS
D_STATE = 128
CONV_K = 3
CONV_CH = D_SSD + 2 * N_BC_GROUPS * D_STATE
CHUNK = 128
D_PROJ = 2 * D_FOURIER + D_SSD + CONV_CH + 2 * N_SSD_HEADS
PROJ_SPLITS = (D_FOURIER, 2 * D_FOURIER, 2 * D_FOURIER + D_SSD, 2 * D_FOURIER + D_SSD + CONV_CH)
EPS = 1e-6


def rmsnorm(x, w):
    xf = x.astype(jnp.float32)
    xf = xf * lax.rsqrt(jnp.mean(xf * xf, axis=-1, keepdims=True) + EPS)
    return xf.astype(x.dtype) * w

def segsum(a):
    cum = jnp.cumsum(a, axis=-1)
    diff = cum[..., :, None] - cum[..., None, :]
    t = a.shape[-1]
    mask = jnp.tril(jnp.ones((t, t), dtype=bool))
    return jnp.where(mask, diff, -jnp.inf)

def ssd_chunked(x, dt, A, B, C, h0):
    bsz, length, g, r, p = x.shape
    n = B.shape[-1]
    nc = length // CHUNK
    xc = (x * dt[..., None]).reshape(bsz, nc, CHUNK, g, r, p)
    bc = B.reshape(bsz, nc, CHUNK, g, n)
    cc = C.reshape(bsz, nc, CHUNK, g, n)
    a = (dt * A).reshape(bsz, nc, CHUNK, g, r).transpose(0, 3, 4, 1, 2)
    a_cum = jnp.cumsum(a, axis=-1)
    lmat = jnp.exp(segsum(a))
    cb = jnp.einsum('bclgn,bcsgn->bgcls', cc, bc)
    y_diag = jnp.einsum('bgcls,bgrcls,bcsgrp->bclgrp', cb, lmat, xc)
    decay_states = jnp.exp(a_cum[..., -1:] - a_cum)
    states = jnp.einsum('bcsgn,bgrcs,bcsgrp->bcgrpn', bc, decay_states, xc)
    states = jnp.concatenate([h0[:, None], states], axis=1)
    chunk_a = jnp.pad(a_cum[..., -1], ((0, 0), (0, 0), (0, 0), (1, 0)))
    decay_chunk = jnp.exp(segsum(chunk_a))
    new_states = jnp.einsum('bgrzc,bcgrpn->bzgrpn', decay_chunk, states)
    prev_states, h_final = new_states[:, :-1], new_states[:, -1]
    y_off = jnp.einsum('bclgn,bcgrpn,bgrcl->bclgrp', cc, prev_states, jnp.exp(a_cum))
    y = (y_diag + y_off).reshape(bsz, length, g, r, p)
    return y, h_final

def depthwise_conv_grid(u, w, bias, rows, cols):
    bsz, length, ch = u.shape
    img = u.reshape(bsz, rows, cols, ch)
    out = lax.conv_general_dilated(img, w[:, :, None, :], window_strides=(1, 1), padding='SAME',
                                   dimension_numbers=('NHWC', 'HWIO', 'NHWC'), feature_group_count=ch)
    return jax.nn.silu(out.reshape(bsz, length, ch) + bias)

def fourier_mixer(u, zf, w_f, b_f):
    bsz, length, _ = u.shape
    uf = u.astype(jnp.float32).reshape(bsz, length, N_FOURIER_GROUPS, FOURIER_GROUP)
    mixed = jnp.fft.fft2(uf, axes=(1, 3), norm='ortho').real.reshape(bsz, length, D_FOURIER)
    mixed = mixed.astype(u.dtype) @ w_f + b_f
    return mixed * jax.nn.silu(zf)

def ssd_mixer(xbc, dt_raw, zs, dt_bias, a_log, d_skip, norm_w, h0_f, h0_b):
    bsz, length, _ = xbc.shape
    f32 = jnp.float32
    g, r, p, n = N_BC_GROUPS, HEADS_PER_GROUP, SSD_HEAD_DIM, D_STATE
    xs, bm, cm = jnp.split(xbc.astype(f32), [D_SSD, D_SSD + g * n], axis=-1)
    xs = xs.reshape(bsz, length, g, r, p)
    bm = bm.reshape(bsz, length, g, n)
    cm = cm.reshape(bsz, length, g, n)
    dt = jax.nn.softplus(dt_raw.astype(f32).reshape(bsz, length, 2, N_SSD_HEADS) + dt_bias.astype(f32))
    A = -jnp.exp(a_log.astype(f32)).reshape(2, g, r)
    dt_f = dt[:, :, 0].reshape(bsz, length, g, r)
    dt_b = dt[:, :, 1].reshape(bsz, length, g, r)
    flip = lambda t: jnp.flip(t, axis=1)
    y_f, h_f = ssd_chunked(xs, dt_f, A[0], bm, cm, h0_f)
    y_b, h_b = ssd_chunked(flip(xs), flip(dt_b), A[1], flip(bm), flip(cm), h0_b)
    y = y_f + flip(y_b) + d_skip.astype(f32).reshape(g, r)[:, :, None] * xs
    gated = y.reshape(bsz, length, g, r * p) * jax.nn.silu(zs.astype(f32)).reshape(bsz, length, g, r * p)
    gated = gated * lax.rsqrt(jnp.mean(gated * gated, axis=-1, keepdims=True) + EPS)
    out = gated.reshape(bsz, length, D_SSD).astype(zs.dtype) * norm_w
    return out, h_f, h_b

def token_mixer(h, rows, cols, w_in, conv_w, conv_b, dt_bias, a_log, d_skip, ssd_norm_w,
                w_fourier, b_fourier, h0_f, h0_b):
    u, zf, zs, xbc, dt_raw = jnp.split(h @ w_in, PROJ_SPLITS, axis=-1)
    four = fourier_mixer(u, zf, w_fourier, b_fourier)
    xbc = depthwise_conv_grid(xbc, conv_w, conv_b, rows, cols)
    ssd, h_f, h_b = ssd_mixer(xbc, dt_raw, zs, dt_bias, a_log, d_skip, ssd_norm_w, h0_f, h0_b)
    return jnp.concatenate([four, ssd], axis=-1), h_f, h_b

def first_inputs(seed: int = 0) -> dict:
    key = jax.random.key(seed)
    ks = jax.random.split(key, 20)
    f32 = jnp.float32
    nrm = lambda k, shape, s: jax.random.normal(k, shape, f32) * s
    dt0 = jnp.exp(jax.random.uniform(ks[9], (DEPTH, 2, N_SSD_HEADS), f32,
                                     minval=np.log(1e-3), maxval=np.log(1e-1)))
    return {
        "x": nrm(ks[0], (BATCH, SEQ, D_MODEL), 1.0),
        "c": nrm(ks[1], (BATCH, D_MODEL), 1.0),
        "ctx": nrm(ks[2], (BATCH, CTX_LEN, D_MODEL), 1.0),
        "c_ctx": nrm(ks[3], (D_MODEL,), 1.0),
        "norm_w": 1.0 + nrm(ks[4], (DEPTH, D_MODEL), 0.05),
        "w_ada": nrm(ks[5], (DEPTH, D_MODEL, 3 * D_MODEL), 0.5 * D_MODEL ** -0.5),
        "b_ada": nrm(ks[6], (DEPTH, 3 * D_MODEL), 0.02),
        "w_in": nrm(ks[7], (DEPTH, D_MODEL, D_PROJ), D_MODEL ** -0.5),
        "conv_w": nrm(ks[8], (DEPTH, CONV_K, CONV_K, CONV_CH), 1.0 / CONV_K),
        "conv_b": nrm(ks[10], (DEPTH, CONV_CH), 0.02),
        "dt_bias": dt0 + jnp.log(-jnp.expm1(-dt0)),
        "a_log": jnp.log(jax.random.uniform(ks[11], (DEPTH, 2, N_SSD_HEADS), f32, minval=1.0, maxval=16.0)),
        "d_skip": 1.0 + nrm(ks[12], (DEPTH, N_SSD_HEADS), 0.1),
        "ssd_norm_w": 1.0 + nrm(ks[13], (DEPTH, D_SSD), 0.05),
        "w_fourier": nrm(ks[14], (DEPTH, D_FOURIER, D_FOURIER), D_FOURIER ** -0.5),
        "b_fourier": nrm(ks[15], (DEPTH, D_FOURIER), 0.02),
        "w_out": nrm(ks[16], (DEPTH, D_INNER, D_MODEL), D_INNER ** -0.5),
        "final_norm_w": 1.0 + nrm(ks[17], (D_MODEL,), 0.05),
    }

def first_block(x, c, ctx, c_ctx, norm_w, w_ada, b_ada, w_in, conv_w, conv_b, dt_bias, a_log, d_skip,
              ssd_norm_w, w_fourier, b_fourier, w_out, final_norm_w):
    bsz, seq_len, _ = x.shape
    ctx_len = ctx.shape[1]
    rows = seq_len // GRID_W
    zeros_state = jnp.zeros((bsz, N_BC_GROUPS, HEADS_PER_GROUP, SSD_HEAD_DIM, D_STATE), jnp.float32)
    silu_c = jax.nn.silu(c)
    silu_cc = jax.nn.silu(c_ctx)
    for i in range(DEPTH):
        mod = silu_c @ w_ada[i] + b_ada[i]
        shift, scale, gate = jnp.split(mod, 3, axis=-1)
        mod_c = silu_cc @ w_ada[i] + b_ada[i]
        shift_c, scale_c, gate_c = jnp.split(mod_c, 3, axis=-1)
        layer = (w_in[i], conv_w[i], conv_b[i], dt_bias[i], a_log[i], d_skip[i], ssd_norm_w[i],
                 w_fourier[i], b_fourier[i])
        hc = rmsnorm(ctx, norm_w[i]) * (1.0 + scale_c) + shift_c
        ctx_mix, h_f, h_b = token_mixer(hc, 1, ctx_len, *layer, zeros_state, zeros_state)
        hx = rmsnorm(x, norm_w[i]) * (1.0 + scale[:, None]) + shift[:, None]
        x_mix, _, _ = token_mixer(hx, rows, GRID_W, *layer, h_f, h_b)
        x = x + gate[:, None] * (x_mix @ w_out[i])
        if i < DEPTH - 1:
            ctx = ctx + gate_c * (ctx_mix @ w_out[i])
    return rmsnorm(x, final_norm_w)


DEPTH_2 = 2

HEAD_DIM = 64
HG_HEADS = 4
HG_WIDTH = HG_HEADS * HEAD_DIM
HG_CHUNK = 64
ATT_HEADS = 8
ATT_KV_HEADS = 2
ATT_WIDTH = ATT_HEADS * HEAD_DIM
ATT_KV_WIDTH = ATT_KV_HEADS * HEAD_DIM
WINDOW = 128
ROPE_THETA = 10000.0
SG_GROUPS = 4
SG_WIDTH = SG_GROUPS * HEAD_DIM
SG_CHUNK = 128

MIX_WIDTH = HG_WIDTH + ATT_WIDTH + SG_WIDTH
IN_SPLITS = (HG_WIDTH, HG_WIDTH, HG_WIDTH, HG_WIDTH,
             ATT_WIDTH, ATT_KV_WIDTH, ATT_KV_WIDTH,
             SG_WIDTH, SG_WIDTH)
IN_WIDTH = sum(IN_SPLITS)
D_FF = 2816
PLE_DIM = 256
N_NORMS = 8
MASK_VALUE = -1e30
LB_FLOOR = 1e-30


def rmsnorm_2(x, g):
    xf = x.astype(jnp.float32)
    y = xf * lax.rsqrt(jnp.mean(xf * xf, axis=-1, keepdims=True) + EPS)
    return (y * g.astype(jnp.float32)).astype(x.dtype)

def layernorm(x, g):
    xf = x.astype(jnp.float32)
    mu = jnp.mean(xf, axis=-1, keepdims=True)
    xc = xf - mu
    y = xc * lax.rsqrt(jnp.mean(xc * xc, axis=-1, keepdims=True) + EPS)
    return (y * g.astype(jnp.float32)).astype(x.dtype)

def swiglu(x, w_gu, w_down):
    gate, up = jnp.split(x @ w_gu, 2, axis=-1)
    return (jax.nn.silu(gate) * up) @ w_down

def rope(x, pos):
    half = x.shape[-1] // 2
    inv = ROPE_THETA ** (-jnp.arange(half, dtype=jnp.float32) / half)
    ang = pos.astype(jnp.float32)[..., None] * inv
    cos = jnp.cos(ang)[:, :, None, :]
    sin = jnp.sin(ang)[:, :, None, :]
    xf = x.astype(jnp.float32)
    x1, x2 = xf[..., :half], xf[..., half:]
    return jnp.concatenate([x1 * cos - x2 * sin, x2 * cos + x1 * sin], axis=-1).astype(x.dtype)

def hgrn2(q, f_raw, i, lb):
    B, S, _ = q.shape
    C = HG_CHUNK
    n = S // C
    q = q.astype(jnp.float32)
    v = i.astype(jnp.float32)
    lb = lb.astype(jnp.float32)
    logf = jnp.logaddexp(jnp.log(jnp.maximum(lb, LB_FLOOR)),
                         jnp.log1p(-lb) + jax.nn.log_sigmoid(f_raw.astype(jnp.float32)))
    k = -jnp.expm1(logf)

    def heads(t):
        return t.reshape(B, n, C, HG_HEADS, HEAD_DIM).transpose(1, 0, 3, 2, 4)

    causal = jnp.tril(jnp.ones((C, C), dtype=bool))[:, :, None]

    def step(state, inp):
        qc, kc, vc, lc = inp
        b = jnp.cumsum(lc, axis=2)
        o_inter = jnp.einsum('bhcd,bhde->bhce', qc * jnp.exp(b), state)
        diff = b[:, :, :, None, :] - b[:, :, None, :, :]
        dec = jnp.where(causal, jnp.exp(jnp.where(causal, diff, 0.0)), 0.0)
        att = jnp.einsum('bhid,bhjd,bhijd->bhij', qc, kc, dec)
        o_intra = jnp.einsum('bhij,bhje->bhie', att, vc)
        b_last = b[:, :, -1:, :]
        new_state = (jnp.exp(b_last[:, :, 0, :])[..., None] * state
                     + jnp.einsum('bhcd,bhce->bhde', kc * jnp.exp(b_last - b), vc))
        return new_state, o_inter + o_intra

    s0 = jnp.zeros((B, HG_HEADS, HEAD_DIM, HEAD_DIM), jnp.float32)
    _, o = lax.scan(step, s0, (heads(q), heads(k), heads(v), heads(logf)))
    return o.transpose(1, 0, 3, 2, 4).reshape(B, S, HG_HEADS, HEAD_DIM)

def swa_sink_attention(q, k, v, sinks, pos):
    B, S, _ = q.shape
    G = ATT_HEADS // ATT_KV_HEADS
    nb = S // WINDOW
    q = rope(q.reshape(B, S, ATT_HEADS, HEAD_DIM), pos)
    k = rope(k.reshape(B, S, ATT_KV_HEADS, HEAD_DIM), pos)
    v = v.reshape(B, S, ATT_KV_HEADS, HEAD_DIM)
    qb = q.reshape(B, nb, WINDOW, ATT_KV_HEADS, G, HEAD_DIM)

    def with_prev(t):
        t = t.reshape(B, nb, WINDOW, ATT_KV_HEADS, HEAD_DIM)
        prev = jnp.concatenate([jnp.zeros_like(t[:, :1]), t[:, :-1]], axis=1)
        return jnp.concatenate([prev, t], axis=2)

    kk, vv = with_prev(k), with_prev(v)
    s = jnp.einsum('bnqkgd,bnskd->bnkgqs', qb, kk).astype(jnp.float32) * (HEAD_DIM ** -0.5)
    qi = jnp.arange(WINDOW)[:, None]
    sj = jnp.arange(2 * WINDOW)[None, :]
    rel = qi + WINDOW - sj
    band = (rel >= 0) & (rel < WINDOW)
    exists = (jnp.arange(nb)[:, None, None] * WINDOW + sj[None] - WINDOW) >= 0
    mask = (band[None] & exists)[None, :, None, None]
    s = jnp.where(mask, s, MASK_VALUE)
    sink = sinks.astype(jnp.float32).reshape(1, 1, ATT_KV_HEADS, G, 1, 1)
    m = jnp.maximum(jnp.max(s, axis=-1, keepdims=True), sink)
    pr = jnp.where(mask, jnp.exp(s - m), 0.0)
    denom = jnp.sum(pr, axis=-1, keepdims=True) + jnp.exp(sink - m)
    o = jnp.einsum('bnkgqs,bnskd->bnqkgd', (pr / denom).astype(v.dtype), vv)
    return o.reshape(B, S, ATT_WIDTH)

def spatial_gating(u, v, ln_g, w_s, b_s):
    B, S, _ = u.shape
    nc = S // SG_CHUNK
    u = jax.nn.gelu(u)
    v = layernorm(jax.nn.gelu(v), ln_g)
    vg = v.reshape(B, nc, SG_CHUNK, SG_GROUPS, HEAD_DIM)
    w = w_s * jnp.tril(jnp.ones((SG_CHUNK, SG_CHUNK), w_s.dtype))
    mix = jnp.einsum('gts,bnsgd->bntgd', w, vg) + b_s.T[:, :, None]
    return (u.reshape(B, nc, SG_CHUNK, SG_GROUPS, HEAD_DIM) * mix).reshape(B, S, SG_WIDTH)

def hybrid_layer(h, p_i, pos, lb, norm_g, w_in, w_out, ffn1_gu, ffn1_down, ffn2_gu, ffn2_down,
                 hg_norm_g, sinks, sg_ln_g, sg_w, sg_b, ple_proj, ple_gate):
    B, S, _ = h.shape
    h = h + 0.5 * rmsnorm_2(swiglu(rmsnorm_2(h, norm_g[0]), ffn1_gu, ffn1_down), norm_g[1])
    z = rmsnorm_2(h, norm_g[2]) @ w_in
    idx = [int(c) for c in np.cumsum(IN_SPLITS)[:-1]]
    hq, hf, hi, hg, aq, ak, av, su, sv = jnp.split(z, idx, axis=-1)
    o_a = hgrn2(hq, hf, hi, lb)
    o_a = rmsnorm_2(o_a, hg_norm_g) * jax.nn.sigmoid(hg.astype(jnp.float32).reshape(B, S, HG_HEADS, HEAD_DIM))
    o_a = o_a.reshape(B, S, HG_WIDTH).astype(h.dtype)
    o_b = swa_sink_attention(aq, ak, av, sinks, pos).astype(h.dtype)
    o_c = spatial_gating(su, sv, sg_ln_g, sg_w, sg_b).astype(h.dtype)
    mixed = jnp.concatenate([o_a, o_b, o_c], axis=-1) @ w_out
    h = h + rmsnorm_2(mixed, norm_g[3])
    h = h + 0.5 * rmsnorm_2(swiglu(rmsnorm_2(h, norm_g[4]), ffn2_gu, ffn2_down), norm_g[5])
    gate = jax.nn.sigmoid(rmsnorm_2(h, norm_g[6]) @ ple_gate)
    h = h + rmsnorm_2((p_i @ ple_proj) * gate, norm_g[7])
    return h

def second_inputs(seed: int = 0) -> dict:
    key = jax.random.key(seed)
    ks = jax.random.split(key, 20)

    def nrm(k, shape, scale):
        return jax.random.normal(k, shape, jnp.float32) * scale

    x = nrm(ks[0], (BATCH, SEQ, D_MODEL), 1.0)
    p = nrm(ks[1], (DEPTH_2, BATCH, SEQ, PLE_DIM), 1.0)
    positions = (jnp.arange(SEQ, dtype=jnp.int32)[None, :]
                 + jax.random.randint(ks[2], (BATCH, 1), 0, 1024, dtype=jnp.int32))
    return {
        "x": x,
        "p": p,
        "positions": positions,
        "norm_gains": 1.0 + nrm(ks[3], (DEPTH_2, N_NORMS, D_MODEL), 0.05),
        "w_in": nrm(ks[4], (DEPTH_2, D_MODEL, IN_WIDTH), D_MODEL ** -0.5),
        "w_out": nrm(ks[5], (DEPTH_2, MIX_WIDTH, D_MODEL), MIX_WIDTH ** -0.5),
        "ffn1_gate_up": nrm(ks[6], (DEPTH_2, D_MODEL, 2 * D_FF), D_MODEL ** -0.5),
        "ffn1_down": nrm(ks[7], (DEPTH_2, D_FF, D_MODEL), D_FF ** -0.5),
        "ffn2_gate_up": nrm(ks[8], (DEPTH_2, D_MODEL, 2 * D_FF), D_MODEL ** -0.5),
        "ffn2_down": nrm(ks[9], (DEPTH_2, D_FF, D_MODEL), D_FF ** -0.5),
        "hgrn_lb_logits": nrm(ks[10], (DEPTH_2, HG_WIDTH), 0.5),
        "hgrn_norm_gain": 1.0 + nrm(ks[11], (DEPTH_2, HEAD_DIM), 0.05),
        "attn_sinks": nrm(ks[12], (DEPTH_2, ATT_HEADS), 0.5),
        "sg_ln_gain": 1.0 + nrm(ks[13], (DEPTH_2, SG_WIDTH), 0.05),
        "sg_spatial_w": nrm(ks[14], (DEPTH_2, SG_GROUPS, SG_CHUNK, SG_CHUNK), SG_CHUNK ** -0.5),
        "sg_spatial_b": 1.0 + nrm(ks[15], (DEPTH_2, SG_GROUPS, SG_CHUNK), 0.1),
        "ple_proj": nrm(ks[16], (DEPTH_2, PLE_DIM, D_MODEL), PLE_DIM ** -0.5),
        "ple_gate": nrm(ks[17], (DEPTH_2, D_MODEL, D_MODEL), D_MODEL ** -0.5),
    }

def second_block(x, p, positions, norm_gains, w_in, w_out, ffn1_gate_up, ffn1_down, ffn2_gate_up,
              ffn2_down, hgrn_lb_logits, hgrn_norm_gain, attn_sinks, sg_ln_gain, sg_spatial_w,
              sg_spatial_b, ple_proj, ple_gate):
    probs = jax.nn.softmax(hgrn_lb_logits.astype(jnp.float32), axis=0)
    lower_bounds = jnp.cumsum(probs, axis=0) - probs[0]
    h = x
    for l in range(DEPTH_2):
        h = hybrid_layer(h, p[l], positions, lower_bounds[l], norm_gains[l], w_in[l], w_out[l],
                         ffn1_gate_up[l], ffn1_down[l], ffn2_gate_up[l], ffn2_down[l],
                         hgrn_norm_gain[l], attn_sinks[l], sg_ln_gain[l], sg_spatial_w[l],
                         sg_spatial_b[l], ple_proj[l], ple_gate[l])
    return h


def setup_inputs(seed=0):
    out = dict(first_inputs(seed))
    for name, value in second_inputs(seed + 1).items():
        if name != "x":
            out[name + "_2"] = value
    return out


def reference(
    x, c, ctx, c_ctx, norm_w, w_ada, b_ada, w_in, conv_w, conv_b, dt_bias, a_log, d_skip,
    ssd_norm_w, w_fourier, b_fourier, w_out, final_norm_w, p_2, positions_2, norm_gains_2,
    w_in_2, w_out_2, ffn1_gate_up_2, ffn1_down_2, ffn2_gate_up_2, ffn2_down_2, hgrn_lb_logits_2,
    hgrn_norm_gain_2, attn_sinks_2, sg_ln_gain_2, sg_spatial_w_2, sg_spatial_b_2, ple_proj_2,
    ple_gate_2,
):
    x = first_block(
        x, c, ctx, c_ctx, norm_w, w_ada, b_ada, w_in, conv_w, conv_b, dt_bias, a_log, d_skip,
        ssd_norm_w, w_fourier, b_fourier, w_out, final_norm_w,
    )
    return second_block(
        x, p_2, positions_2, norm_gains_2, w_in_2, w_out_2, ffn1_gate_up_2, ffn1_down_2,
        ffn2_gate_up_2, ffn2_down_2, hgrn_lb_logits_2, hgrn_norm_gain_2, attn_sinks_2,
        sg_ln_gain_2, sg_spatial_w_2, sg_spatial_b_2, ple_proj_2, ple_gate_2,
    )


_drawn_inputs = setup_inputs


def setup_inputs(seed=0):
    import zlib

    import numpy as np

    out = dict(_drawn_inputs(seed))
    spreads = {}
    factors = {'ctx': 8.0,
     'c_ctx': 8.0,
     'conv_b': 4.689,
     'd_skip': 4.04,
     'ssd_norm_w': 2.971,
     'b_fourier': 24.215,
     'attn_sinks_2': 8.0,
     'sg_ln_gain_2': 3.16,
     'hgrn_norm_gain_2': 3.584}
    for name, (base, spread) in spreads.items():
        noise = np.random.default_rng([zlib.crc32(name.encode()), seed]).standard_normal(out[name].shape)
        drawn = base * np.exp(spread * noise) if base else spread * noise
        out[name] = __import__('jax').numpy.asarray(drawn.astype(out[name].dtype))
    for name, factor in factors.items():
        out[name] = (out[name] * factor).astype(out[name].dtype)
    return out
```

```python
from contextlib import ExitStack

import numpy as np

import concourse.bass as bass
from concourse import mybir

F32 = mybir.dt.float32
F32R = mybir.dt.float32r
I32 = mybir.dt.int32
U8 = mybir.dt.uint8
ALU = mybir.AluOpType
ACT = mybir.ActivationFunctionType
AX = mybir.AxisListType

P = 128
SEQ = 512
CTX = 256
D = 1024
KT = D // P
EPS = 1e-6
SLOTS = 4
UNIT = 8

DEPTH = 2
FF = 2816
FT = FF // P
IN_T = 2304 // P
PLE = 256
SCALE = 64 ** -0.5
MASK_VALUE = -1e30
LB_FLOOR = 1e-30
PLE_T = PLE // P

D_FOUR = 512
D_SSD = 1536
HEADS = 24
GROUPS = 4
GRID_W = 64
ROWS = SEQ // GRID_W
FT4 = D_FOUR // P
ST = D_SSD // P
ADA_T = 3 * KT
DT_ROWS = 2 * HEADS

MIX_T = FT4 + ST
DT0, B0, XS0, C0, U0, ZF0, IN1A_T = 0, 1, 5, 17, 21, 25, 29
STREAM = [("ada", ADA_T, KT), ("in1a", IN1A_T, KT), ("in1b", ST, KT), ("four", FT4, FT4), ("out1", KT, MIX_T)]
for _layer in range(DEPTH):
    STREAM += [(("gu", _layer, 0), 2 * FT, KT), (("down", _layer, 0), KT, FT),
               (("in2", _layer), IN_T, KT), (("out2", _layer), KT, KT),
               (("gu", _layer, 1), 2 * FT, KT), (("down", _layer, 1), KT, FT),
               (("gate", _layer), KT, KT), (("proj", _layer), KT, PLE_T)]


def stream_plan(stages):
    first, tile, block, tiles = {}, {}, 0, 0
    for name, n, k in stages:
        first[name], tile[name] = block, tiles
        block += n * k
        tiles += n
    units = -(-block // UNIT)
    return first, tile, -(-units // SLOTS) * SLOTS


class Events:

    def __init__(self, nc, ctx, counted):
        self.nc, self.ctx, self.counted = nc, ctx, counted
        self.sems, self.n, self.values, self.freed = {}, {}, {}, {}

    def sem(self, name):
        if name not in self.sems:
            self.sems[name] = self.ctx.enter_context(self.nc.semaphore(name))
            self.n[name] = 0
        return self.sems[name]

    def done(self, name, *keys, bank_of=None):
        s = self.sem(name)
        self.n[name] += 1
        for key in keys:
            assert (name, key) not in self.values, (name, key)
            self.values[name, key] = self.n[name]
        if bank_of is not None:
            self.freed[bank_of] = (name, self.n[name])
        return s, 1

    def after(self, name, key):
        if self.counted is None:
            return self.sem(name), 1
        return self.sem(name), self.counted[0][name, key]

    def bank_free(self, tile):
        if self.counted is None:
            return None
        name, value = self.counted[1][tile]
        return self.sem(name), value


LEVELS = [1, 2, 4, 8, 16, 32, 64]
C_ID, C_ONE, C_BLK, C_ROT, C_TRI, C_NEGF, C_NEGB = range(0, 7 * P, P)
C_AMASK = 7 * P
C_INV = C_AMASK + 2 * P
C_SEL = C_INV + 1
C_COLS = C_SEL + 1


def fixed_tables():
    p, f = np.arange(P)[:, None], np.arange(P)[None, :]
    table = np.zeros((P, C_COLS), np.float32)
    table[:, C_ID:C_ID + P] = p == f
    table[:, C_ONE:C_ONE + P] = 1.0
    table[:, C_BLK:C_BLK + P] = p // 64 == f // 64
    table[:, C_ROT:C_ROT + P] = (p == f - 32) * (f % 64 >= 32) * 1.0 - (p == f + 32) * (f % 64 < 32) * 1.0
    table[:, C_TRI:C_TRI + P] = p <= f
    table[:, C_NEGF:C_NEGF + P] = np.where(f >= p, 0.0, MASK_VALUE)
    table[:, C_NEGB:C_NEGB + P] = np.where(f <= p, 0.0, MASK_VALUE)
    j = np.arange(2 * P)[None, :]
    table[:, C_AMASK:C_AMASK + 2 * P] = np.where((p + P - j >= 0) & (p + P - j < P), 0.0, MASK_VALUE)
    table[:, C_INV] = 10000.0 ** (-(np.arange(P) % 32).astype(np.float32) / np.float32(32))
    table[:, C_SEL] = np.arange(P) < HEADS
    levels = np.zeros((P, len(LEVELS) + 1, P), np.float32)
    levels[:, 0] = p == f
    for n, b in enumerate(LEVELS):
        levels[:, n + 1] = (p // (2 * b) == f // (2 * b)) & (p % (2 * b) < b) & (f % (2 * b) >= b)
    t, c = np.arange(SEQ), np.arange(64)
    full = 2 * np.pi * np.outer(t, t) / SEQ
    part = 2 * np.pi * np.outer(c, c) / 64
    norm = 1.0 / np.sqrt(SEQ * 64.0)
    blocks = np.zeros((P, 2, P))
    for h in range(2):
        s = slice(64 * h, 64 * h + 64)
        blocks[s, 0, s], blocks[s, 1, s] = np.cos(part), np.sin(part)
    dft_c = blocks.reshape(P, 2 * P).astype(np.float32)
    dft_t = np.stack([np.cos(full) * norm, -np.sin(full) * norm])
    dft_t = dft_t.reshape(2, SEQ // P, P, SEQ).transpose(2, 0, 1, 3).astype(np.float32)
    return table, levels.reshape(P, -1), dft_c, np.ascontiguousarray(dft_t.reshape(P, -1))


P2_NORM, P2_HG, P2_LB, P2_LN, P2_SINK = 0, 64, 65, 69, 71
P2_COLS = 79
M2_SGB, M2_SGW, M2_COLS = 0, 2 * P, 2 * P + 4 * P
P1_NORM, P1_ADA, P1_CONV, P1_CB, P1_SSD, P1_BF = 0, 8, 32, 32 + 180, 32 + 180 + 20, 32 + 180 + 32
P1_FIN, P1_C, P1_D, P1_DTB = P1_BF + 4, P1_BF + 12, P1_BF + 28, P1_BF + 52
P1_COLS = P1_DTB + 2


def build(nc, a, out, counted, stages, blocks=(1, 2)):
    first_block, first_tile, units = stream_plan(stages)
    ctx = ExitStack()
    with ctx:
        ev = Events(nc, ctx, counted)
        done, after, bank_free = ev.done, ev.after, ev.bank_free
        base = -(-nc.sbuf_base // 32) * 32

        def at(name, offset, shape, dt=F32):
            return nc.alloc_sbuf_tensor_at(name, [P, *shape], dt, offset=base + offset)

        def loads(*names):
            return {n: ctx.enter_context(nc.semaphore(f"loaded_{n}")) for n in names}

        KB = 1024
        raw = at("raw", 0, [SLOTS, UNIT, P])
        whi = at("whi", 16 * KB, [SLOTS, UNIT, P], F32R)
        wlo = at("wlo", 32 * KB, [SLOTS, UNIT, P], F32R)
        xhi = at("xhi", 48 * KB, [KT, SEQ], F32R)
        xlo = at("xlo", 64 * KB, [KT, SEQ], F32R)
        y_over_x = at("y_over_x", 48 * KB, [KT, SEQ])
        h = at("h", 80 * KB, [KT, SEQ])
        CONST = 96 * KB
        DYN = CONST + 15 * KB
        table = at("table", CONST, [C_COLS])
        masks = at("masks", CONST + 5 * KB, [len(LEVELS) + 1, P], U8)
        masks_f = at("masks_f", DYN + 28 * KB, [len(LEVELS) + 1, P])
        par2 = at("par2", CONST + 6 * KB, [DEPTH, P2_COLS])
        lower = at("lower", CONST + 6 * KB + 640, [DEPTH, 2, 2])
        small = at("small", CONST + 6 * KB + 704, [80])
        cos_t = at("cos_t", CONST + 7 * KB, [SEQ])
        sin_t = at("sin_t", CONST + 9 * KB, [SEQ])
        inv_rms = at("inv_rms", CONST + 11 * KB, [SEQ])
        sq_sum = at("sq_sum", CONST + 13 * KB, [SEQ])
        tmp = [at(f"tmp{i}", DYN + 88 * KB + 2 * KB * i, [SEQ]) for i in range(3)]
        SM = DYN + 94 * KB
        act_hi = at("act_hi", DYN, [FT, SEQ], F32R)
        act_lo = at("act_lo", DYN + 44 * KB, [FT, SEQ], F32R)
        y_dyn = at("y_dyn", DYN, [KT, SEQ])
        z = at("z", DYN, [IN_T, SEQ])
        mixpar = at("mixpar", DYN + 36 * KB, [M2_COLS])
        MX = DYN + 39 * KB
        gate_b = at("gate_b", MX, [2, SEQ])
        key_k = at("key_k", MX + 4 * KB, [2, SEQ])
        diff = at("diff", MX + 8 * KB, [2, SEQ])
        q_dec = at("q_dec", MX + 12 * KB, [2, SEQ])
        k_dec = at("k_dec", MX + 16 * KB, [2, SEQ])
        hg_att = at("hg_att", MX + 20 * KB, [4, SEQ])
        k_tok = at("k_tok", MX + 28 * KB, [2, 4, P])
        v_tok = at("v_tok", MX + 32 * KB, [2, 4, P])
        state = at("state", MX + 36 * KB, [3, 2, P])
        tot = at("tot", MX + 48 * KB, [2, 4])
        e_tot = at("e_tot", MX + 48 * KB + 32, [2, 4])
        hg_o = at("hg_o", MX + 40 * KB, [2, SEQ])
        va_tok = at("va_tok", MX, [4, P])
        scores = [at(f"scores{i}", MX + 2 * KB * (8 + i), [2, 2 * P]) for i in range(3)]
        probs_t = [at(f"probs_t{i}", MX + 2 * KB * (3 + i), [2, 2, P]) for i in range(2)]
        att_o = [at(f"att_o{i}", MX + 2 * KB * (5 + i), [SEQ]) for i in range(2)]
        stat = [at(f"stat{i}", MX + 14 * KB + 64 * i, [7, 2]) for i in range(3)]
        ln_x = at("ln_x", MX, [2, SEQ])
        sg_tok = at("sg_tok", MX + 4 * KB, [4, 2 * P])
        sg_w = at("sg_w", MX + 8 * KB, [4, P])
        sg_o = at("sg_o", MX + 10 * KB, [2, SEQ])
        ln_sq = at("ln_sq", MX + 14 * KB, [2, SEQ])
        ctx_raw = at("ctx_raw", DYN + 56 * KB, [KT, CTX])
        ctx_hi = at("ctx_hi", DYN + 40 * KB, [KT, CTX], F32R)
        ctx_lo = at("ctx_lo", DYN + 48 * KB, [KT, CTX], F32R)
        x_sq = at("x_sq", DYN, [KT, SEQ])
        ctx_sq = at("ctx_sq", DYN + 16 * KB, [KT, CTX])
        x_scaled = at("x_scaled", DYN, [KT, SEQ])
        ctx_scaled = at("ctx_scaled", DYN + 64 * KB, [KT, CTX])
        x_tok = at("x_tok", DYN, [4, D_SSD])
        b_x = at("b_x", DYN + 24 * KB, [4, SEQ])
        c_x = at("c_x", DYN + 32 * KB, [4, SEQ])
        zs = at("zs", DYN + 40 * KB, [ST, SEQ])
        ctx_weighted = at("ctx_weighted", DYN + 40 * KB, [2, D_SSD])
        dt = [at(f"dt{i}", DYN + (52 + 3 * i) * KB, [SEQ + CTX]) for i in range(4)]
        dt_raw = at("dt_raw", 80 * KB + 8 * KB, [SEQ + CTX])
        ctx_tok = at("ctx_tok", DYN + 64 * KB, [2, D_SSD])
        ctx_b_tok = at("ctx_b_tok", DYN + 76 * KB, [2, 4 * P])
        conv = [at(f"conv{i}", DYN + (80 + 3 * i) * KB, [SEQ + CTX]) for i in range(2)]
        zf = at("zf", DYN + 80 * KB, [FT4, SEQ])
        cum = at("cum", CONST + 7 * KB, [SEQ + CTX])
        dft_c = at("dft_c", CONST + 10 * KB, [2 * P])
        u_in = at("u_in", 80 * KB, [FT4, SEQ])
        h0 = [at("h0_f", 88 * KB, [D_SSD]), at("h0_b", DYN + 64 * KB, [D_SSD])]
        dft_t = at("dft_t", 48 * KB, [2, 4, SEQ])
        four_tok = at("four_tok", 64 * KB, [4, FT4, 2, P])
        four_hi = at("four_hi", 80 * KB, [FT4, SEQ], F32R)
        four_lo = at("four_lo", DYN + 71 * KB, [FT4, SEQ], F32R)
        cum_hi = at("cum_hi", 80 * KB, [SEQ], F32R)
        cum_lo = at("cum_lo", 82 * KB, [SEQ], F32R)
        ident_r = at("ident_r", 84 * KB, [P], F32R)
        cbt = at("cbt", 48 * KB, [4, SEQ])
        diag = [at(f"diag{i}", (56 + 4 * i) * KB, [2, 4, P]) for i in range(2)]
        decay_all = [at(f"decay{i}", (64 + 8 * i) * KB, [4 * (SEQ + P)]) for i in range(2)]
        decay = [d[:, 0:4 * SEQ].rearrange("p (i t) -> p i t", t=SEQ) for d in decay_all]
        decay_d = [d[:, :].rearrange("p (i t) -> p i t", t=SEQ + P)[:, :, 0:P] for d in decay_all]
        c_dec = [at(f"c_dec{i}", DYN + (76 - 4 * i) * KB, [2, SEQ]) for i in range(2)]
        mix_hi2 = at("mix_hi2", DYN, [MIX_T - KT, SEQ], F32R)
        mix_lo2 = at("mix_lo2", DYN + 16 * KB, [MIX_T - KT, SEQ], F32R)
        par1 = at("par1", SM, [P1_COLS])
        mod = at("mod", SM + 1216, [ADA_T, 2])
        in_scale = at("in_scale", SM + 1408, [KT, 2])
        bias_tok = at("bias_tok", SM + 1472, [4, DT_ROWS])
        ctx_w_tok = at("ctx_w_tok", SM + 2240, [2, DT_ROWS])
        dt_small = at("dt_small", SM + 2624, [8])
        c_silu = at("c_silu", DYN + 24 * KB, [KT, 2])
        c_hi = at("c_hi", DYN + 24 * KB + 64, [KT, 2], F32R)
        c_lo = at("c_lo", DYN + 24 * KB + 128, [KT, 2], F32R)
        ple_raw = at("ple_raw", DYN + 16 * KB, [PLE_T, SEQ])
        ple_hi = at("ple_hi", DYN + 20 * KB, [PLE_T, SEQ], F32R)
        ple_lo = at("ple_lo", DYN + 24 * KB, [PLE_T, SEQ], F32R)

        ident = table[:, C_ID:C_ID + P]
        ones = table[:, C_ONE:C_ONE + P]
        blk64 = table[:, C_BLK:C_BLK + P]
        rot = table[:, C_ROT:C_ROT + P]

        banks = ctx.enter_context(nc.psum_tensor("banks", [P, 8, SEQ], F32))
        bank = [banks[:, i] for i in range(8)]
        acc = bank[:4]
        norm_bank = bank[4]
        mix_bank = bank[5:]
        turn_bank = [norm_bank, mix_bank[2]]
        ctx_bank = [norm_bank, mix_bank[0]]

        raw_loaded = [ctx.enter_context(nc.semaphore(f"raw_loaded{i}")) for i in range(SLOTS)]
        unit_split = ctx.enter_context(nc.semaphore("unit_split"))
        ld = loads("par1", "ctx", "dft_c", "dft_t", "x_again", "table", "masks", "par2", "pos", "h", *[f"mix{i}" for i in range(DEPTH)],
                   *[f"ple{i}" for i in range(DEPTH)])
        stored = ctx.enter_context(nc.semaphore("stored"))

        block = ctx.enter_context(nc.Block())

        @block.sync
        def _(sp):
            for i in range(SLOTS):
                sp.dma_start(raw[:, i], a["stream"][i]).then_inc(raw_loaded[i], 16)
            with sp.Fori(1, units // SLOTS) as r:
                for i in range(SLOTS):
                    sp.wait_ge(unit_split, r * SLOTS + (i + 1 - SLOTS))
                    sp.dma_start(raw[:, i], a["stream"][r * SLOTS + i]).then_inc(raw_loaded[i], 16)
            sp.wait_ge(*after("h_new", ("last", KT - 1)))
            sp.dma_start(out, h[:, :, :]).then_inc(stored, 16)
            sp.wait_ge(stored, 16)

        @block.gpsimd
        def _(pool):
            unit_high = ev.sem("unit_high")
            with pool.Fori(0, units // SLOTS) as r:
                for i in range(SLOTS):
                    pool.wait_ge(unit_high, r * SLOTS + (i + 1))
                    pool.tensor_tensor(wlo[:, i], raw[:, i], whi[:, i].bitcast(F32), ALU.subtract)\
                        .then_inc(unit_split, 1)

        def mix1(t):
            return zf[:, t] if t < FT4 else zs[:, t - FT4]

        def mix1_hi(t):
            return xhi[:, t] if t < KT else mix_hi2[:, t - KT]

        def mix1_lo(t):
            return xlo[:, t] if t < KT else mix_lo2[:, t - KT]

        def units_to(q):
            layer, n = q
            return first_block[(("gu", layer, 0), ("in2", layer), ("gu", layer, 1), ("gate", layer))[n]] // UNIT

        @block.scalar
        def _(act):
            cast = [0]

            def high_parts(upto):
                while cast[0] < min(upto, units):
                    u = cast[0]
                    act.wait_ge(raw_loaded[u % SLOTS], 16 * (u // SLOTS + 1))
                    if u >= SLOTS:
                        act.wait_ge(*after("product", ("unit", u - SLOTS)))
                    act.activation(whi[:, u % SLOTS], raw[:, u % SLOTS], ACT.Copy)\
                        .then_inc(*done("unit_high", ("unit", u)))
                    cast[0] += 1

            def tile_ready(stage, m, k):
                last = (first_block[stage] + (m + 1) * k - 1) // UNIT
                high_parts(last + SLOTS)
                act.wait_ge(*after("product", (stage, m)))

            def squares(name, q, k, src, bank_of=None):
                dst = sq_sum[:] if k == 0 else tmp[1 + k % 2][:]
                if k >= 3:
                    act.wait_ge(*after("sq_added", (name, q, k - 2)))
                act.activation(dst, src, ACT.Square).then_inc(*done(name, (q, k), bank_of=bank_of))

            def norm_in(q, gain):
                high_parts(units_to(q) + SLOTS)
                for k in range(KT):
                    act.wait_ge(*after("h_new", (q, k)))
                    act.activation(xhi[:, k], h[:, k], ACT.Copy, scale=gain[:, k:k + 1])\
                        .then_inc(*done("x_high", (q, k)))
                    squares("h_sq", q, k, h[:, k])

            def inverse_root(key, n, src=None, dst=None):
                dst = inv_rms[:] if dst is None else dst
                act.wait_ge(*after("summed", key))
                act.activation(dst, norm_bank[:] if src is None else src, ACT.Ln, scale=1.0 / n, bias=eps)\
                    .then_inc(*done("log", key))
                act.wait_ge(*after("log", key))
                act.activation(dst, dst, ACT.Exp, scale=-0.5).then_inc(*done("inverse", key))

            def y_out(stage, q, k, y):
                for m in range(KT):
                    tile_ready(stage, m, k)
                    t = first_tile[stage] + m
                    act.activation(y[:, m], acc[t % 4][:], ACT.Copy).then_inc(*done("y_copied", (q, m)))
                    squares("y_sq", q, m, acc[t % 4][:], bank_of=t)
                inverse_root(("post", q), D)

            def mix_high(layer, t, src):
                act.activation(xhi[:, t], src, ACT.Copy).then_inc(*done("mix_high", (layer, t)))

            def hgrn(layer):
                act.wait_ge(*after("z", (layer, 3)))
                act.activation(gate_b[:, :, :], z[:, 2:4], ACT.Sigmoid)
                act.activation(key_k[:, :, :], z[:, 2:4], ACT.Sigmoid, scale=-1.0).then_inc(*done("hg_sig", layer))
                act.wait_ge(*after("z", (layer, 7)))
                act.activation(z[:, 6:8], z[:, 6:8], ACT.Sigmoid).then_inc(*done("hg_out_gate", layer))
                for g in range(2):
                    act.wait_ge(*after("hg_vt", (layer, g)))
                    act.activation(v_tok[:, g], mix_bank[g][:].rearrange("p (n f) -> p n f", f=P), ACT.Copy)\
                        .then_inc(*done("hg_vtok", (layer, g)))
                act.wait_ge(*after("hg_ln_in", layer))
                act.activation(diff[:, :, :], diff[:, :, :], ACT.Ln)
                act.activation(q_dec[:, :, :], q_dec[:, :, :], ACT.Ln).then_inc(*done("hg_ln", layer))
                for n, b in enumerate(LEVELS, 1):
                    act.wait_ge(*after("hg_diff", (layer, n)))
                    d = diff[:, :, :].rearrange("p g (r s) -> p (g r) s", s=2 * b)
                    act.activation(d[:, :, b:2 * b], d[:, :, b:2 * b], ACT.Exp)
                    act.activation(d[:, :, 0:b], d[:, :, 0:b], ACT.Exp, scale=-1.0)\
                        .then_inc(*done("hg_exp", (layer, n)))
                act.wait_ge(*after("hg_diff", (layer, "end")))
                act.activation(diff[:, :, :], diff[:, :, :], ACT.Exp)
                act.activation(e_tot[:, :, :], tot[:, :, :], ACT.Exp)
                act.activation(gate_b[:, :, :], gate_b[:, :, :], ACT.Exp).then_inc(*done("hg_exp", (layer, "end")))
                for g in range(2):
                    act.wait_ge(*after("hg_kt", (layer, g)))
                    act.activation(k_tok[:, g], bank[4 + g][:].rearrange("p (n f) -> p n f", f=P), ACT.Copy)\
                        .then_inc(*done("hg_ktok", (layer, g)))
                for g in range(2):
                    act.wait_ge(*after("hg_o", (layer, g)))
                    act.activation(hg_o[:, g], acc[2 + g][:], ACT.Copy).then_inc(*done("hg_o_copied", (layer, g)))
                    act.activation(diff[:, g], acc[2 + g][:], ACT.Square).then_inc(*done("hg_o_sq", (layer, g)))
                for g in range(2):
                    inverse_root((layer, "hg", g), 64, mix_bank[g][:], k_dec[:, g])
                for g in range(2):
                    act.wait_ge(*after("mix_out", (layer, g)))
                    mix_high(layer, g, hg_o[:, g])

            def attention(layer):
                act.wait_ge(*after("att_vt", layer))
                act.activation(va_tok[:, :, :], mix_bank[2][:].rearrange("p (n f) -> p n f", f=P), ACT.Copy)\
                    .then_inc(*done("att_vtok", layer))

                def exps(i):
                    w0 = P if i % 4 == 0 else 0
                    st, sc = stat[i % 3], scores[i % 3]
                    act.wait_ge(*after("att_shift", (layer, i)))
                    for e in range(2):
                        act.activation(sc[:, e, w0:], sc[:, e, w0:], ACT.Exp, bias=st[:, 1, e:e + 1],
                                       accum_out=st[:, 3, e:e + 1])
                    act.activation(st[:, 4], st[:, 2], ACT.Exp).then_inc(*done("att_exp", (layer, i)))

                def turned(i):
                    k0 = 1 if i % 4 == 0 else 0
                    act.wait_ge(*after("att_turned", (layer, i)))
                    act.activation(probs_t[i % 2][:, :, k0:], turn_bank[i % 2][:].rearrange(
                        "p (e k f) -> p e k f", e=2, f=P)[:, :, k0:], ACT.Copy).then_inc(*done("att_pt", (layer, i)))

                def heads_out(t):
                    act.wait_ge(*after("att_o", (layer, t)))
                    mix_high(layer, 2 + t, mix_bank[t % 2][:])

                for i in range(16 + 2):
                    if i < 16:
                        exps(i)
                    if 1 <= i <= 16:
                        turned(i - 1)
                    if i >= 5 and (i - 5) % 4 == 0:
                        heads_out((i - 5) // 4)

            def gating(layer):
                act.wait_ge(*after("z", (layer, IN_T - 1)))
                act.activation(z[:, 14:18], z[:, 14:18], ACT.Gelu_apprx_tanh).then_inc(*done("gelu", layer))
                act.wait_ge(*after("ln_x", layer))
                act.activation(ln_sq[:, :, :], ln_x[:, :, :], ACT.Square).then_inc(*done("ln_sq", layer))
                inverse_root((layer, "ln"), 2 * P, mix_bank[1][:], tmp[0][:])
                for g in range(2):
                    act.wait_ge(*after("sg_vt", (layer, g)))
                    act.activation(sg_tok[:, :, g * P:(g + 1) * P], acc[g][:].rearrange("p (n f) -> p n f", f=P),
                                   ACT.Copy).then_inc(*done("sg_tok", (layer, g)))
                for g in range(2):
                    act.wait_ge(*after("mix_out", (layer, 6 + g)))
                    mix_high(layer, 6 + g, sg_o[:, g])

            def first_block_act():
                act.dma_start(h[:, :, :], a["x"].rearrange("p (k t) -> p k t", t=SEQ)).then_inc(ld["h"], 16)
                act.dma_start(par1[:, :], a["par1"]).then_inc(ld["par1"], 16)
                act.dma_start(ctx_raw[:, :, :], a["ctx"].rearrange("p (k t) -> p k t", t=CTX)).then_inc(ld["ctx"], 16)
                act.dma_start(dft_c[:, :], a["dft_c"]).then_inc(ld["dft_c"], 16)
                act.wait_ge(ld["par1"], 16)
                act.activation(c_silu[:, :, :], par1[:, P1_C:P1_C + 2 * KT].rearrange("p (k c) -> p k c", c=2), ACT.Silu)\
                    .then_inc(*done("c_silu", 0))
                act.wait_ge(*after("c_silu", 0))
                act.activation(c_hi[:, :, :], c_silu[:, :, :], ACT.Copy).then_inc(*done("c_high", 0))
                high_parts(SLOTS)
                act.wait_ge(ld["h"], 16)
                act.activation(x_sq[:, :, :], h[:, :, :], ACT.Square).then_inc(*done("x_sq", "x"))
                act.wait_ge(ld["ctx"], 16)
                act.activation(ctx_sq[:, :, :], ctx_raw[:, :, :], ACT.Square).then_inc(*done("x_sq", "ctx"))
                act.wait_ge(*after("eps", 0))
                inverse_root("x", D)
                inverse_root("ctx", D, mix_bank[0][:, 0:CTX], sq_sum[:, 0:CTX])
                for m in range(ADA_T):
                    tile_ready("ada", m, KT)
                for k in range(KT):
                    act.wait_ge(*after("in_scaled", (k, 0)))
                    act.activation(xhi[:, k], x_scaled[:, k], ACT.Identity, bias=mod[:, k, 0:1])\
                        .then_inc(*done("in_high", (k, 0)))
                    act.wait_ge(*after("in_scaled", (k, 1)))
                    act.activation(ctx_hi[:, k], ctx_scaled[:, k], ACT.Identity, bias=mod[:, k, 1:2])\
                        .then_inc(*done("in_high", (k, 1)))
                for m in range(IN1A_T):
                    tile_ready("in1a", m, KT)
                    t = first_tile["in1a"] + m
                    if m == DT0:
                        act.activation(dt_raw[:, 0:SEQ], acc[t % 4][:], ACT.Identity, bias=par1[:, P1_DTB:P1_DTB + 1])\
                            .then_inc(*done("dt_raw", 0, bank_of=t))
                        act.activation(dt_raw[:, SEQ:], ctx_bank[0][:, 0:CTX], ACT.Identity,
                                       bias=par1[:, P1_DTB:P1_DTB + 1]).then_inc(*done("dt_raw", 1))
                    elif U0 <= m < ZF0:
                        act.activation(u_in[:, m - U0], acc[t % 4][:], ACT.Copy).then_inc(*done("u", m - U0, bank_of=t))
                    elif m >= ZF0:
                        if m == ZF0:
                            act.wait_ge(*after("conv_turned", C0 - 1))
                        act.activation(zf[:, m - ZF0], acc[t % 4][:], ACT.Silu).then_inc(*done("zf", m - ZF0, bank_of=t))
                    if B0 + 1 <= m <= U0:
                        conv_out(m - 1)
                    if B0 + 2 <= m:
                        conv_tokens(m - 2)
                step_sizes()
                for d in range(2):
                    for g in range(GROUPS):
                        act.wait_ge(*after("state", (d, g)))
                        if d == 1 and g == 0:
                            act.wait_ge(*after("ctx_weighted", 1))
                        act.activation(h0[d][:, g * 384:(g + 1) * 384], bank[4 + g][:, 0:384], ACT.Copy)\
                            .then_inc(*done("h0", (d, g)))
                for m in range(ST):
                    tile_ready("in1b", m, KT)
                    t = first_tile["in1b"] + m
                    act.activation(zs[:, m], acc[t % 4][:], ACT.Silu).then_inc(*done("zs", m, bank_of=t))
                act.dma_start(dft_t[:, :, :, :], a["dft_t"].rearrange("p (a i t) -> p a i t", a=2, i=4))\
                    .then_inc(ld["dft_t"], 16)
                for i in range(4):
                    act.wait_ge(*after("four_tok", i))
                    b = 4 + 2 * (i % 2)
                    act.activation(four_tok[:, i].rearrange("p (a j) c f -> p a (j c f)", a=2), banks[:, b:b + 2, :], ACT.Copy)\
                        .then_inc(*done("four_tok_out", i))
                for j in range(FT4):
                    act.wait_ge(*after("four", 3))
                    act.activation(four_hi[:, j], bank[4 + j], ACT.Copy).then_inc(*done("four_high", j))
                for m in range(FT4):
                    tile_ready("four", m, FT4)
                act.activation(cum_hi[:], cum[:, 0:SEQ], ACT.Copy)
                act.activation(ident_r[:], ident, ACT.Copy).then_inc(*done("cum_high", 0))
                for g in range(GROUPS):
                    for hd in range(6 * g, 6 * g + 6):
                        head(hd)
                        if hd % 6 == 0:
                            for i in range(4):
                                act.wait_ge(*after("cb", (g, i)))
                                act.activation(cbt[:, i], bank[6 + i % 2], ACT.Copy).then_inc(*done("cbt", (g, i)))
                        if hd % 6 == 1 and g:
                            group_squares(g - 1)
                        if hd % 6 == 2 and g:
                            inverse_root(("ssd", g - 1), 3 * P, bank[6], inv_rms[:])
                group_squares(GROUPS - 1)
                inverse_root(("ssd", GROUPS - 1), 3 * P, bank[6], inv_rms[:])
                for t in range(MIX_T):
                    act.wait_ge(*after("mix1", MIX_T - 1))
                    act.activation(mix1_hi(t), mix1(t), ACT.Copy).then_inc(*done("mix1_high", t))
                act.dma_start(h[:, :, :], a["x"].rearrange("p (k t) -> p k t", t=SEQ)).then_inc(ld["x_again"], 16)
                act.dma_start(tmp[0][:].bitcast(I32), a["positions"].broadcast_to([P, SEQ])).then_inc(ld["pos"], 16)
                turn_angles()
                for m in range(KT):
                    tile_ready("out1", m, MIX_T)
                    act.wait_ge(*after("residual", m))
                    squares("res_sq", "first", m, h[:, m])
                inverse_root("first", D)

            def conv_out(m):
                n = m - B0 if m < XS0 else m - XS0 if m < C0 else m - C0
                buf, b = conv[m % 2], par1[:, P1_CB + m - B0:P1_CB + m - B0 + 1]
                act.wait_ge(*after("conv", m))
                if m >= C0:
                    act.activation(c_x[:, n], buf[:, 0:SEQ], ACT.Silu, bias=b).then_inc(*done("conv_out", m))
                elif m < XS0:
                    act.activation(b_x[:, n], buf[:, 0:SEQ], ACT.Silu, bias=b)
                    act.activation(buf[:, SEQ:], buf[:, SEQ:], ACT.Silu, bias=b).then_inc(*done("conv_out", m))
                else:
                    act.activation(buf[:, :], buf[:, :], ACT.Silu, bias=b).then_inc(*done("conv_out", m))

            def conv_tokens(m):
                if not B0 <= m < C0:
                    return
                act.wait_ge(*after("conv_turned", m))
                if m >= XS0:
                    n = m - XS0
                    act.activation(x_tok[:, :, n * P:(n + 1) * P], mix_bank[1][:].rearrange("p (i f) -> p i f", f=P), ACT.Copy)
                    dst = ctx_tok[:, :, n * P:(n + 1) * P]
                else:
                    dst = ctx_b_tok[:, :, (m - B0) * P:(m - B0 + 1) * P]
                act.activation(dst, mix_bank[2][:, 0:CTX].rearrange("p (i f) -> p i f", f=P), ACT.Copy)\
                    .then_inc(*done("conv_tok", m))

            def step_sizes():
                act.wait_ge(*after("dt_raw", 1))
                act.activation(dt[1][:, :], dt_raw[:, :], ACT.Abs).then_inc(*done("dt_act", "abs"))
                act.wait_ge(*after("dt_act", "abs"))
                act.activation(dt_small[:, 0:1], par1[:, P1_DTB + 1:P1_DTB + 2], ACT.Exp)
                act.activation(dt[1][:, :], dt[1][:, :], ACT.Exp, scale=-1.0).then_inc(*done("dt_act", "exp"))
                act.wait_ge(*after("dt_cum", 0))
                act.activation(dt[2][:, SEQ:], cum[:, SEQ:], ACT.Exp, scale=-1.0, bias=dt_small[:, 2:3])\
                    .then_inc(*done("dt_act", "end"))
                act.activation(dt[3][:, 0:SEQ], dt[1][:, 0:SEQ], ACT.Ln).then_inc(*done("dt_act", "ln"))
                act.wait_ge(*after("dt_turned", 0))
                act.activation(bias_tok[:, :, :], bank[4].rearrange("p (i r) -> p i r", r=P)[:, :, 0:DT_ROWS], ACT.Copy)
                act.activation(ctx_w_tok[:, :, :], bank[5][:, 0:CTX].rearrange("p (i r) -> p i r", r=P)[:, :, 0:DT_ROWS], ACT.Copy)\
                    .then_inc(*done("dt_tok", 0))

            def head(hd):
                rf, rb = bank[2 * (hd % 2)], bank[2 * (hd % 2) + 1]
                e, dg = decay[hd % 2], diag[hd % 2]
                act.wait_ge(*after("ssd_diag", hd))
                if hd >= 2:
                    act.wait_ge(*after("ssd_y", hd - 2))
                for i in range(4):
                    bf, bb = bias_tok[:, i, hd:hd + 1], bias_tok[:, i, HEADS + hd:HEADS + hd + 1]
                    if i < 3:
                        act.activation(e[:, i, (i + 1) * P:], rf[:, (i + 1) * P:], ACT.Exp, bias=bf)
                    if i:
                        act.activation(e[:, i, 0:i * P], rb[:, 0:i * P], ACT.Exp, bias=bb)
                    act.activation(e[:, i, i * P:(i + 1) * P], dg[:, 0, i], ACT.Exp, bias=bf)
                    ins = act.activation(dg[:, 1, i], dg[:, 1, i], ACT.Exp, bias=bb)
                ins.then_inc(*done("ssd_exp", hd))
                act.activation(c_dec[hd % 2][:, :, :], banks[:, 2 * (hd % 2):2 * (hd % 2) + 2], ACT.Exp)\
                    .then_inc(*done("ssd_row_exp", hd))

            def group_squares(g):
                for t in range(3):
                    act.wait_ge(*after("ssd_gated", 3 * g + t))
                    act.activation(tmp[t][:], zs[:, 3 * g + t], ACT.Square).then_inc(*done("ssd_sq", (g, t)))
            eps = small[:, 0:1]
            act.dma_start(table[:, :], a["table"]).then_inc(ld["table"], 16)
            act.dma_start(masks_f[:, :, :], a["masks"].rearrange("p (l f) -> p l f", f=P)).then_inc(ld["masks"], 16)
            act.dma_start(par2[:, :, :], a["par2"].rearrange("l p c -> p l c")).then_inc(ld["par2"], 16)
            if 1 not in blocks:
                act.dma_start(tmp[0][:].bitcast(I32), a["positions"].broadcast_to([P, SEQ])).then_inc(ld["pos"], 16)
                act.dma_start(h[:, :, :], a["x"].rearrange("p (k t) -> p k t", t=SEQ)).then_inc(ld["h"], 16)
            act.wait_ge(*after("prepared", "logits"))
            act.activation(small[:, 8:12], small[:, 8:12], ACT.Exp).then_inc(*done("prepared_act", "logits"))

            def turn_angles():
                act.wait_ge(*after("prepared", "angles"))
                act.activation(cos_t[:], cos_t[:], ACT.Sin)
                act.activation(sin_t[:], sin_t[:], ACT.Sin).then_inc(*done("prepared_act", "angles"))

            if 1 in blocks:
                first_block_act()
            else:
                turn_angles()
                high_parts(SLOTS)

            for layer in range(DEPTH):
                for s in range(4):
                    q = (layer, s)
                    norm_in(q, par2[:, layer, P2_NORM + 16 * s:P2_NORM + 16 * s + KT])
                    high_parts(units_to(q) + SLOTS + 1)
                    inverse_root(("pre", q), D)
                    if s in (0, 2):
                        gu = ("gu", layer, s // 2)
                        for j in range(FT):
                            tile_ready(gu, 2 * j + 1, KT)
                            act.wait_ge(*after("gate_scaled", (q, j)))
                            act.activation(tmp[0][:], tmp[0][:], ACT.Silu).then_inc(*done("silu", (q, j)))
                            act.wait_ge(*after("act_formed", (q, j)))
                            act.activation(act_hi[:, j], tmp[1][:], ACT.Copy).then_inc(*done("act_high", (q, j)))
                        y_out(("down", layer, s // 2), q, FT, y_over_x)
                    elif s == 1:
                        act.dma_start(mixpar[:, :], a["mixpar"][layer]).then_inc(ld[f"mix{layer}"], 16)
                        for m in range(IN_T):
                            tile_ready(("in2", layer), m, KT)
                        hgrn(layer)
                        attention(layer)
                        gating(layer)
                        y_out(("out2", layer), q, KT, y_dyn)
                    else:
                        act.dma_start(ple_raw[:, :, :], a["ple"][layer].rearrange("p (k t) -> p k t", t=SEQ))\
                            .then_inc(ld[f"ple{layer}"], 16)
                        act.wait_ge(ld[f"ple{layer}"], 16)
                        act.activation(ple_hi[:, :, :], ple_raw[:, :, :], ACT.Copy)\
                            .then_inc(*done("ple_high", layer))
                        for m in range(KT):
                            tile_ready(("gate", layer), m, KT)
                            act.wait_ge(*after("gate2_scaled", (layer, m)))
                            act.activation(y_dyn[:, m], tmp[m % 2][:], ACT.Sigmoid)\
                                .then_inc(*done("gate2", (layer, m)))
                        for m in range(KT):
                            tile_ready(("proj", layer), m, PLE_T)
                            act.wait_ge(*after("y_formed", (q, m)))
                            squares("y_sq", q, m, y_dyn[:, m])
                        inverse_root(("post", q), D)
            high_parts(units)

        @block.vector
        def _(v):
            def sq_add(name, q, k):
                v.wait_ge(*after(name, (q, k)))
                if k:
                    if k > 1:
                        v.wait_ge(*after("sq_added", (name, q, k - 1)))
                    v.tensor_tensor(sq_sum[:], sq_sum[:], tmp[1 + k % 2][:], ALU.add)\
                        .then_inc(*done("sq_added", (name, q, k)))

            def boundary(q_post, y, q_pre, gain_post, gain_pre):
                if q_post is not None:
                    post = q_post if q_post == "first" else ("post", q_post)
                for k in range(KT + 1):
                    if k == 0 and q_post is not None:
                        v.wait_ge(*after("inverse", post))
                    if k < KT and q_post == "first":
                        v.scalar_tensor_tensor(h[:, k], h[:, k], gain_post[:, k:k + 1], inv_rms[:],
                                               ALU.mult, ALU.mult).then_inc(*done("h_new", (q_pre, k)))
                    elif k < KT and q_post is not None:
                        if k:
                            v.wait_ge(*after("h_new", (q_pre, k - 1)))
                        v.scalar_tensor_tensor(tmp[0][:], y[:, k], gain_post[:, k:k + 1], inv_rms[:],
                                               ALU.mult, ALU.mult).then_inc(*done("y_normed", (q_post, k)))
                        v.wait_ge(*after("y_normed", (q_post, k)))
                        v.tensor_tensor(h[:, k], h[:, k], tmp[0][:], ALU.add)\
                            .then_inc(*done("h_new", (q_pre, k)))
                    if k and q_pre != "last":
                        v.wait_ge(*after("x_high", (q_pre, k - 1)))
                        v.scalar_tensor_tensor(xlo[:, k - 1], h[:, k - 1], gain_pre[:, k - 1:k],
                                               xhi[:, k - 1].bitcast(F32), ALU.mult, ALU.subtract)\
                            .then_inc(*done("x_low", (q_pre, k - 1)))
                        sq_add("h_sq", q_pre, k - 1)

            def mix_low(layer, t, src):
                v.wait_ge(*after("mix_high", (layer, t)))
                v.tensor_tensor(xlo[:, t], src, xhi[:, t].bitcast(F32), ALU.subtract)\
                    .then_inc(*done("mix_low", (layer, t)))

            def hgrn(layer):
                v.memset(hg_att[:, :, :], 0.0)
                v.memset(k_dec[:, :, :], 0.0)
                v.memset(state[:, :, :, :], 0.0).then_inc(*done("hg_cleared", layer))
                v.wait_ge(*after("hg_sig", layer))
                for g in range(2):
                    floor, rest = lower[:, layer, g, 0:1], lower[:, layer, g, 1:2]
                    v.tensor_scalar(key_k[:, g], key_k[:, g], rest, None, ALU.mult)
                    v.tensor_scalar(gate_b[:, g], gate_b[:, g], rest, floor, ALU.mult, ALU.add)\
                        .then_inc(*done("hg_gate", (layer, g)))
                v.wait_ge(*after("hg_gate", (layer, 1)))
                v.tensor_scalar(diff[:, :, :], gate_b[:, :, :], 2.0 ** -60, None, ALU.max)
                v.tensor_scalar(q_dec[:, :, :], gate_b[:, :, :], 2.0 ** 60, 1.0, ALU.mult, ALU.min)\
                    .then_inc(*done("hg_ln_in", layer))
                v.wait_ge(*after("hg_ln", layer))
                v.tensor_tensor(diff[:, :, :], diff[:, :, :], q_dec[:, :, :], ALU.add)\
                    .then_inc(*done("hg_log", layer))
                v.wait_ge(*after("hg_log", layer))
                for g in range(2):
                    for n in range(4):
                        c = slice(n * P, (n + 1) * P)
                        v.tensor_tensor_scan(gate_b[:, g, c], diff[:, g, c], diff[:, g, c], 0.0,
                                             ALU.add, ALU.bypass).then_inc(*done("hg_cum", (layer, g, n)))
                v.wait_ge(*after("hg_cum", (layer, 1, 3)))
                b4 = gate_b[:, :, :].rearrange("p g (n f) -> p g n f", f=P)
                v.tensor_copy(tot[:, :, :], b4[:, :, :, P - 1]).then_inc(*done("hg_tot", layer))

                def diffs(n):
                    b = LEVELS[n - 1]
                    src = gate_b[:, :, :].rearrange("p g (r s) -> p (g r) s", s=2 * b)
                    dst = diff[:, :, :].rearrange("p g (r s) -> p (g r) s", s=2 * b)
                    v.tensor_tensor(dst, src, src[:, :, b - 1:b].broadcast_to([P, SEQ // b, 2 * b]), ALU.subtract)\
                        .then_inc(*done("hg_diff", (layer, n)))

                def masked(n):
                    v.wait_ge(*after("hg_scores", (layer, n)))
                    if n:
                        v.wait_ge(*after("hg_masked", (layer, n - 1, 3)))
                    m = masks[:, n].unsqueeze(1).broadcast_to([P, 4, P])
                    for e in range(4):
                        v.copy_predicated(hg_att[:, e].rearrange("p (n f) -> p n f", f=P), m,
                                          bank[4 * (n % 2) + e][:].rearrange("p (n f) -> p n f", f=P))\
                            .then_inc(*done("hg_masked", (layer, n, e)))

                diffs(1)
                v.wait_ge(*after("hg_cleared", layer))
                for n, b in enumerate(LEVELS, 1):
                    v.wait_ge(*after("hg_exp", (layer, n)))
                    v.wait_ge(*after("hg_scores", (layer, n - 1)))

                    def halves(x):
                        return x.rearrange("p g (r s) -> p (g r) s", s=2 * b)

                    d, qs, ks = halves(diff[:, :, :]), halves(z[:, 0:2]), halves(key_k[:, :, :])
                    qd, kd = halves(q_dec[:, :, :]), halves(k_dec[:, :, :])
                    v.tensor_tensor(qd[:, :, b:], qs[:, :, b:], d[:, :, b:], ALU.mult)
                    v.tensor_tensor(kd[:, :, 0:b], ks[:, :, 0:b], d[:, :, 0:b], ALU.mult)\
                        .then_inc(*done("hg_dec", (layer, n)))
                    v.wait_ge(*after("hg_dec", (layer, n)))
                    if n < len(LEVELS):
                        diffs(n + 1)
                    else:
                        v.tensor_tensor(diff[:, :, :].rearrange("p g (n f) -> p (g n) f", f=P),
                                        tot[:, :, :].rearrange("p g n -> p (g n)").unsqueeze(2).broadcast_to([P, 8, P]),
                                        gate_b[:, :, :].rearrange("p g (n f) -> p (g n) f", f=P), ALU.subtract)\
                            .then_inc(*done("hg_diff", (layer, "end")))
                    masked(n - 1)
                v.wait_ge(*after("hg_exp", (layer, "end")))
                v.wait_ge(*after("hg_scores", (layer, len(LEVELS))))
                v.tensor_tensor(k_dec[:, :, :], key_k[:, :, :], diff[:, :, :], ALU.mult)
                v.tensor_tensor(q_dec[:, :, :], z[:, 0:2], gate_b[:, :, :], ALU.mult)\
                    .then_inc(*done("hg_dec", (layer, "end")))
                masked(len(LEVELS))
                for g in range(2):
                    v.wait_ge(*after("hg_kv", (layer, g)))
                    for n in range(3):
                        for e in range(2):
                            s = slice(64 * e, 64 * e + 64)
                            kv = acc[g][s, n * P + 64 * e:n * P + 64 * e + 64]
                            if n == 0:
                                v.tensor_copy(state[s, 0, g, s], kv).then_inc(*done("hg_state", (layer, g, n, e)))
                            else:
                                v.wait_ge(*after("hg_state", (layer, g, n - 1, e)))
                                v.scalar_tensor_tensor(state[s, n, g, s], state[s, n - 1, g, s],
                                                       e_tot[s, g, n:n + 1], kv, ALU.mult, ALU.add)\
                                    .then_inc(*done("hg_state", (layer, g, n, e)))
                for g in range(2):
                    v.wait_ge(*after("inverse", (layer, "hg", g)))
                    v.wait_ge(*after("hg_o_copied", (layer, g)))
                    v.tensor_tensor(hg_o[:, g], hg_o[:, g], k_dec[:, g], ALU.mult)\
                        .then_inc(*done("hg_normed", (layer, g)))
                    v.wait_ge(*after("hg_normed", (layer, g)))
                    v.scalar_tensor_tensor(hg_o[:, g], hg_o[:, g], par2[:, layer, P2_HG:P2_HG + 1], z[:, 6 + g],
                                           ALU.mult, ALU.mult).then_inc(*done("mix_out", (layer, g)))
                for g in range(2):
                    mix_low(layer, g, hg_o[:, g])

            def attention(layer):
                for i in range(5):
                    zi = z[:, 12 if i == 0 else 7 + i]
                    v.wait_ge(*after("att_rot", (layer, i)))
                    if i:
                        v.wait_ge(*after("att_roped", (layer, i - 1)))
                    v.tensor_tensor(tmp[0][:], zi, cos_t[:], ALU.mult)
                    v.tensor_tensor(tmp[1][:], acc[i % 4][:], sin_t[:], ALU.mult)\
                        .then_inc(*done("att_rot_terms", (layer, i)))
                    v.wait_ge(*after("att_rot_terms", (layer, i)))
                    v.tensor_tensor(zi, tmp[0][:], tmp[1][:], ALU.add).then_inc(*done("att_roped", (layer, i)))

                def shifts(i):
                    t, w0 = i // 4, P if i % 4 == 0 else 0
                    st, sc = stat[i % 3], scores[i % 3]
                    sink = par2[:, layer, P2_SINK + 2 * t:P2_SINK + 2 * t + 2]
                    v.wait_ge(*after("att_scores", (layer, i)))
                    if i >= 3:
                        v.wait_ge(*after("att_turned", (layer, i - 3)))
                    mask = table[:, C_AMASK + w0:C_AMASK + 2 * P].unsqueeze(1).broadcast_to([P, 2, 2 * P - w0])
                    v.scalar_tensor_tensor(sc[:, :, w0:], banks[:, 2 * (i % 2):2 * (i % 2) + 2, w0:2 * P],
                                           SCALE, mask, ALU.mult, ALU.add).then_inc(*done("att_masked", (layer, i)))
                    v.wait_ge(*after("att_masked", (layer, i)))
                    v.tensor_reduce(st[:, 0], sc[:, :, w0:], AX.X, ALU.max).then_inc(*done("att_max", (layer, i)))
                    v.wait_ge(*after("att_max", (layer, i)))
                    v.tensor_tensor(st[:, 0], st[:, 0], sink, ALU.max).then_inc(*done("att_max2", (layer, i)))
                    v.wait_ge(*after("att_max2", (layer, i)))
                    v.tensor_scalar(st[:, 1], st[:, 0], -1.0, None, ALU.mult)
                    v.tensor_tensor(st[:, 2], sink, st[:, 0], ALU.subtract).then_inc(*done("att_shift", (layer, i)))

                def probabilities(i):
                    w0 = P if i % 4 == 0 else 0
                    st, sc = stat[i % 3], scores[i % 3]
                    v.wait_ge(*after("att_exp", (layer, i)))
                    v.tensor_tensor(st[:, 5], st[:, 3], st[:, 4], ALU.add).then_inc(*done("att_den", (layer, i)))
                    v.wait_ge(*after("att_den", (layer, i)))
                    v.reciprocal(st[:, 6], st[:, 5]).then_inc(*done("att_rden", (layer, i)))
                    v.wait_ge(*after("att_rden", (layer, i)))
                    v.tensor_tensor(sc[:, :, w0:], sc[:, :, w0:], st[:, 6].unsqueeze(2).broadcast_to([P, 2, 2 * P - w0]),
                                    ALU.mult).then_inc(*done("att_probs", (layer, i)))

                for i in range(16 + 3):
                    if i < 16:
                        shifts(i)
                    if 1 <= i <= 16:
                        probabilities(i - 1)
                    if i >= 6 and (i - 6) % 4 == 0:
                        mix_low(layer, 2 + (i - 6) // 4, mix_bank[(i - 6) // 4 % 2][:])

            def gating(layer):
                v.wait_ge(ld[f"mix{layer}"], 16)
                tri = table[:, C_TRI:C_TRI + P].unsqueeze(1).broadcast_to([P, 4, P])
                v.tensor_tensor(sg_w[:, :, :], mixpar[:, M2_SGW:M2_COLS].rearrange("p (g t) -> p g t", t=P), tri,
                                ALU.mult).then_inc(*done("sg_w", layer))
                v.wait_ge(*after("ln_mean", layer))
                v.scalar_tensor_tensor(ln_x[:, :, :], mix_bank[0][:].unsqueeze(1).broadcast_to([P, 2, SEQ]), -1.0 / (2 * P),
                                       z[:, 16:18], ALU.mult, ALU.add).then_inc(*done("ln_x", layer))
                v.wait_ge(*after("inverse", (layer, "ln")))
                for g in range(2):
                    v.scalar_tensor_tensor(ln_x[:, g], ln_x[:, g], par2[:, layer, P2_LN + g:P2_LN + g + 1], tmp[0][:],
                                           ALU.mult, ALU.mult).then_inc(*done("ln_out", (layer, g)))
                for g in range(2):
                    v.wait_ge(*after("sg_mixed", (layer, g)))
                    bias = mixpar[:, M2_SGB + g * P:M2_SGB + (g + 1) * P].unsqueeze(1).broadcast_to([P, 4, P])
                    v.tensor_tensor(sg_o[:, g].rearrange("p (n f) -> p n f", f=P),
                                    mix_bank[2 * g][:].rearrange("p (n f) -> p n f", f=P), bias, ALU.add)\
                        .then_inc(*done("sg_biased", (layer, g)))
                    v.wait_ge(*after("sg_biased", (layer, g)))
                    v.tensor_tensor(sg_o[:, g], sg_o[:, g], z[:, 14 + g], ALU.mult)\
                        .then_inc(*done("mix_out", (layer, 6 + g)))
                for g in range(2):
                    mix_low(layer, 6 + g, sg_o[:, g])

            def prepare():
                ready = lambda key: v.wait_ge(*after("prepared", key))
                v.memset(small[:, 0:1], EPS).then_inc(*done("eps", 0))
                v.wait_ge(ld["masks"], 16)
                v.tensor_copy(masks[:, :, :], masks_f[:, :, :]).then_inc(*done("masks", 0))
                v.wait_ge(ld["par2"], 16)
                lg = par2[:, 0, P2_LB:P2_LB + 4]
                v.tensor_tensor(small[:, 4:6], lg[:, 0:2], lg[:, 2:4], ALU.max).then_inc(*done("prepared", "lmax"))
                ready("lmax")
                for l in range(DEPTH):
                    v.tensor_tensor(small[:, 8 + 2 * l:10 + 2 * l], lg[:, 2 * l:2 * l + 2], small[:, 4:6], ALU.subtract)\
                        .then_inc(*done("prepared", ("lsub", l), *(["logits"] if l else [])))
                v.wait_ge(*after("prepared_act", "logits"))
                v.tensor_tensor(small[:, 4:6], small[:, 8:10], small[:, 10:12], ALU.add).then_inc(*done("prepared", "lsum"))
                ready("lsum")
                v.reciprocal(small[:, 6:8], small[:, 4:6]).then_inc(*done("prepared", "linv"))
                ready("linv")
                v.tensor_tensor(small[:, 8:12].rearrange("p (l g) -> p l g", l=2), small[:, 8:12].rearrange("p (l g) -> p l g", l=2),
                                small[:, 6:8].unsqueeze(1).broadcast_to([P, 2, 2]), ALU.mult).then_inc(*done("prepared", "probs"))
                ready("probs")
                v.tensor_tensor(small[:, 12:14], small[:, 8:10], small[:, 8:10], ALU.subtract)
                v.tensor_tensor(small[:, 16:18], small[:, 8:10], small[:, 10:12], ALU.add).then_inc(*done("prepared", "psum"))
                ready("psum")
                v.tensor_tensor(small[:, 14:16], small[:, 16:18], small[:, 8:10], ALU.subtract).then_inc(*done("prepared", "lb"))
                ready("lb")
                bounds = small[:, 12:16].rearrange("p (l g) -> p l g", l=2)
                v.tensor_scalar(lower[:, :, :, 0], bounds, LB_FLOOR, None, ALU.max)
                v.tensor_scalar(lower[:, :, :, 1], bounds, -1.0, 1.0, ALU.mult, ALU.add)
                for l in range(DEPTH):
                    for n in (1, 5):
                        gains = par2[:, l, P2_NORM + 8 * n:P2_NORM + 8 * n + 8]
                        v.tensor_scalar(gains, gains, 0.5, None, ALU.mult).then_inc(*done("prepared", ("half", l, n)))

            def prepare_angles():
                ready = lambda key: v.wait_ge(*after("prepared", key))
                v.wait_ge(ld["table"], 16)
                v.wait_ge(ld["pos"], 16)
                v.tensor_copy(tmp[1][:], tmp[0][:].bitcast(I32)).then_inc(*done("prepared", "pos"))
                ready("pos")
                v.tensor_scalar(tmp[2][:], tmp[1][:], table[:, C_INV:C_INV + 1], None, ALU.mult)\
                    .then_inc(*done("prepared", "angle"))
                ready("angle")
                two_pi = 2 * np.pi
                c1 = 6.28125
                c2 = float(np.float32(np.float16(two_pi - c1)))
                c3 = two_pi - c1 - c2
                for name, dst, turn in (("cos", cos_t, 0.25), ("sin", sin_t, 0.0)):
                    v.tensor_scalar(tmp[1][:], tmp[2][:], 1 / two_pi, turn, ALU.mult, ALU.add)\
                        .then_inc(*done("prepared", (name, 0)))
                    ready((name, 0))
                    v.tensor_scalar(tmp[1][:], tmp[1][:], 12582912.0, None, ALU.add).then_inc(*done("prepared", (name, 1)))
                    ready((name, 1))
                    v.tensor_scalar(tmp[1][:], tmp[1][:], -12582912.0, None, ALU.add).then_inc(*done("prepared", (name, 2)))
                    ready((name, 2))
                    src = tmp[2]
                    for n, c in enumerate((c1, c2, c3)):
                        v.scalar_tensor_tensor(dst[:], tmp[1][:], -c, src[:], ALU.mult, ALU.add)\
                            .then_inc(*done("prepared", (name, 3 + n)))
                        ready((name, 3 + n))
                        src = dst
                    v.tensor_scalar(dst[:], dst[:], turn * two_pi, 3.1415925, ALU.add, ALU.min)\
                        .then_inc(*done("prepared", (name, 6)))
                    ready((name, 6))
                    v.tensor_scalar(dst[:], dst[:], -3.1415925, None, ALU.max)\
                        .then_inc(*done("prepared", (name, 7), *(["angles"] if name == "sin" else [])))

            def first_block_dve():
                v.wait_ge(*after("c_high", 0))
                v.tensor_tensor(c_lo[:, :, :], c_silu[:, :, :], c_hi[:, :, :].bitcast(F32), ALU.subtract)\
                    .then_inc(*done("c_low", 0))
                v.wait_ge(*after("product", ("ada", ADA_T - 1)))
                v.tensor_tensor(mod[:, :, :], bank[7][:, 0:2 * ADA_T].rearrange("p (m c) -> p m c", c=2),
                                par1[:, P1_ADA:P1_ADA + ADA_T].unsqueeze(2).broadcast_to([P, ADA_T, 2]), ALU.add)\
                    .then_inc(*done("mod", 0))
                v.wait_ge(*after("mod", 0))
                v.scalar_tensor_tensor(in_scale[:, :, :], mod[:, KT:2 * KT], 1.0,
                                       par1[:, P1_NORM:P1_NORM + KT].unsqueeze(2).broadcast_to([P, KT, 2]),
                                       ALU.add, ALU.mult).then_inc(*done("in_scale", 0))
                v.wait_ge(*after("in_scale", 0))
                v.wait_ge(*after("inverse", "ctx"))

                def lows(k):
                    for c, (src, hi, lo) in enumerate(((x_scaled, xhi, xlo), (ctx_scaled, ctx_hi, ctx_lo))):
                        v.wait_ge(*after("in_high", (k, c)))
                        v.scalar_tensor_tensor(lo[:, k], src[:, k], mod[:, k, c:c + 1], hi[:, k].bitcast(F32),
                                               ALU.add, ALU.subtract).then_inc(*done("in_low", (k, c)))

                for k in range(KT):
                    v.scalar_tensor_tensor(x_scaled[:, k], h[:, k], in_scale[:, k, 0:1], inv_rms[:], ALU.mult, ALU.mult)\
                        .then_inc(*done("in_scaled", (k, 0)))
                    v.scalar_tensor_tensor(ctx_scaled[:, k], ctx_raw[:, k], in_scale[:, k, 1:2], sq_sum[:, 0:CTX],
                                           ALU.mult, ALU.mult).then_inc(*done("in_scaled", (k, 1)))
                    if k:
                        lows(k - 1)
                lows(KT - 1)
                for m in range(B0, U0):
                    convolve(m)
                step_sizes()
                for d in range(2):
                    if d:
                        v.wait_ge(*after("state", (0, GROUPS - 1)))
                    for i in range(2):
                        ins = v.tensor_tensor(ctx_weighted[:, i].rearrange("p (h f) -> p h f", f=64),
                                              ctx_tok[:, i].rearrange("p (h f) -> p h f", f=64),
                                              ctx_w_tok[:, i, d * HEADS:(d + 1) * HEADS].unsqueeze(2)
                                              .broadcast_to([P, HEADS, 64]), ALU.mult)
                    ins.then_inc(*done("ctx_weighted", d))
                for j in range(FT4):
                    v.wait_ge(*after("four_high", j))
                    v.tensor_tensor(four_lo[:, j], bank[4 + j], four_hi[:, j].bitcast(F32), ALU.subtract)\
                        .then_inc(*done("four_low", j))
                for m in range(FT4):
                    t = first_tile["four"] + m
                    v.wait_ge(*after("product", ("four", m)))
                    v.scalar_tensor_tensor(zf[:, m], acc[t % 4][:], par1[:, P1_BF + m:P1_BF + m + 1], zf[:, m],
                                           ALU.add, ALU.mult).then_inc(*done("mix1", m, bank_of=t))
                v.wait_ge(*after("cum_high", 0))
                v.tensor_tensor(cum_lo[:], cum[:, 0:SEQ], cum_hi[:].bitcast(F32), ALU.subtract)\
                    .then_inc(*done("cum_low", 0))
                masked_diagonals(0)
                masked_diagonals(1)
                for hd in range(HEADS):
                    head(hd)
                    if hd + 2 < HEADS:
                        masked_diagonals(hd + 2)
                    if hd % 2 and hd > 1:
                        gate_tile(hd // 2 - 1)
                    if hd % 6 == 3 and hd > 6:
                        group_norm(hd // 6 - 1)
                gate_tile(ST - 1)
                group_norm(GROUPS - 1)
                for t in range(MIX_T):
                    v.wait_ge(*after("mix1_high", t))
                    v.tensor_tensor(mix1_lo(t), mix1(t), mix1_hi(t).bitcast(F32), ALU.subtract)\
                        .then_inc(*done("mix1_low", t))
                prepare_angles()
                v.wait_ge(*after("prepared_act", "angles"))
                v.wait_ge(ld["x_again"], 16)
                for m in range(KT):
                    t = first_tile["out1"] + m
                    v.wait_ge(*after("product", ("out1", m)))
                    v.scalar_tensor_tensor(h[:, m], acc[t % 4][:], mod[:, 2 * KT + m, 0:1], h[:, m], ALU.mult, ALU.add)\
                        .then_inc(*done("residual", m, bank_of=t))
                    if m:
                        sq_add("res_sq", "first", m - 1)
                sq_add("res_sq", "first", KT - 1)

            def convolve(m):
                t = first_tile["in1a"] + m
                w = par1[:, P1_CONV + 9 * (m - B0):P1_CONV + 9 * (m - B0) + 9]
                buf = conv[m % 2]
                v.wait_ge(*after("product", ("in1a", m)))
                if m >= B0 + 2:
                    v.wait_ge(*after("conv_out" if m - 2 >= C0 else "conv_turned", m - 2))
                src = acc[t % 4][:].rearrange("p (y x) -> p y x", x=GRID_W)
                dst = buf[:, 0:SEQ].rearrange("p (y x) -> p y x", x=GRID_W)
                v.tensor_scalar(dst, src, w[:, 4:5], None, ALU.mult).then_inc(*done("conv_tap", (m, 4)))
                last = 4
                for tap in (0, 1, 2, 3, 5, 6, 7, 8):
                    dy, dx = tap // 3 - 1, tap % 3 - 1
                    ys, xs_ = slice(max(0, -dy), ROWS - max(0, dy)), slice(max(0, -dx), GRID_W - max(0, dx))
                    yi, xi = slice(max(0, dy), ROWS - max(0, -dy)), slice(max(0, dx), GRID_W - max(0, -dx))
                    v.wait_ge(*after("conv_tap", (m, last)))
                    v.scalar_tensor_tensor(dst[:, ys, xs_], src[:, yi, xi], w[:, tap:tap + 1], dst[:, ys, xs_],
                                           ALU.mult, ALU.add)\
                        .then_inc(*(done("conv", m, bank_of=t) if tap == 8 and m >= C0 else
                                    done("conv_tap", (m, tap), bank_of=t if tap == 8 else None)))
                    last = tap
                if m < C0:
                    src, dst = ctx_bank[m % 2][:, 0:CTX], buf[:, SEQ:]
                    v.tensor_scalar(dst, src, w[:, 4:5], None, ALU.mult).then_inc(*done("conv_tap", (m, "c")))
                    v.wait_ge(*after("conv_tap", (m, "c")))
                    v.scalar_tensor_tensor(dst[:, 1:], src[:, 0:CTX - 1], w[:, 3:4], dst[:, 1:], ALU.mult, ALU.add)\
                        .then_inc(*done("conv_tap", (m, "l")))
                    v.wait_ge(*after("conv_tap", (m, "l")))
                    v.scalar_tensor_tensor(dst[:, 0:CTX - 1], src[:, 1:], w[:, 5:6], dst[:, 0:CTX - 1], ALU.mult, ALU.add)\
                        .then_inc(*done("conv", m))

            def step_sizes():
                n = [0]

                def link(ins, *keys):
                    n[0] += 1
                    ins.then_inc(*done("dt_step", n[0], *keys))
                    v.wait_ge(*after("dt_step", n[0]))

                e, q, z2 = dt[1], dt[2], dt[3]
                v.wait_ge(*after("dt_act", "exp"))
                v.tensor_scalar(dt_small[:, 1:2], dt_small[:, 0:1], -1.0, None, ALU.mult)
                link(v.tensor_scalar(q[:], e[:], 2.0, None, ALU.add))
                link(v.reciprocal(q[:], q[:]))
                link(v.tensor_tensor(e[:], e[:], q[:], ALU.mult))
                link(v.tensor_tensor(z2[:], e[:], e[:], ALU.mult))
                link(v.tensor_scalar(q[:], z2[:], 1.0 / 19, None, ALU.mult))
                for k in range(8, 0, -1):
                    link(v.scalar_tensor_tensor(q[:], q[:], 1.0 / (2 * k + 1), z2[:], ALU.add, ALU.mult))
                link(v.scalar_tensor_tensor(q[:], q[:], 1.0, e[:], ALU.add, ALU.mult))
                link(v.tensor_scalar(e[:], dt_raw[:], 0.0, None, ALU.max))
                link(v.scalar_tensor_tensor(e[:], q[:], 2.0, e[:], ALU.mult, ALU.add))
                link(v.tensor_scalar(q[:], e[:], dt_small[:, 1:2], None, ALU.mult))
                for s in (slice(0, SEQ), slice(SEQ, SEQ + CTX)):
                    link(v.tensor_tensor_scan(z2[:, s], q[:, s], q[:, s], 0.0, ALU.add, ALU.bypass))
                    link(v.tensor_tensor_scan(dt_raw[:, s][:, ::-1], q[:, s][:, ::-1], q[:, s][:, ::-1], 0.0,
                                              ALU.add, ALU.bypass))
                sel = table[:, C_SEL:C_SEL + 1]
                link(v.scalar_tensor_tensor(dt_raw[:], dt_raw[:], sel, dt_raw[:], ALU.mult, ALU.subtract))
                link(v.scalar_tensor_tensor(cum[:], z2[:], sel, dt_raw[:], ALU.mult, ALU.subtract))
                link(v.scalar_tensor_tensor(dt_small[:, 3:4], cum[:, SEQ:SEQ + 1], sel, cum[:, SEQ:SEQ + 1],
                                            ALU.mult, ALU.subtract))
                link(v.scalar_tensor_tensor(dt_small[:, 2:3], cum[:, SEQ + CTX - 1:], sel, dt_small[:, 3:4],
                                            ALU.mult, ALU.subtract))
                v.tensor_scalar(e[:, 0:SEQ], e[:, 0:SEQ], 1e-18, None, ALU.max).then_inc(*done("dt_cum", 0))
                v.wait_ge(*after("dt_act", "end"))
                v.tensor_tensor(e[:, SEQ:], e[:, SEQ:], dt[2][:, SEQ:], ALU.mult)
                v.wait_ge(*after("dt_act", "ln"))
                v.tensor_tensor(e[:, 0:SEQ], dt[3][:, 0:SEQ], cum[:, 0:SEQ], ALU.subtract).then_inc(*done("dt_bias", 0))
                v.wait_ge(*after("dt_tok", 0))

            def masked_diagonals(hd):
                v.wait_ge(*after("ssd_rows", hd))
                for d, neg in enumerate((C_NEGF, C_NEGB)):
                    ins = v.tensor_tensor(diag[hd % 2][:, d], bank[2 * (hd % 2) + d].rearrange("p (i f) -> p i f", f=P),
                                          table[:, neg:neg + P].unsqueeze(1).broadcast_to([P, 4, P]), ALU.add)
                ins.then_inc(*done("ssd_diag", hd))

            def head(hd):
                e, ed, dg = decay[hd % 2], decay_d[hd % 2], diag[hd % 2]
                v.wait_ge(*after("ssd_exp", hd))
                v.tensor_tensor(ed, ed, dg[:, 1], ALU.add).then_inc(*done("ssd_sum", hd))
                v.wait_ge(*after("ssd_sum", hd))
                if hd % 6 == 0:
                    v.wait_ge(*after("cbt", (hd // 6, 3)))
                v.tensor_tensor(e[:, :, :], e[:, :, :], cbt[:, :, :], ALU.mult).then_inc(*done("ssd_cb", hd))
                v.wait_ge(*after("ssd_cb", hd))
                v.scalar_tensor_tensor(ed, ident.unsqueeze(1).broadcast_to([P, 4, P]), par1[:, P1_D + hd:P1_D + hd + 1],
                                       ed, ALU.mult, ALU.add).then_inc(*done("ssd_m", hd))
                v.wait_ge(*after("ssd_row_exp", hd))
                cd = c_dec[hd % 2][:, :, :]
                v.tensor_tensor(cd, cd, c_x[:, hd // 6].unsqueeze(1).broadcast_to([P, 2, SEQ]), ALU.mult)\
                    .then_inc(*done("ssd_c", hd))

            def gate_tile(t):
                v.wait_ge(*after("ssd_y", 2 * t + 1))
                v.tensor_tensor(zs[:, t], zs[:, t], bank[4 + t % 2], ALU.mult).then_inc(*done("ssd_gated", t))

            def group_norm(g):
                v.wait_ge(*after("inverse", ("ssd", g)))
                for t in range(3 * g, 3 * g + 3):
                    v.scalar_tensor_tensor(zs[:, t], zs[:, t], par1[:, P1_SSD + t:P1_SSD + t + 1], inv_rms[:],
                                           ALU.mult, ALU.mult).then_inc(*done("mix1", FT4 + t))

            prepare()
            if 1 in blocks:
                first_block_dve()
            else:
                prepare_angles()
            if 1 not in blocks:
                v.wait_ge(ld["h"], 16)
                for k in range(KT):
                    v.tensor_copy(h[:, k], h[:, k]).then_inc(*done("h_new", ((0, 0), k)))

            def gains(layer, n):
                return par2[:, layer, P2_NORM + 8 * n:P2_NORM + 8 * n + 8]

            before = None
            for layer in range(DEPTH):
                for s in range(4):
                    q = (layer, s)
                    if before is None and 1 in blocks:
                        boundary("first", None, q, par1[:, P1_FIN:P1_FIN + KT], gains(layer, 2 * s))
                    elif before is None:
                        boundary(None, None, q, None, gains(layer, 2 * s))
                    else:
                        y = y_over_x if before[1] in (0, 2) else y_dyn
                        boundary(before, y, q, gains(before[0], 2 * before[1] + 1), gains(layer, 2 * s))
                    v.wait_ge(*after("inverse", ("pre", q)))
                    if s in (0, 2):
                        gu = ("gu", layer, s // 2)
                        for j in range(FT):
                            t = first_tile[gu] + 2 * j
                            v.wait_ge(*after("product", (gu, 2 * j)))
                            v.tensor_tensor(tmp[0][:], acc[t % 4][:], inv_rms[:], ALU.mult)\
                                .then_inc(*done("gate_scaled", (q, j), bank_of=t))
                            v.wait_ge(*after("product", (gu, 2 * j + 1)))
                            v.tensor_tensor(tmp[2][:], acc[(t + 1) % 4][:], inv_rms[:], ALU.mult)\
                                .then_inc(*done("up_scaled", (q, j), bank_of=t + 1))
                            v.wait_ge(*after("up_scaled", (q, j)))
                            v.wait_ge(*after("silu", (q, j)))
                            v.tensor_tensor(tmp[1][:], tmp[0][:], tmp[2][:], ALU.mult)\
                                .then_inc(*done("act_formed", (q, j)))
                            v.wait_ge(*after("act_high", (q, j)))
                            v.tensor_tensor(act_lo[:, j], tmp[1][:], act_hi[:, j].bitcast(F32), ALU.subtract)\
                                .then_inc(*done("act_low", (q, j)))
                        for m in range(KT):
                            sq_add("y_sq", q, m)
                    elif s == 1:
                        for m in range(IN_T):
                            t = first_tile["in2", layer] + m
                            v.wait_ge(*after("product", (("in2", layer), m)))
                            v.tensor_tensor(z[:, m], acc[t % 4][:], inv_rms[:], ALU.mult)\
                                .then_inc(*done("z", (layer, m), bank_of=t))
                        hgrn(layer)
                        attention(layer)
                        gating(layer)
                        for m in range(KT):
                            sq_add("y_sq", q, m)
                    else:
                        v.wait_ge(*after("ple_high", layer))
                        v.tensor_tensor(ple_lo[:, :, :], ple_raw[:, :, :], ple_hi[:, :, :].bitcast(F32), ALU.subtract)\
                            .then_inc(*done("ple_low", layer))
                        for m in range(KT):
                            t = first_tile["gate", layer] + m
                            v.wait_ge(*after("product", (("gate", layer), m)))
                            if m >= 2:
                                v.wait_ge(*after("gate2", (layer, m - 2)))
                            v.tensor_tensor(tmp[m % 2][:], acc[t % 4][:], inv_rms[:], ALU.mult)\
                                .then_inc(*done("gate2_scaled", (layer, m), bank_of=t))
                        for m in range(KT):
                            t = first_tile["proj", layer] + m
                            v.wait_ge(*after("product", (("proj", layer), m)))
                            v.wait_ge(*after("gate2", (layer, m)))
                            v.tensor_tensor(y_dyn[:, m], y_dyn[:, m], acc[t % 4][:], ALU.mult)\
                                .then_inc(*done("y_formed", (q, m), bank_of=t))
                            if m:
                                sq_add("y_sq", q, m - 1)
                        sq_add("y_sq", q, KT - 1)
                    before = q
            boundary(before, y_dyn, "last", gains(DEPTH - 1, 7), None)

        @block.tensor
        def _(pe):
            def product(stage, tiles, k_tiles, hi, lo, low_ready, after_first=None, side_by_side=False):
                side = 3 if side_by_side else 1
                order = []
                for k in range(k_tiles):
                    order += [(m, k) for m in range(side)]
                    if side_by_side and k % 2:
                        order.append((side, k // 2))
                group_end = len(order)
                order += [(m, k) for m in range(side, tiles) for k in range(k_tiles) if (m, k) not in order]
                for n, (m, k) in enumerate(order):
                    t = first_tile[stage] + m
                    dst = acc[t % 4][:]
                    if k == 0 and t >= 4:
                        pe.wait_ge(*(bank_free(t - 4) or (ev.sem("product"), 1)))
                    b = first_block[stage] + m * k_tiles + k
                    u, i = b // UNIT, b % UNIT
                    if i == 0 or n == 0:
                        pe.wait_ge(unit_split, u + 1)
                    if m == 0:
                        pe.wait_ge(*low_ready(k))
                    w_h, w_l = whi[:, u % SLOTS, i], wlo[:, u % SLOTS, i]
                    x_h, x_l = (hi[:, k], lo[:, k]) if hi is not None else (mix1_hi(k), mix1_lo(k))
                    pe.matmul(dst, w_h, x_h, start=(k == 0), stop=False)
                    pe.matmul(dst, w_h, x_l, start=False, stop=False)
                    mm = pe.matmul(dst, w_l, x_h, start=False, stop=(k == k_tiles - 1))
                    keys = [("unit", u)] if i == UNIT - 1 else []
                    if k == k_tiles - 1:
                        keys.append((stage, m))
                    if keys:
                        mm.then_inc(*done("product", *keys))
                    if n + 1 == group_end and after_first:
                        after_first()

            def sum_features(key, last, dst=None, srcs=None, lhs=None):
                srcs = srcs or [sq_sum[:]]
                pe.wait_ge(*last)
                for n, s in enumerate(srcs):
                    mm = pe.matmul(norm_bank[:] if dst is None else dst, ones if lhs is None else lhs, s,
                                   start=(n == 0), stop=(n == len(srcs) - 1))
                mm.then_inc(*done("summed", key))

            def turn(dst, src):
                for n in range(4):
                    mm = pe.transpose(dst[:, n * P:(n + 1) * P], src[:, n * P:(n + 1) * P], ident)
                return mm

            def hgrn(layer):
                pe.wait_ge(*after("z", (layer, IN_T - 1)))
                for g in range(2):
                    turn(mix_bank[g], z[:, 4 + g]).then_inc(*done("hg_vt", (layer, g)))
                for n in range(len(LEVELS) + 1):
                    if n == 0:
                        pe.wait_ge(*after("hg_gate", (layer, 1)))
                    else:
                        pe.wait_ge(*after("hg_dec", (layer, n)))
                    if n == 1:
                        pe.wait_ge(*after("hg_vtok", (layer, 1)))
                    if n >= 2:
                        pe.wait_ge(*after("hg_masked", (layer, n - 2, 3)))
                    qs, ks = (z[:, 0:2], key_k[:, :, :]) if n == 0 else (q_dec[:, :, :], k_dec[:, :, :])
                    for e in range(4):
                        g, s = e // 2, slice(64 * (e % 2), 64 * (e % 2) + 64)
                        for c in range(4):
                            cs = slice(c * P, (c + 1) * P)
                            mm = pe.matmul(bank[4 * (n % 2) + e][:, cs], ks[s, g, cs], qs[s, g, cs],
                                           start=True, stop=True)
                    mm.then_inc(*done("hg_scores", (layer, n)))
                pe.wait_ge(*after("hg_dec", (layer, "end")))
                pe.wait_ge(*after("hg_masked", (layer, len(LEVELS), 3)))
                for g in range(2):
                    turn(bank[4 + g], k_dec[:, g]).then_inc(*done("hg_kt", (layer, g)))
                for g in range(2):
                    pe.wait_ge(*after("hg_ktok", (layer, g)))
                    for n in range(3):
                        mm = pe.matmul(acc[g][:, n * P:(n + 1) * P], k_tok[:, g, n], v_tok[:, g, n],
                                       start=True, stop=True)
                    mm.then_inc(*done("hg_kv", (layer, g)))
                for g in range(2):
                    pe.wait_ge(*after("hg_state", (layer, g, 2, 1)))
                    for n in range(4):
                        cs = slice(n * P, (n + 1) * P)
                        if n:
                            pe.matmul(acc[2 + g][:, cs], state[:, n - 1, g], q_dec[:, g, cs], start=True, stop=False,
                                      skip_group_check=True)
                        for e in range(2):
                            s = slice(64 * e, 64 * e + 64)
                            mm = pe.matmul(acc[2 + g][s, cs], v_tok[:, g, n, s], hg_att[:, 2 * g + e, cs],
                                           start=(n == 0), stop=True, skip_group_check=True)
                    mm.then_inc(*done("hg_o", (layer, g)))
                for g in range(2):
                    sum_features((layer, "hg", g), after("hg_o_sq", (layer, g)), mix_bank[g][:], [diff[:, g]], blk64)

            def attention(layer):
                for i in range(5):
                    zi = z[:, 12 if i == 0 else 7 + i]
                    if i >= 4:
                        pe.wait_ge(*after("att_roped", (layer, i - 4)))
                    pe.matmul(acc[i % 4][:], rot, zi, start=True, stop=True).then_inc(*done("att_rot", (layer, i)))
                turn(mix_bank[2], z[:, 13]).then_inc(*done("att_vt", layer))

                def score(i):
                    t, n = divmod(i, 4)
                    if i == 0:
                        pe.wait_ge(*after("att_roped", (layer, 4)))
                    if i >= 2:
                        pe.wait_ge(*after("att_masked", (layer, i - 2)))
                    w0 = P if n == 0 else 0
                    for e in range(2):
                        s = slice(64 * e, 64 * e + 64)
                        mm = pe.matmul(acc[2 * (i % 2) + e][:, w0:2 * P], z[s, 8 + t, n * P:(n + 1) * P],
                                       z[s, 12, (n - 1) * P + w0:(n + 1) * P], start=True, stop=True)
                    mm.then_inc(*done("att_scores", (layer, i)))

                def turn_probs(i):
                    pe.wait_ge(*after("att_probs", (layer, i)))
                    if i >= 2:
                        pe.wait_ge(*after("att_pt", (layer, i - 2)))
                    for e in range(2):
                        for k in range(1 if i % 4 == 0 else 0, 2):
                            c = (2 * e + k) * P
                            mm = pe.transpose(turn_bank[i % 2][:, c:c + P], scores[i % 3][:, e, k * P:(k + 1) * P], ident)
                    mm.then_inc(*done("att_turned", (layer, i)))

                def values(i):
                    t, n = divmod(i, 4)
                    pe.wait_ge(*after("att_pt", (layer, i)))
                    if n == 0 and t >= 2:
                        pe.wait_ge(*after("mix_low", (layer, 2 + t - 2)))
                    k0 = 1 if n == 0 else 0
                    for e in range(2):
                        s = slice(64 * e, 64 * e + 64)
                        for k in range(k0, 2):
                            mm = pe.matmul(mix_bank[t % 2][s, n * P:(n + 1) * P], va_tok[:, n - 1 + k, s],
                                           probs_t[i % 2][:, e, k], start=(k == k0), stop=(k == 1))
                    mm.then_inc(*done("att_o", (layer, "part", i), *([(layer, t)] if n == 3 else [])))

                pe.wait_ge(*after("att_vtok", layer))
                score(0)
                score(1)
                for i in range(16 + 1):
                    if i + 2 < 16:
                        score(i + 2)
                    if i < 16:
                        turn_probs(i)
                    if i:
                        values(i - 1)

            def gating(layer):
                pe.wait_ge(*after("gelu", layer))
                pe.wait_ge(*after("mix_low", (layer, 5)))
                for g in range(2):
                    mm = pe.matmul(mix_bank[0][:], ones, z[:, 16 + g], start=(g == 0), stop=(g == 1))
                mm.then_inc(*done("ln_mean", layer))
                sum_features((layer, "ln"), after("ln_sq", layer), mix_bank[1][:], [ln_sq[:, 0], ln_sq[:, 1]])
                for g in range(2):
                    pe.wait_ge(*after("ln_out", (layer, g)))
                    turn(acc[g], ln_x[:, g]).then_inc(*done("sg_vt", (layer, g)))
                pe.wait_ge(*after("sg_tok", (layer, 1)))
                pe.wait_ge(*after("sg_w", layer))
                for g in range(2):
                    for n in range(4):
                        for e in range(2):
                            s, f = slice(64 * e, 64 * e + 64), (2 * g + e) * 64
                            mm = pe.matmul(mix_bank[2 * g][s, n * P:(n + 1) * P], sg_tok[:, n, f:f + 64], sg_w[:, 2 * g + e],
                                           start=True, stop=True)
                    mm.then_inc(*done("sg_mixed", (layer, g)))

            def first_block_pe():
                sum_features("x", after("x_sq", "x"), None, [x_sq[:, k] for k in range(KT)])
                sum_features("ctx", after("x_sq", "ctx"), mix_bank[0][:, 0:CTX], [ctx_sq[:, k] for k in range(KT)])
                pe.wait_ge(*after("c_low", 0))
                for m in range(ADA_T):
                    u = first_block["ada"] // UNIT + m
                    pe.wait_ge(unit_split, u + 1)
                    dst = bank[7][:, 2 * m:2 * m + 2]
                    for k in range(KT):
                        w_h, w_l = whi[:, u % SLOTS, k], wlo[:, u % SLOTS, k]
                        pe.matmul(dst, w_h, c_hi[:, k], start=(k == 0), stop=False)
                        pe.matmul(dst, w_h, c_lo[:, k], start=False, stop=False)
                        mm = pe.matmul(dst, w_l, c_hi[:, k], start=False, stop=(k == KT - 1))
                    mm.then_inc(*done("product", ("unit", u), ("ada", m)))
                for m in range(IN1A_T):
                    in_tile("in1a", m, m < C0)
                    if B0 <= m - 2 < C0:
                        turn_conv(m - 2)
                states()
                for m in range(ST):
                    in_tile("in1b", m, False)
                fourier()
                product("four", FT4, FT4, four_hi, four_lo, lambda k: after("four_low", k))
                ssd()
                product("out1", KT, MIX_T, None, None, lambda k: after("mix1_low", k))
                sum_features("first", after("sq_added", ("res_sq", "first", KT - 1)))

            def in_tile(stage, m, with_ctx):
                t, u = first_tile[stage] + m, first_block[stage] // UNIT + m
                dst, cdst = acc[t % 4][:], ctx_bank[m % 2][:, 0:CTX]
                if counted and t - 4 >= ADA_T:
                    pe.wait_ge(*bank_free(t - 4))
                if with_ctx and m >= 2:
                    pe.wait_ge(*(after("dt_raw", 1) if m == 2 else after("conv", m - 2)))
                elif with_ctx and m == 0:
                    pe.wait_ge(*after("inverse", "ctx"))
                pe.wait_ge(unit_split, u + 1)
                for k in range(KT):
                    if m == 0 and stage == "in1a":
                        pe.wait_ge(*after("in_low", (k, 1)))
                    w_h, w_l = whi[:, u % SLOTS, k], wlo[:, u % SLOTS, k]
                    first, last = k == 0, k == KT - 1
                    pe.matmul(dst, w_h, xhi[:, k], start=first, stop=False)
                    pe.matmul(dst, w_h, xlo[:, k], start=False, stop=False)
                    if with_ctx:
                        pe.matmul(cdst, w_h, ctx_hi[:, k], start=first, stop=False)
                        pe.matmul(cdst, w_h, ctx_lo[:, k], start=False, stop=False)
                        pe.matmul(cdst, w_l, ctx_hi[:, k], start=False, stop=last)
                    mm = pe.matmul(dst, w_l, xhi[:, k], start=False, stop=last)
                mm.then_inc(*done("product", ("unit", u), (stage, m)))

            def turn_conv(m):
                pe.wait_ge(*after("conv_out", m))
                if m > B0:
                    pe.wait_ge(*after("conv_tok", m - 1))
                buf = conv[m % 2]
                if m >= XS0:
                    turn(mix_bank[1], buf)
                for i in range(2):
                    mm = pe.transpose(mix_bank[2][:, i * P:(i + 1) * P], buf[:, SEQ + i * P:SEQ + (i + 1) * P], ident)
                mm.then_inc(*done("conv_turned", m))

            def states():
                pe.wait_ge(*after("dt_bias", 0))
                pe.wait_ge(*after("conv_tok", C0 - 1))
                turn(bank[4], dt[1])
                for i in range(2):
                    mm = pe.transpose(bank[5][:, i * P:(i + 1) * P], dt[1][:, SEQ + i * P:SEQ + (i + 1) * P], ident)
                mm.then_inc(*done("dt_turned", 0))
                for d in range(2):
                    pe.wait_ge(*after("ctx_weighted", d))
                    for g in range(GROUPS):
                        if d:
                            pe.wait_ge(*after("h0", (0, g)))
                        for i in range(2):
                            mm = pe.matmul(bank[4 + g][:, 0:384], ctx_b_tok[:, i, g * P:(g + 1) * P],
                                           ctx_weighted[:, i, g * 384:(g + 1) * 384], start=(i == 0), stop=(i == 1))
                        mm.then_inc(*done("state", (d, g)))

            def fourier():
                pe.wait_ge(ld["dft_c"], 16)
                pe.wait_ge(*after("h0", (1, GROUPS - 1)))
                for i in range(4):
                    if i >= 2:
                        pe.wait_ge(*after("four_tok_out", i - 2))
                    for j in range(FT4):
                        mm = pe.matmul(bank[4 + 2 * (i % 2) + j // 2][:, (j % 2) * 2 * P:(j % 2 + 1) * 2 * P],
                                       u_in[:, j, i * P:(i + 1) * P], dft_c[:, :], start=True, stop=True)
                    mm.then_inc(*done("four_tok", i))
                pe.wait_ge(*after("four_tok_out", 3))
                pe.wait_ge(ld["dft_t"], 16)
                for j in range(FT4):
                    for n in range(8):
                        c, i = n % 2, n // 2
                        mm = pe.matmul(bank[4 + j], four_tok[:, i, j, c], dft_t[:, c, i], start=(n == 0), stop=(n == 7))
                    mm.then_inc(*done("four", j))

            def ssd():
                def rows(hd):
                    if hd >= 2:
                        pe.wait_ge(*after("ssd_row_exp", hd - 2))
                    elif hd == 0:
                        pe.wait_ge(*after("cum_low", 0))
                    for d in range(2):
                        r = d * HEADS + hd
                        one_row = ident_r[:, r:r + 1].broadcast_to([P, P])
                        for n, part in enumerate((cum_hi, cum_lo)):
                            mm = pe.matmul(bank[2 * (hd % 2) + d], one_row, part[:], start=(n == 0), stop=(n == 1))
                    mm.then_inc(*done("ssd_rows", hd))

                def cb(g):
                    for i in range(4):
                        if i >= 2:
                            pe.wait_ge(*after("cbt", (g, i - 2)))
                        elif i == 0 and g:
                            pe.wait_ge(*after("ssd_cb", 6 * g - 1))
                        pe.matmul(bank[6 + i % 2], b_x[:, g, i * P:(i + 1) * P], c_x[:, g], start=True, stop=True)\
                            .then_inc(*done("cb", (g, i)))

                def y(hd):
                    dst = bank[4 + hd // 2 % 2][64 * (hd % 2):64 * (hd % 2) + 64, :]
                    if hd >= 4 and hd % 2 == 0:
                        pe.wait_ge(*after("ssd_gated", hd // 2 - 2))
                    s = slice(64 * hd, 64 * hd + 64)
                    pe.wait_ge(*after("ssd_m", hd))
                    for i in range(4):
                        pe.matmul(dst, x_tok[:, i, s], decay[hd % 2][:, i], start=(i == 0), stop=False)
                    pe.wait_ge(*after("ssd_c", hd))
                    for d in range(2):
                        mm = pe.matmul(dst, h0[d][:, s], c_dec[hd % 2][:, d], start=False, stop=(d == 1))
                    mm.then_inc(*done("ssd_y", hd))

                def group_sum(g):
                    sum_features(("ssd", g), after("ssd_sq", (g, 2)), bank[6], [tmp[t][:] for t in range(3)])

                pe.wait_ge(*after("four_low", 3))
                rows(0)
                rows(1)
                cb(0)
                for hd in range(HEADS):
                    if hd + 2 < HEADS:
                        rows(hd + 2)
                    if hd % 6 == 2 and hd > 6:
                        group_sum(hd // 6 - 1)
                    y(hd)
                    if hd % 6 == 5 and hd + 1 < HEADS:
                        cb((hd + 1) // 6)
                group_sum(GROUPS - 1)

            pe.wait_ge(ld["table"], 16)
            if 1 in blocks:
                first_block_pe()
            for layer in range(DEPTH):
                for s in range(4):
                    q = (layer, s)
                    x_low = lambda k: after("x_low", (q, k))
                    pre_sum = lambda: sum_features(("pre", q), after("sq_added", ("h_sq", q, KT - 1)))
                    if s in (0, 2):
                        product(("gu", layer, s // 2), 2 * FT, KT, xhi, xlo, x_low, pre_sum, True)
                        product(("down", layer, s // 2), KT, FT, act_hi, act_lo, lambda k: after("act_low", (q, k)))
                    elif s == 1:
                        product(("in2", layer), IN_T, KT, xhi, xlo, x_low, pre_sum, True)
                        hgrn(layer)
                        attention(layer)
                        gating(layer)
                        product(("out2", layer), KT, KT, xhi, xlo, lambda k: after("mix_low", (layer, k)))
                    else:
                        product(("gate", layer), KT, KT, xhi, xlo, x_low, pre_sum, True)
                        product(("proj", layer), KT, PLE_T, ple_hi, ple_lo, lambda k: after("ple_low", layer))
                    sum_features(("post", q), after("sq_added", ("y_sq", q, KT - 1)))
    return ev.values, ev.freed


def blocks_of(w, rows=None):
    k, m = w.shape[0] // P, w.shape[1] // P
    return w.reshape(k, P, m, P).transpose(2, 0, 1, 3).reshape(m * k, P, P)


def columns(x):
    return x.reshape(-1, P).T


def feature_major(x):
    t, f = x.shape
    return np.ascontiguousarray(x.T.reshape(f // P, P, t).transpose(1, 0, 2).reshape(P, -1))


HEAD_ORDER = np.concatenate([np.r_[64 * t:64 * t + 64, 64 * (4 + t):64 * (4 + t) + 64] for t in range(4)])


def lay_out_second(i, into):
    weights = []
    order = np.r_[0:1024, 1024 + HEAD_ORDER, 1536:2304]
    order_out = np.r_[0:256, 256 + HEAD_ORDER, 768:1024]
    for l in range(DEPTH):
        for s in range(2):
            gu = blocks_of(i[f"ffn{s + 1}_gate_up_2"][l]).reshape(2, FT, KT, P, P)
            weights.append(gu.transpose(1, 0, 2, 3, 4).reshape(-1, P, P))
            weights.append(blocks_of(i[f"ffn{s + 1}_down_2"][l]))
            if s == 0:
                weights.append(blocks_of(i["w_in_2"][l][:, order]))
                weights.append(blocks_of(i["w_out_2"][l][order_out]))
        weights.append(blocks_of(i["ple_gate_2"][l]))
        weights.append(blocks_of(i["ple_proj_2"][l]))
    par = np.zeros((DEPTH, P, P2_COLS), np.float32)
    mix = np.zeros((DEPTH, P, M2_COLS), np.float32)
    for l in range(DEPTH):
        par[l, :, P2_NORM:P2_NORM + 64] = columns(i["norm_gains_2"][l].reshape(-1))
        par[l, :, P2_HG] = np.tile(i["hgrn_norm_gain_2"][l], 2)
        par[l, :, P2_LB:P2_LB + 4] = columns(i["hgrn_lb_logits_2"].reshape(-1))
        par[l, :, P2_LN:P2_LN + 2] = columns(i["sg_ln_gain_2"][l])
        par[l, :, P2_SINK:P2_SINK + 8] = i["attn_sinks_2"][l].reshape(2, 4).T.reshape(-1)[None]
        mix[l, :, :2 * P] = np.repeat(i["sg_spatial_b_2"][l].reshape(2, 2, P).transpose(1, 0, 2), 64, 0).reshape(P, -1)
        mix[l, :, 2 * P:] = i["sg_spatial_w_2"][l].transpose(2, 0, 1).reshape(P, -1)
    into["par2"], into["mixpar"] = par, mix
    into["ple"] = np.stack([feature_major(i["p_2"][l, 0]) for l in range(DEPTH)])
    into["positions"] = i["positions_2"]
    return weights


def lay_out_first(i, into):
    w = i["w_in"][0]
    u, zf, zs, xs, b, c, dt = np.split(w, np.cumsum([D_FOUR, D_FOUR, D_SSD, D_SSD, 512, 512]), axis=1)
    dt = np.concatenate([dt, np.zeros((D, P - DT_ROWS), np.float32)], axis=1)
    weights = [blocks_of(i["w_ada"][0]), blocks_of(np.concatenate([dt, b, xs, c, u, zf, zs], axis=1)),
               blocks_of(i["w_fourier"][0]), blocks_of(i["w_out"][0])]
    par = np.zeros((P, P1_COLS), np.float32)
    par[:, P1_NORM:P1_NORM + KT] = columns(i["norm_w"][0])
    par[:, P1_ADA:P1_ADA + ADA_T] = columns(i["b_ada"][0])
    order = np.r_[D_SSD:D_SSD + 512, 0:D_SSD, D_SSD + 512:D_SSD + 1024]
    taps = i["conv_w"][0].reshape(9, -1)[:, order]
    par[:, P1_CONV:P1_CONV + 180] = taps.reshape(9, 20, P).transpose(2, 1, 0).reshape(P, 180)
    par[:, P1_CB:P1_CB + 20] = columns(i["conv_b"][0][order])
    par[:, P1_SSD:P1_SSD + ST] = columns(i["ssd_norm_w"][0])
    par[:, P1_BF:P1_BF + FT4] = columns(i["b_fourier"][0])
    par[:, P1_FIN:P1_FIN + KT] = columns(i["final_norm_w"])
    par[:, P1_C:P1_C + 2 * KT] = np.stack([columns(i["c"][0]), columns(i["c_ctx"])], 2).reshape(P, -1)
    par[:, P1_D:P1_D + HEADS] = i["d_skip"][0][None]
    par[:DT_ROWS, P1_DTB] = i["dt_bias"][0].reshape(-1)
    par[:DT_ROWS, P1_DTB + 1] = i["a_log"][0].reshape(-1)
    into["par1"] = par
    into["x"], into["ctx"] = feature_major(i["x"][0]), feature_major(i["ctx"][0])
    return weights


def stream_of(weights, units):
    w = np.concatenate(weights)
    pad = units * UNIT - len(w)
    if pad:
        w = np.concatenate([w, np.zeros((pad, P, P), np.float32)])
    return np.ascontiguousarray(w.reshape(units, UNIT, P, P).transpose(0, 2, 1, 3))


def kernel(**inputs):
    import concourse.bacc as bacc
    from concourse.bass_utils import run_bass_kernel_spmd

    i = {name: np.asarray(value) for name, value in inputs.items()}
    arrays = {}
    weights = lay_out_first(i, arrays) + lay_out_second(i, arrays)
    units = stream_plan(STREAM)[2]
    arrays["stream"] = stream_of(weights, units)
    arrays["table"], arrays["masks"], arrays["dft_c"], arrays["dft_t"] = fixed_tables()

    def program(counted):
        nc = bacc.Bacc("TRN2", target_bir_lowering=False, num_devices=1)
        a = {name: nc.dram_tensor(f"in_{name}", v.shape, mybir.dt.from_np(v.dtype), kind="ExternalInput").ap()
             for name, v in arrays.items()}
        out = nc.dram_tensor("out", (P, KT * SEQ), F32, kind="ExternalOutput").ap()
        return nc, build(nc, a, out.rearrange("p (k t) -> p k t", t=SEQ), counted, STREAM)

    _, counted = program(None)
    nc, _ = program(counted)
    r = run_bass_kernel_spmd(nc, [{f"in_{name}": v for name, v in arrays.items()}], core_ids=[0])
    got = r.results[0]["out"].reshape(P, KT, SEQ)
    return np.ascontiguousarray(got.transpose(2, 1, 0).reshape(1, SEQ, D))
```

```python
from contextlib import ExitStack

import numpy as np

import concourse.bass as bass
from concourse import mybir

F32 = mybir.dt.float32
F32R = mybir.dt.float32r
I32 = mybir.dt.int32
U8 = mybir.dt.uint8
ALU = mybir.AluOpType
ACT = mybir.ActivationFunctionType
AX = mybir.AxisListType

P = 128
SEQ = 512
CTX = 256
D = 1024
KT = D // P
EPS = 1e-6
SLOTS = 4
UNIT = 8

DEPTH = 2
FF = 2816
FT = FF // P
IN_T = 2304 // P
PLE = 256
SCALE = 64 ** -0.5
MASK_VALUE = -1e30
LB_FLOOR = 1e-30
PLE_T = PLE // P

D_FOUR = 512
D_SSD = 1536
HEADS = 24
GROUPS = 4
GRID_W = 64
ROWS = SEQ // GRID_W
FT4 = D_FOUR // P
ST = D_SSD // P
ADA_T = 3 * KT
DT_ROWS = 2 * HEADS

MIX_T = FT4 + ST
DT0, B0, XS0, C0, U0, ZF0, IN1A_T = 0, 1, 5, 17, 21, 25, 29
STREAM = [("ada", ADA_T, KT), ("in1a", IN1A_T, KT), ("in1b", ST, KT), ("four", FT4, FT4), ("out1", KT, MIX_T)]
for _layer in range(DEPTH):
    STREAM += [(("gu", _layer, 0), 2 * FT, KT), (("down", _layer, 0), KT, FT),
               (("in2", _layer), IN_T, KT), (("out2", _layer), KT, KT),
               (("gu", _layer, 1), 2 * FT, KT), (("down", _layer, 1), KT, FT),
               (("gate", _layer), KT, KT), (("proj", _layer), KT, PLE_T)]

WHOLE_UNITS = ADA_T * KT // UNIT


def stream_plan(stages):
    first, tile, block, tiles = {}, {}, 0, 0
    for name, n, k in stages:
        first[name], tile[name] = block, tiles
        block += n * k
        tiles += n
    units = -(-block // UNIT)
    return first, tile, -(-units // SLOTS) * SLOTS


def accumulators(stages):
    bank, earlier, last = [], [], {}
    for name, n, _ in stages:
        for m in range(n):
            t = len(bank)
            bank.append(m % 2 if name[0] == "in2" and m >= 4 else t % 4)
            earlier.append(last.get(bank[t]))
            last[bank[t]] = t
    return bank, earlier


class Events:

    def __init__(self, nc, ctx, counted):
        self.nc, self.ctx, self.counted = nc, ctx, counted
        self.sems, self.n, self.values, self.freed = {}, {}, {}, {}

    def sem(self, name):
        if name not in self.sems:
            self.sems[name] = self.ctx.enter_context(self.nc.semaphore(name))
            self.n[name] = 0
        return self.sems[name]

    def done(self, name, *keys, bank_of=None):
        s = self.sem(name)
        self.n[name] += 1
        for key in keys:
            assert (name, key) not in self.values, (name, key)
            self.values[name, key] = self.n[name]
        if bank_of is not None:
            self.freed[bank_of] = (name, self.n[name])
        return s, 1

    def after(self, name, key):
        if self.counted is None:
            return self.sem(name), 1
        return self.sem(name), self.counted[0][name, key]

    def bank_free(self, tile):
        if self.counted is None:
            return None
        name, value = self.counted[1][tile]
        return self.sem(name), value


LEVELS = [1, 2, 4, 8, 16, 32, 64]
C_ID, C_ONE, C_BLK, C_ROT, C_TRI, C_NEGF, C_NEGB = range(0, 7 * P, P)
C_AMASK = 7 * P
C_INV = C_AMASK + 2 * P
C_SEL = C_INV + 1
C_COLS = C_SEL + 1


def fixed_tables():
    p, f = np.arange(P)[:, None], np.arange(P)[None, :]
    table = np.zeros((P, C_COLS), np.float32)
    table[:, C_ID:C_ID + P] = p == f
    table[:, C_ONE:C_ONE + P] = 1.0
    table[:, C_BLK:C_BLK + P] = p // 64 == f // 64
    table[:, C_ROT:C_ROT + P] = (p == f - 32) * (f % 64 >= 32) * 1.0 - (p == f + 32) * (f % 64 < 32) * 1.0
    table[:, C_TRI:C_TRI + P] = p <= f
    table[:, C_NEGF:C_NEGF + P] = np.where(f >= p, 0.0, MASK_VALUE)
    table[:, C_NEGB:C_NEGB + P] = np.where(f <= p, 0.0, MASK_VALUE)
    j = np.arange(2 * P)[None, :]
    table[:, C_AMASK:C_AMASK + 2 * P] = np.where((p + P - j >= 0) & (p + P - j < P), 0.0, MASK_VALUE)
    table[:, C_INV] = 10000.0 ** (-(np.arange(P) % 32).astype(np.float32) / np.float32(32))
    table[:, C_SEL] = np.arange(P) < HEADS
    levels = np.zeros((P, len(LEVELS) + 1, P), np.float32)
    levels[:, 0] = p == f
    for n, b in enumerate(LEVELS):
        levels[:, n + 1] = (p // (2 * b) == f // (2 * b)) & (p % (2 * b) < b) & (f % (2 * b) >= b)
    t, c = np.arange(SEQ), np.arange(64)
    full = 2 * np.pi * np.outer(t, t) / SEQ
    part = 2 * np.pi * np.outer(c, c) / 64
    norm = 1.0 / np.sqrt(SEQ * 64.0)
    blocks = np.zeros((P, 2, P))
    for h in range(2):
        s = slice(64 * h, 64 * h + 64)
        blocks[s, 0, s], blocks[s, 1, s] = np.cos(part), np.sin(part)
    dft_c = blocks.reshape(P, 2 * P).astype(np.float32)
    dft_t = np.stack([np.cos(full) * norm, -np.sin(full) * norm])
    dft_t = dft_t.reshape(2, SEQ // P, P, SEQ).transpose(2, 0, 1, 3).astype(np.float32)
    return table, levels.reshape(P, -1), dft_c, np.ascontiguousarray(dft_t.reshape(P, -1))


P2_NORM, P2_HG, P2_LB, P2_LN, P2_SINK = 0, 64, 65, 69, 71
P2_COLS = 79
M2_SGB, M2_SGW, M2_COLS = 0, 2 * P, 2 * P + 4 * P
P1_NORM, P1_ADA, P1_CONV, P1_CB, P1_SSD, P1_BF = 0, 8, 32, 32 + 180, 32 + 180 + 20, 32 + 180 + 32
P1_FIN, P1_C, P1_D, P1_DTB = P1_BF + 4, P1_BF + 12, P1_BF + 28, P1_BF + 52
P1_COLS = P1_DTB + 2


def build(nc, a, out, counted, stages):
    first_block, first_tile, units = stream_plan(stages)
    acc_of, earlier = accumulators(stages)
    ctx = ExitStack()
    with ctx:
        ev = Events(nc, ctx, counted)
        done, after, bank_free = ev.done, ev.after, ev.bank_free
        base = -(-nc.sbuf_base // 32) * 32

        def at(name, offset, shape, dt=F32):
            return nc.alloc_sbuf_tensor_at(name, [P, *shape], dt, offset=base + offset)

        def loads(*names):
            return {n: ctx.enter_context(nc.semaphore(f"loaded_{n}")) for n in names}

        KB = 1024
        raw = at("raw", 0, [SLOTS, UNIT, P])
        whi = at("whi", 16 * KB, [SLOTS, UNIT, P], F32R)
        wlo = at("wlo", 32 * KB, [SLOTS, UNIT, P], F32R)
        xhi = at("xhi", 48 * KB, [KT, SEQ], F32R)
        xlo = at("xlo", 64 * KB, [KT, SEQ], F32R)
        y_over_x = at("y_over_x", 48 * KB, [KT, SEQ])
        h = at("h", 80 * KB, [KT, SEQ])
        CONST = 96 * KB
        DYN = CONST + 15 * KB
        table = at("table", CONST, [C_COLS])
        masks = at("masks", CONST + 5 * KB, [len(LEVELS) + 1, P], U8)
        masks_f = at("masks_f", DYN + 28 * KB, [len(LEVELS) + 1, P])
        par2 = at("par2", CONST + 6 * KB, [DEPTH, P2_COLS])
        lower = at("lower", CONST + 6 * KB + 640, [DEPTH, 2, 2])
        small = at("small", CONST + 6 * KB + 704, [80])
        cos_t = at("cos_t", CONST + 7 * KB, [SEQ])
        sin_t = at("sin_t", CONST + 9 * KB, [SEQ])
        inv_rms = at("inv_rms", CONST + 11 * KB, [SEQ])
        sq_sum = at("sq_sum", CONST + 13 * KB, [SEQ])
        tmp = [at(f"tmp{i}", DYN + 88 * KB + 2 * KB * i, [SEQ]) for i in range(3)]
        SM = DYN + 94 * KB
        act_hi = at("act_hi", DYN, [FT, SEQ], F32R)
        act_lo = at("act_lo", DYN + 44 * KB, [FT, SEQ], F32R)
        y_dyn = at("y_dyn", DYN, [KT, SEQ])
        z = at("z", DYN, [IN_T, SEQ])
        mixpar = at("mixpar", DYN + 36 * KB, [M2_COLS])
        MX = DYN + 39 * KB
        gate_b = at("gate_b", MX, [2, SEQ])
        key_k = at("key_k", MX + 4 * KB, [2, SEQ])
        diff = at("diff", MX + 8 * KB, [2, SEQ])
        q_dec = at("q_dec", MX + 12 * KB, [2, SEQ])
        k_dec = at("k_dec", MX + 16 * KB, [2, SEQ])
        hg_att = at("hg_att", MX + 20 * KB, [4, SEQ])
        k_tok = at("k_tok", MX + 28 * KB, [2, 4, P])
        v_tok = at("v_tok", MX + 32 * KB, [2, 4, P])
        state = at("state", MX + 36 * KB, [3, 2, P])
        tot = at("tot", MX + 48 * KB, [2, 4])
        e_tot = at("e_tot", MX + 48 * KB + 32, [2, 4])
        hg_o = at("hg_o", MX + 40 * KB, [2, SEQ])
        va_tok = at("va_tok", MX, [4, P])
        scores = [at(f"scores{i}", MX + 2 * KB * (8 + i), [2, 2 * P]) for i in range(3)]
        probs_t = [at(f"probs_t{i}", MX + 2 * KB * (3 + i), [2, 2, P]) for i in range(2)]
        att_o = [at(f"att_o{i}", MX + 2 * KB * (5 + i), [SEQ]) for i in range(2)]
        stat = [at(f"stat{i}", MX + 14 * KB + 64 * i, [7, 2]) for i in range(3)]
        ln_sq = at("ln_sq", MX + 44 * KB, [2, SEQ])
        sg_tok = ln_sq[:, :, :].rearrange("p g (n f) -> p (g n) f", f=2 * P)
        sg_w = at("sg_w", SM, [4, P])
        ctx_raw = at("ctx_raw", DYN + 56 * KB, [KT, CTX])
        ctx_hi = at("ctx_hi", DYN + 40 * KB, [KT, CTX], F32R)
        ctx_lo = at("ctx_lo", DYN + 48 * KB, [KT, CTX], F32R)
        x_sq = at("x_sq", DYN, [KT, SEQ])
        ctx_sq = at("ctx_sq", DYN + 16 * KB, [KT, CTX])
        x_scaled = at("x_scaled", DYN, [KT, SEQ])
        ctx_scaled = at("ctx_scaled", DYN + 64 * KB, [KT, CTX])
        x_tok = at("x_tok", DYN, [4, D_SSD])
        b_x = at("b_x", DYN + 24 * KB, [4, SEQ])
        c_x = at("c_x", DYN + 32 * KB, [4, SEQ])
        zs = at("zs", DYN + 40 * KB, [ST, SEQ])
        ctx_weighted = at("ctx_weighted", DYN + 40 * KB, [2, D_SSD])
        dt = [at(f"dt{i}", DYN + (52 + 3 * i) * KB, [SEQ + CTX]) for i in range(4)]
        dt_raw = at("dt_raw", 80 * KB + 8 * KB, [SEQ + CTX])
        ctx_tok = at("ctx_tok", DYN + 64 * KB, [2, D_SSD])
        ctx_b_tok = at("ctx_b_tok", DYN + 76 * KB, [2, 4 * P])
        conv = [at(f"conv{i}", DYN + (80 + 3 * i) * KB, [SEQ + CTX]) for i in range(2)]
        zf = at("zf", DYN + 80 * KB, [FT4, SEQ])
        cum = at("cum", CONST + 7 * KB, [SEQ + CTX])
        dft_c = at("dft_c", CONST + 10 * KB, [2 * P])
        u_in = at("u_in", 80 * KB, [FT4, SEQ])
        h0 = [at("h0_f", 88 * KB, [D_SSD]), at("h0_b", DYN + 64 * KB, [D_SSD])]
        dft_t = at("dft_t", 48 * KB, [2, 4, SEQ])
        four_tok = at("four_tok", 64 * KB, [4, FT4, 2, P])
        four_hi = at("four_hi", 80 * KB, [FT4, SEQ], F32R)
        four_lo = at("four_lo", DYN + 71 * KB, [FT4, SEQ], F32R)
        cum_hi = at("cum_hi", 80 * KB, [SEQ], F32R)
        cum_lo = at("cum_lo", 82 * KB, [SEQ], F32R)
        ident_r = at("ident_r", 84 * KB, [P], F32R)
        cbt = at("cbt", 48 * KB, [4, SEQ])
        diag = [at(f"diag{i}", (56 + 4 * i) * KB, [2, 4, P]) for i in range(2)]
        neg_bias = [[at(f"neg_bias{i}{d}", o, [4, P]) for d, o in enumerate(os)]
                    for i, os in enumerate(((CONST + 7 * KB, CONST + 9 * KB), (CONST + 13 * KB, DYN + 70 * KB)))]
        decay_all = [at(f"decay{i}", (64 + 8 * i) * KB, [4 * (SEQ + P)]) for i in range(2)]
        decay = [d[:, 0:4 * SEQ].rearrange("p (i t) -> p i t", t=SEQ) for d in decay_all]
        decay_d = [d[:, :].rearrange("p (i t) -> p i t", t=SEQ + P)[:, :, 0:P] for d in decay_all]
        c_dec = [at(f"c_dec{i}", DYN + (76 - 4 * i) * KB, [2, SEQ]) for i in range(2)]
        mix_hi2 = at("mix_hi2", DYN, [MIX_T - KT, SEQ], F32R)
        mix_lo2 = at("mix_lo2", DYN + 16 * KB, [MIX_T - KT, SEQ], F32R)
        par1 = at("par1", SM, [P1_COLS])
        mod = at("mod", SM + 1216, [ADA_T, 2])
        in_scale = at("in_scale", SM + 1408, [KT, 2])
        bias_tok = at("bias_tok", SM + 1472, [4, DT_ROWS])
        ctx_w_tok = at("ctx_w_tok", SM + 2240, [2, DT_ROWS])
        dt_small = at("dt_small", SM + 2624, [8])
        mod_rows = at("mod_rows", DYN + 25 * KB, [D * 3])
        c_silu = at("c_silu", DYN + 24 * KB, [KT, 2])
        ple_raw = at("ple_raw", DYN + 16 * KB, [PLE_T, SEQ])
        ple_hi = at("ple_hi", DYN + 20 * KB, [PLE_T, SEQ], F32R)
        ple_lo = at("ple_lo", DYN + 24 * KB, [PLE_T, SEQ], F32R)

        ident = table[:, C_ID:C_ID + P]
        ones = table[:, C_ONE:C_ONE + P]
        blk64 = table[:, C_BLK:C_BLK + P]
        rot = table[:, C_ROT:C_ROT + P]

        banks = ctx.enter_context(nc.psum_tensor("banks", [P, 8, SEQ], F32))
        bank = [banks[:, i] for i in range(8)]
        acc = bank[:4]
        norm_bank = bank[4]
        mix_bank = bank[5:]
        rot_bank = [bank[i] for i in (2, 3, 4, 5, 7)]
        turn_bank = [norm_bank, mix_bank[2]]
        mod_bank = [bank[i] for i in (0, 1, 2, 3, 6, 7)]
        ctx_bank = [norm_bank, mix_bank[0]]

        raw_loaded = [ctx.enter_context(nc.semaphore(f"raw_loaded{i}")) for i in range(SLOTS)]
        unit_split = ctx.enter_context(nc.semaphore("unit_split"))
        ld = loads("par1", "ctx", "dft_c", "dft_t", "x_again", "table", "masks", "par2", "pos", "h", *[f"mix{i}" for i in range(DEPTH)],
                   *[f"ple{i}" for i in range(DEPTH)])
        stored = ctx.enter_context(nc.semaphore("stored"))

        block = ctx.enter_context(nc.Block())

        split_units = units - WHOLE_UNITS

        @block.sync
        def _(sp):
            for i in range(SLOTS):
                sp.dma_start(raw[:, i], a["stream"][i]).then_inc(raw_loaded[i], 16)
            product = ev.sem("product")
            with sp.Fori(1, WHOLE_UNITS // SLOTS + 1) as r:
                for i in range(SLOTS):
                    sp.wait_ge(product, r * SLOTS + (i + 1 - SLOTS))
                    sp.dma_start(raw[:, i], a["stream"][r * SLOTS + i]).then_inc(raw_loaded[i], 16)
            with sp.Fori(1, split_units // SLOTS) as r:
                for i in range(SLOTS):
                    sp.wait_ge(unit_split, r * SLOTS + (i + 1 - SLOTS))
                    sp.dma_start(raw[:, i], a["stream"][r * SLOTS + (WHOLE_UNITS + i)]).then_inc(raw_loaded[i], 16)
            for k in range(0, KT, 2):
                sp.wait_ge(*after("h_new", ("last", k + 1)))
                sp.dma_start(out[:, k:k + 2], h[:, k:k + 2]).then_inc(stored, 16)
            sp.wait_ge(stored, 16 * (KT // 2))

        @block.gpsimd
        def _(pool):
            unit_high = ev.sem("unit_high")
            before_ssd = (first_block["out1"] // UNIT - WHOLE_UNITS) // SLOTS + 1

            def low_parts(first, end):
                with pool.Fori(first, end) as r:
                    for i in range(SLOTS):
                        pool.wait_ge(unit_high, r * SLOTS + (i + 1))
                        pool.tensor_tensor(wlo[:, i], raw[:, i], whi[:, i].bitcast(F32), ALU.subtract)\
                            .then_inc(unit_split, 1)

            def biased_masks(hd):
                if hd >= 2:
                    pool.wait_ge(*after("ssd_diag", hd - 2))
                for d, neg in enumerate((C_NEGF, C_NEGB)):
                    r = d * HEADS + hd
                    ins = pool.tensor_tensor(neg_bias[hd % 2][d][:, :, :],
                                             table[:, neg:neg + P].unsqueeze(1).broadcast_to([P, 4, P]),
                                             bias_tok[:, :, r:r + 1].broadcast_to([P, 4, P]), ALU.add)
                ins.then_inc(*done("neg_bias", hd))

            low_parts(0, before_ssd)
            pool.wait_ge(*after("product", ("four", FT4 - 1)))
            pool.wait_ge(*after("cum_low", 0))
            biased_masks(0)
            biased_masks(1)
            for hd in range(HEADS):
                pool.wait_ge(*after("ssd_row_exp", hd))
                cd = c_dec[hd % 2][:, :, :]
                pool.tensor_tensor(cd, cd, c_x[:, hd // 6].unsqueeze(1).broadcast_to([P, 2, SEQ]), ALU.mult)\
                    .then_inc(*done("ssd_c", hd))
                if hd + 2 < HEADS:
                    biased_masks(hd + 2)
            low_parts(before_ssd, split_units // SLOTS)
        def mix1(t):
            return zf[:, t] if t < FT4 else zs[:, t - FT4]

        def mix1_hi(t):
            return xhi[:, t] if t < KT else mix_hi2[:, t - KT]

        def mix1_lo(t):
            return xlo[:, t] if t < KT else mix_lo2[:, t - KT]

        def units_to(q):
            layer, n = q
            return first_block[(("gu", layer, 0), ("in2", layer), ("gu", layer, 1), ("gate", layer))[n]] // UNIT

        @block.scalar
        def _(act):
            cast = [WHOLE_UNITS]

            def high_parts(upto):
                while cast[0] < min(upto, units):
                    u = cast[0]
                    act.wait_ge(raw_loaded[u % SLOTS], 16 * (u // SLOTS + 1))
                    if u >= WHOLE_UNITS + SLOTS:
                        act.wait_ge(*after("product", ("unit", u - SLOTS)))
                    act.activation(whi[:, u % SLOTS], raw[:, u % SLOTS], ACT.Copy)\
                        .then_inc(*done("unit_high", ("unit", u)))
                    cast[0] += 1

            def tile_ready(stage, m, k):
                used = (first_block[stage] + (m + 1) * k) // UNIT
                high_parts(used + SLOTS)
                act.wait_ge(*after("product", (stage, m)))

            def squares(name, q, k, src):
                dst = sq_sum[:] if k == 0 else tmp[1 + k % 2][:]
                if k >= 3:
                    act.wait_ge(*after("sq_added", (name, q, k - 2)))
                act.activation(dst, src, ACT.Square).then_inc(*done(name, (q, k)))

            def norm_in(q, gain):
                high_parts(units_to(q) + SLOTS)
                for k in range(KT):
                    act.wait_ge(*after("h_new", (q, k)))
                    act.activation(xhi[:, k], h[:, k], ACT.Copy, scale=gain[:, k:k + 1])\
                        .then_inc(*done("x_high", (q, k)))
                    squares("h_sq", q, k, h[:, k])

            def inverse_root(*sums):
                for key, n, src, dst in sums:
                    act.wait_ge(*after("summed", key))
                    act.activation(dst, src, ACT.Ln, scale=1.0 / n, bias=eps).then_inc(*done("log", key))
                for key, n, src, dst in sums:
                    act.wait_ge(*after("log", key))
                    act.activation(dst, dst, ACT.Exp, scale=-0.5).then_inc(*done("inverse", key))

            def y_out(stage, q, k, y):
                for m in range(KT):
                    tile_ready(stage, m, k)
                    t = first_tile[stage] + m
                    squares("y_sq", q, m, acc[acc_of[t]][:])
                    act.activation(y[:, m], acc[acc_of[t]][:], ACT.Copy).then_inc(*done("y_copied", (q, m), bank_of=t))
                inverse_root((("post", q), D, norm_bank[:], inv_rms[:]))

            def mix_high(layer, t, src):
                act.activation(xhi[:, t], src, ACT.Copy).then_inc(*done("mix_high", (layer, t)))

            def hgrn_gates(layer):
                act.wait_ge(*after("z", (layer, 3)))
                act.activation(gate_b[:, :, :], z[:, 2:4], ACT.Sigmoid)
                act.activation(key_k[:, :, :], z[:, 2:4], ACT.Sigmoid, scale=-1.0).then_inc(*done("hg_sig", layer))

            def hgrn_logs(layer):
                act.wait_ge(*after("hg_ln_in", layer))
                act.activation(diff[:, :, :], diff[:, :, :], ACT.Ln)
                act.activation(q_dec[:, :, :], q_dec[:, :, :], ACT.Ln).then_inc(*done("hg_ln", layer))

            def hgrn_decays(layer, n):
                b = LEVELS[n - 1]
                act.wait_ge(*after("hg_diff", (layer, n)))
                d = diff[:, :, :].rearrange("p g (r s) -> p (g r) s", s=2 * b)
                act.activation(d[:, :, b:2 * b], d[:, :, b:2 * b], ACT.Exp)
                act.activation(d[:, :, 0:b], d[:, :, 0:b], ACT.Exp, scale=-1.0)\
                    .then_inc(*done("hg_exp", (layer, n)))

            def hgrn_chunk_decays(layer):
                act.wait_ge(*after("hg_diff", (layer, "end")))
                act.activation(diff[:, :, :], diff[:, :, :], ACT.Exp)
                act.activation(e_tot[:, :, :], tot[:, :, :], ACT.Exp)
                act.activation(gate_b[:, :, :], gate_b[:, :, :], ACT.Exp).then_inc(*done("hg_exp", (layer, "end")))

            def hgrn_tokens(layer):
                for g in range(2):
                    for name, b, tok in (("hg_kt", 4 + g, k_tok), ("hg_vt", 6 + g, v_tok)):
                        act.wait_ge(*after(name, (layer, g)))
                        act.activation(tok[:, g], bank[b].rearrange("p (n f) -> p n f", f=P), ACT.Copy)\
                            .then_inc(*done(name + "ok", (layer, g)))

            def hgrn_out(layer):
                for g in range(2):
                    act.wait_ge(*after("hg_o", (layer, g)))
                    act.activation(hg_o[:, g], bank[6 + g], ACT.Copy).then_inc(*done("hg_o_copied", (layer, g)))
                    act.activation(diff[:, g], bank[6 + g], ACT.Square).then_inc(*done("hg_o_sq", (layer, g)))

            def hgrn_norm(layer):
                inverse_root(*(((layer, "hg", g), 64, bank[4 + g], k_dec[:, g]) for g in range(2)))
                act.activation(z[:, 6:8], z[:, 6:8], ACT.Sigmoid).then_inc(*done("hg_out_gate", layer))

            def hgrn_high(layer):
                for g in range(2):
                    act.wait_ge(*after("mix_out", (layer, g)))
                    mix_high(layer, g, hg_o[:, g])

            def attention(layer):
                act.wait_ge(*after("att_vt", layer))
                act.activation(va_tok[:, :, :], mix_bank[1][:].rearrange("p (n f) -> p n f", f=P), ACT.Copy)\
                    .then_inc(*done("att_vtok", layer))

                def exps(i):
                    w0 = P if i % 4 == 0 else 0
                    st, sc = stat[i % 3], scores[i % 3]
                    act.wait_ge(*after("att_shift", (layer, i)))
                    for e in range(2):
                        act.activation(sc[:, e, w0:], sc[:, e, w0:], ACT.Exp, bias=st[:, 1, e:e + 1],
                                       accum_out=st[:, 3, e:e + 1])
                    act.activation(st[:, 4], st[:, 2], ACT.Exp).then_inc(*done("att_exp", (layer, i)))

                def turned(i):
                    k0 = 1 if i % 4 == 0 else 0
                    act.wait_ge(*after("att_turned", (layer, i)))
                    act.activation(probs_t[i % 2][:, :, k0:], turn_bank[i % 2][:].rearrange(
                        "p (e k f) -> p e k f", e=2, f=P)[:, :, k0:], ACT.Copy).then_inc(*done("att_pt", (layer, i)))

                def heads_out(t):
                    act.wait_ge(*after("att_o", (layer, t)))
                    mix_high(layer, 4 + t, mix_bank[t % 2][:])

                for i in range(16 + 2):
                    if i < 16:
                        exps(i)
                    if 1 <= i <= 16:
                        turned(i - 1)
                    if i >= 5 and (i - 5) % 4 == 0:
                        heads_out((i - 5) // 4)

            def gating_gelu(layer):
                act.wait_ge(*after("z", (layer, 11)))
                act.activation(z[:, 8:12], z[:, 8:12], ACT.Gelu_apprx_tanh).then_inc(*done("gelu", layer))

            def gating_squares(layer):
                act.wait_ge(*after("ln_x", layer))
                act.activation(ln_sq[:, :, :], z[:, 10:12], ACT.Square).then_inc(*done("ln_sq", layer))

            def gating_tokens(layer):
                for g in range(2):
                    act.wait_ge(*after("sg_vt", (layer, g)))
                    act.activation(sg_tok[:, :, g * P:(g + 1) * P], acc[2 + g][:].rearrange("p (n f) -> p n f", f=P),
                                   ACT.Copy).then_inc(*done("sg_tok", (layer, g)))

            def gating_high(layer):
                for g in range(2):
                    act.wait_ge(*after("mix_out", (layer, 2 + g)))
                    mix_high(layer, 2 + g, z[:, 8 + g])

            def first_block_act():
                act.dma_start(par1[:, :], a["par1"]).then_inc(ld["par1"], 16)
                load_tables()
                act.dma_start(h[:, :, :], a["x"].rearrange("p (k t) -> p k t", t=SEQ)).then_inc(ld["h"], 16)
                act.dma_start(ctx_raw[:, :, :], a["ctx"].rearrange("p (k t) -> p k t", t=CTX)).then_inc(ld["ctx"], 16)
                act.dma_start(dft_c[:, :], a["dft_c"]).then_inc(ld["dft_c"], 16)
                act.wait_ge(ld["par1"], 16)
                act.activation(c_silu[:, :, :], par1[:, P1_C:P1_C + 2 * KT].rearrange("p (k c) -> p k c", c=2), ACT.Silu)\
                    .then_inc(*done("c_silu", 0))
                act.wait_ge(ld["h"], 16)
                act.activation(x_sq[:, :, :], h[:, :, :], ACT.Square).then_inc(*done("x_sq", "x"))
                act.wait_ge(ld["ctx"], 16)
                act.activation(ctx_sq[:, :, :], ctx_raw[:, :, :], ACT.Square).then_inc(*done("x_sq", "ctx"))
                lower_bounds()
                for n in range(ADA_T // 4):
                    act.wait_ge(*after("product", ("ada", n)))
                    act.activation(mod_rows[0:2, n * SEQ:(n + 1) * SEQ], mod_bank[n][0:2, :], ACT.Copy)\
                        .then_inc(*done("mod_rows", n))
                act.wait_ge(*after("eps", 0))
                inverse_root(("x", D, norm_bank[:], inv_rms[:]), ("ctx", D, mix_bank[0][:, 0:CTX], sq_sum[:, 0:CTX]))
                high_parts(WHOLE_UNITS + SLOTS)
                for k in range(KT):
                    act.wait_ge(*after("in_scaled", (k, 0)))
                    act.activation(xhi[:, k], x_scaled[:, k], ACT.Identity, bias=mod[:, k, 0:1])\
                        .then_inc(*done("in_high", (k, 0)))
                    act.wait_ge(*after("in_scaled", (k, 1)))
                    act.activation(ctx_hi[:, k], ctx_scaled[:, k], ACT.Identity, bias=mod[:, k, 1:2])\
                        .then_inc(*done("in_high", (k, 1)))
                for m in range(IN1A_T):
                    tile_ready("in1a", m, KT)
                    t = first_tile["in1a"] + m
                    if m == DT0:
                        act.activation(dt_raw[:, 0:SEQ], acc[acc_of[t]][:], ACT.Identity, bias=par1[:, P1_DTB:P1_DTB + 1])\
                            .then_inc(*done("dt_raw", 0, bank_of=t))
                        act.activation(dt_raw[:, SEQ:], ctx_bank[0][:, 0:CTX], ACT.Identity,
                                       bias=par1[:, P1_DTB:P1_DTB + 1]).then_inc(*done("dt_raw", 1))
                    elif U0 <= m < ZF0:
                        act.activation(u_in[:, m - U0], acc[acc_of[t]][:], ACT.Copy).then_inc(*done("u", m - U0, bank_of=t))
                    elif m >= ZF0:
                        if m == ZF0:
                            act.wait_ge(*after("conv_turned", C0 - 1))
                        act.activation(zf[:, m - ZF0], acc[acc_of[t]][:], ACT.Silu).then_inc(*done("zf", m - ZF0, bank_of=t))
                    if B0 + 1 <= m <= U0:
                        conv_out(m - 1)
                    if B0 + 2 <= m:
                        conv_tokens(m - 2)
                    if m == U0 + 1:
                        step_sizes_start()
                step_sizes()
                for d in range(2):
                    for g in range(GROUPS):
                        act.wait_ge(*after("state", (d, g)))
                        if d == 1 and g == 0:
                            act.wait_ge(*after("ctx_weighted", 1))
                        act.activation(h0[d][:, g * 384:(g + 1) * 384], bank[4 + g][:, 0:384], ACT.Copy)\
                            .then_inc(*done("h0", (d, g)))
                for m in range(ST):
                    tile_ready("in1b", m, KT)
                    t = first_tile["in1b"] + m
                    act.activation(zs[:, m], acc[acc_of[t]][:], ACT.Silu).then_inc(*done("zs", m, bank_of=t))
                act.dma_start(dft_t[:, :, :, :], a["dft_t"].rearrange("p (a i t) -> p a i t", a=2, i=4))\
                    .then_inc(ld["dft_t"], 16)
                for i in range(4):
                    act.wait_ge(*after("four_tok", i))
                    b = 4 + 2 * (i % 2)
                    act.activation(four_tok[:, i].rearrange("p (a j) c f -> p a (j c f)", a=2), banks[:, b:b + 2, :], ACT.Copy)\
                        .then_inc(*done("four_tok_out", i))
                for j in range(FT4):
                    act.wait_ge(*after("four", 3))
                    act.activation(four_hi[:, j], bank[4 + j], ACT.Copy).then_inc(*done("four_high", j))
                for m in range(FT4):
                    tile_ready("four", m, FT4)
                act.activation(cum_hi[:], cum[:, 0:SEQ], ACT.Copy)
                act.activation(ident_r[:], ident, ACT.Copy).then_inc(*done("cum_high", 0))
                for g in range(GROUPS):
                    for hd in range(6 * g, 6 * g + 6):
                        head(hd)
                        if hd % 6 == 0:
                            for i in range(4):
                                if g and i == 0:
                                    act.wait_ge(*after("ssd_cb", (hd - 1, 1)))
                                act.wait_ge(*after("cb", (g, i)))
                                act.activation(cbt[:, i], bank[6 + i % 2], ACT.Copy).then_inc(*done("cbt", (g, i)))
                        if hd % 6 == 2 and g:
                            group_squares(g - 1)
                        if hd % 6 == 4 and g:
                            inverse_root((("ssd", g - 1), 3 * P, bank[6], inv_rms[:]))
                group_squares(GROUPS - 1)
                for t in range(MIX_T):
                    act.wait_ge(*(after("mix1", t) if t >= MIX_T - 3 else after("ssd_y", HEADS - 1)))
                    if t == 5:
                        inverse_root((("ssd", GROUPS - 1), 3 * P, bank[6], inv_rms[:]))
                    act.activation(mix1_hi(t), mix1(t), ACT.Copy).then_inc(*done("mix1_high", t))
                act.dma_start(h[:, :, :], a["x"].rearrange("p (k t) -> p k t", t=SEQ)).then_inc(ld["x_again"], 16)
                act.dma_start(tmp[0][:].bitcast(I32), a["positions"].broadcast_to([P, SEQ])).then_inc(ld["pos"], 16)
                for m in range(KT):
                    tile_ready("out1", m, MIX_T)
                    if m == 0:
                        turn_angles()
                    act.wait_ge(*after("residual", m))
                    squares("res_sq", "first", m, h[:, m])
                inverse_root(("first", D, norm_bank[:], inv_rms[:]))

            def conv_out(m):
                n = m - B0 if m < XS0 else m - XS0 if m < C0 else m - C0
                buf, b = conv[m % 2], par1[:, P1_CB + m - B0:P1_CB + m - B0 + 1]
                act.wait_ge(*after("conv", m))
                if m >= C0:
                    act.activation(c_x[:, n], buf[:, 0:SEQ], ACT.Silu, bias=b).then_inc(*done("conv_out", m))
                elif m < XS0:
                    act.activation(b_x[:, n], buf[:, 0:SEQ], ACT.Silu, bias=b)
                    act.activation(buf[:, SEQ:], buf[:, SEQ:], ACT.Silu, bias=b).then_inc(*done("conv_out", m))
                else:
                    act.activation(buf[:, :], buf[:, :], ACT.Silu, bias=b).then_inc(*done("conv_out", m))

            def conv_tokens(m):
                if not B0 <= m < C0:
                    return
                act.wait_ge(*after("conv_turned", m))
                if m >= XS0:
                    n = m - XS0
                    act.activation(x_tok[:, :, n * P:(n + 1) * P], mix_bank[1][:].rearrange("p (i f) -> p i f", f=P), ACT.Copy)
                    dst = ctx_tok[:, :, n * P:(n + 1) * P]
                else:
                    dst = ctx_b_tok[:, :, (m - B0) * P:(m - B0 + 1) * P]
                act.activation(dst, mix_bank[2][:, 0:CTX].rearrange("p (i f) -> p i f", f=P), ACT.Copy)\
                    .then_inc(*done("conv_tok", m))

            def step_sizes_start():
                act.wait_ge(*after("dt_raw", 1))
                act.activation(dt[1][:, :], dt_raw[:, :], ACT.Abs).then_inc(*done("dt_act", "abs"))
                act.wait_ge(*after("dt_act", "abs"))
                act.activation(dt_small[:, 0:1], par1[:, P1_DTB + 1:P1_DTB + 2], ACT.Exp)
                act.activation(dt[1][:, :], dt[1][:, :], ACT.Exp, scale=-1.0).then_inc(*done("dt_act", "exp"))

            def step_sizes():
                act.wait_ge(*after("dt_cum", 0))
                act.activation(dt[2][:, SEQ:], cum[:, SEQ:], ACT.Exp, scale=-1.0, bias=dt_small[:, 2:3])\
                    .then_inc(*done("dt_act", "end"))
                act.activation(dt[3][:, 0:SEQ], dt[1][:, 0:SEQ], ACT.Ln).then_inc(*done("dt_act", "ln"))
                act.wait_ge(*after("dt_turned", 0))
                act.activation(bias_tok[:, :, :], bank[4].rearrange("p (i r) -> p i r", r=P)[:, :, 0:DT_ROWS], ACT.Copy)
                act.activation(ctx_w_tok[:, :, :], bank[5][:, 0:CTX].rearrange("p (i r) -> p i r", r=P)[:, :, 0:DT_ROWS], ACT.Copy)\
                    .then_inc(*done("dt_tok", 0))

            def head(hd):
                rf, rb = bank[2 * (hd % 2)], bank[2 * (hd % 2) + 1]
                e, dg = decay[hd % 2], diag[hd % 2]
                act.wait_ge(*after("ssd_diag", hd))
                for half in range(2):
                    if hd >= 2:
                        act.wait_ge(*after("ssd_y_inner", (hd - 2, half)))
                    act.activation(dg[:, :, 2 * half:2 * half + 2], dg[:, :, 2 * half:2 * half + 2], ACT.Exp)
                    for i in (2 * half, 2 * half + 1):
                        bf, bb = bias_tok[:, i, hd:hd + 1], bias_tok[:, i, HEADS + hd:HEADS + hd + 1]
                        if i < 3:
                            ins = act.activation(e[:, i, (i + 1) * P:], rf[:, (i + 1) * P:], ACT.Exp, bias=bf)
                        if i:
                            ins = act.activation(e[:, i, 0:i * P], rb[:, 0:i * P], ACT.Exp, bias=bb)
                    ins.then_inc(*done("ssd_exp", (hd, half)))
                if hd >= 2:
                    act.wait_ge(*after("ssd_y", hd - 2))
                act.activation(c_dec[hd % 2][:, :, :], banks[:, 2 * (hd % 2):2 * (hd % 2) + 2], ACT.Exp)\
                    .then_inc(*done("ssd_row_exp", hd))

            def group_squares(g):
                for t in range(3):
                    act.wait_ge(*after("ssd_gated", 3 * g + t))
                    act.activation(tmp[t][:], zs[:, 3 * g + t], ACT.Square).then_inc(*done("ssd_sq", (g, t)))
            eps = small[:, 0:1]

            def load_tables():
                act.dma_start(table[:, :], a["table"]).then_inc(ld["table"], 16)
                act.dma_start(masks_f[:, :, :], a["masks"].rearrange("p (l f) -> p l f", f=P)).then_inc(ld["masks"], 16)
                act.dma_start(par2[:, :, :], a["par2"].rearrange("l p c -> p l c")).then_inc(ld["par2"], 16)

            def lower_bounds():
                act.wait_ge(*after("prepared", "logits"))
                act.activation(small[:, 8:12], small[:, 8:12], ACT.Exp).then_inc(*done("prepared_act", "logits"))

            def turn_angles():
                act.wait_ge(*after("prepared", "angles"))
                act.activation(cos_t[:], cos_t[:], ACT.Sin)
                act.activation(sin_t[:], sin_t[:], ACT.Sin).then_inc(*done("prepared_act", "angles"))

            first_block_act()

            for layer in range(DEPTH):
                for s in range(4):
                    q = (layer, s)
                    if s == 3:
                        act.dma_start(ple_raw[:, :, :], a["ple"][layer].rearrange("p (k t) -> p k t", t=SEQ))\
                            .then_inc(ld[f"ple{layer}"], 16)
                    norm_in(q, par2[:, layer, P2_NORM + 16 * s:P2_NORM + 16 * s + KT])
                    high_parts(units_to(q) + SLOTS + 1)
                    inverse_root((("pre", q), D, norm_bank[:], inv_rms[:]))
                    if s in (0, 2):
                        gu = ("gu", layer, s // 2)
                        for j in range(FT):
                            tile_ready(gu, 2 * j + 1, KT)
                            act.wait_ge(*after("gate_scaled", (q, j)))
                            act.activation(tmp[0][:], tmp[0][:], ACT.Silu).then_inc(*done("silu", (q, j)))
                            act.wait_ge(*after("act_formed", (q, j)))
                            act.activation(act_hi[:, j], tmp[1][:], ACT.Copy).then_inc(*done("act_high", (q, j)))
                        y_out(("down", layer, s // 2), q, FT, y_over_x)
                    elif s == 1:
                        act.dma_start(mixpar[:, :], a["mixpar"][layer]).then_inc(ld[f"mix{layer}"], 16)
                        def projected(m):
                            tile_ready(("in2", layer), m, KT)

                        for m in range(4):
                            projected(m)
                        hgrn_gates(layer)
                        projected(4)
                        hgrn_logs(layer)
                        for n in range(1, len(LEVELS) + 1):
                            hgrn_decays(layer, n)
                            projected(4 + n)
                        hgrn_chunk_decays(layer)
                        gating_gelu(layer)
                        projected(12)
                        gating_squares(layer)
                        projected(13)
                        hgrn_tokens(layer)
                        inverse_root(((layer, "ln"), 2 * P, acc[3][:], tmp[2][:]))
                        projected(14)
                        projected(15)
                        hgrn_out(layer)
                        gating_tokens(layer)
                        projected(16)
                        hgrn_norm(layer)
                        projected(17)
                        gating_high(layer)
                        hgrn_high(layer)
                        attention(layer)
                        y_out(("out2", layer), q, KT, y_dyn)
                    else:
                        for m in range(KT):
                            tile_ready(("gate", layer), m, KT)
                            if m == 3:
                                act.wait_ge(ld[f"ple{layer}"], 16)
                                act.activation(ple_hi[:, :, :], ple_raw[:, :, :], ACT.Copy)\
                                    .then_inc(*done("ple_high", layer))
                            act.wait_ge(*after("gate2_scaled", (layer, m)))
                            act.activation(y_dyn[:, m], tmp[m % 2][:], ACT.Sigmoid)\
                                .then_inc(*done("gate2", (layer, m)))
                        for m in range(KT):
                            tile_ready(("proj", layer), m, PLE_T)
                            act.wait_ge(*after("y_formed", (q, m)))
                            squares("y_sq", q, m, y_dyn[:, m])
                        inverse_root((("post", q), D, norm_bank[:], inv_rms[:]))
            high_parts(units)

        @block.vector
        def _(v):
            def sq_add(name, q, k):
                v.wait_ge(*after(name, (q, k)))
                if 0 < k < KT - 1:
                    if k > 1:
                        v.wait_ge(*after("sq_added", (name, q, k - 1)))
                    v.tensor_tensor(sq_sum[:], sq_sum[:], tmp[1 + k % 2][:], ALU.add)\
                        .then_inc(*done("sq_added", (name, q, k)))

            def boundary(q_post, y, q_pre, gain_post, gain_pre):
                post = q_post if q_post == "first" else ("post", q_post)
                for k in range(KT + 1):
                    if k == 0:
                        v.wait_ge(*after("inverse", post))
                        if q_post != "first" and q_post[1] != 3:
                            v.wait_ge(*after("y_copied", (q_post, KT - 1)))
                    if k < KT and q_post == "first":
                        v.scalar_tensor_tensor(h[:, k], h[:, k], gain_post[:, k:k + 1], inv_rms[:],
                                               ALU.mult, ALU.mult).then_inc(*done("h_new", (q_pre, k)))
                    elif k < KT:
                        if k:
                            v.wait_ge(*after("h_new", (q_pre, k - 1)))
                        v.scalar_tensor_tensor(tmp[0][:], y[:, k], gain_post[:, k:k + 1], inv_rms[:],
                                               ALU.mult, ALU.mult).then_inc(*done("y_normed", (q_post, k)))
                        v.wait_ge(*after("y_normed", (q_post, k)))
                        v.tensor_tensor(h[:, k], h[:, k], tmp[0][:], ALU.add)\
                            .then_inc(*done("h_new", (q_pre, k)))
                    if k and q_pre != "last":
                        v.wait_ge(*after("x_high", (q_pre, k - 1)))
                        v.scalar_tensor_tensor(xlo[:, k - 1], h[:, k - 1], gain_pre[:, k - 1:k],
                                               xhi[:, k - 1].bitcast(F32), ALU.mult, ALU.subtract)\
                            .then_inc(*done("x_low", (q_pre, k - 1)))
                        sq_add("h_sq", q_pre, k - 1)

            def mix_low(layer, t, src):
                v.wait_ge(*after("mix_high", (layer, t)))
                v.tensor_tensor(xlo[:, t], src, xhi[:, t].bitcast(F32), ALU.subtract)\
                    .then_inc(*done("mix_low", (layer, t)))

            def hgrn_clear(layer):
                v.memset(hg_att[:, :, :], 0.0)
                v.memset(k_dec[:, :, :], 0.0)
                v.memset(state[:, :, :, :], 0.0).then_inc(*done("hg_cleared", layer))

            def hgrn_gates(layer):
                v.wait_ge(*after("hg_sig", layer))
                for g in range(2):
                    floor, rest = lower[:, layer, g, 0:1], lower[:, layer, g, 1:2]
                    v.tensor_scalar(key_k[:, g], key_k[:, g], rest, None, ALU.mult)
                    v.tensor_scalar(gate_b[:, g], gate_b[:, g], rest, floor, ALU.mult, ALU.add)\
                        .then_inc(*done("hg_gate", (layer, g)))
                v.wait_ge(*after("hg_gate", (layer, 1)))
                v.tensor_scalar(diff[:, :, :], gate_b[:, :, :], 2.0 ** -60, None, ALU.max)
                v.tensor_scalar(q_dec[:, :, :], gate_b[:, :, :], 2.0 ** 60, 1.0, ALU.mult, ALU.min)\
                    .then_inc(*done("hg_ln_in", layer))

            def hgrn_cumulate(layer):
                v.wait_ge(*after("hg_ln", layer))
                v.tensor_tensor(diff[:, :, :], diff[:, :, :], q_dec[:, :, :], ALU.add)\
                    .then_inc(*done("hg_log", layer))
                v.wait_ge(*after("hg_log", layer))
                for g in range(2):
                    for n in range(4):
                        c = slice(n * P, (n + 1) * P)
                        v.tensor_tensor_scan(gate_b[:, g, c], diff[:, g, c], diff[:, g, c], 0.0,
                                             ALU.add, ALU.bypass).then_inc(*done("hg_cum", (layer, g, n)))
                v.wait_ge(*after("hg_cum", (layer, 1, 3)))
                b4 = gate_b[:, :, :].rearrange("p g (n f) -> p g n f", f=P)
                v.tensor_copy(tot[:, :, :], b4[:, :, :, P - 1]).then_inc(*done("hg_tot", layer))
                hgrn_diffs(layer, 1)

            def hgrn_diffs(layer, n):
                b = LEVELS[n - 1]
                src = gate_b[:, :, :].rearrange("p g (r s) -> p (g r) s", s=2 * b)
                dst = diff[:, :, :].rearrange("p g (r s) -> p (g r) s", s=2 * b)
                v.tensor_tensor(dst, src, src[:, :, b - 1:b].broadcast_to([P, SEQ // b, 2 * b]), ALU.subtract)\
                    .then_inc(*done("hg_diff", (layer, n)))

            def hgrn_masked(layer, n):
                v.wait_ge(*after("hg_scores", (layer, n)))
                if n:
                    v.wait_ge(*after("hg_masked", (layer, n - 1, 3)))
                else:
                    v.wait_ge(*after("hg_cleared", layer))
                m = masks[:, n].unsqueeze(1).broadcast_to([P, 4, P])
                for e in range(4):
                    v.copy_predicated(hg_att[:, e].rearrange("p (n f) -> p n f", f=P), m,
                                      bank[4 + e].rearrange("p (n f) -> p n f", f=P))\
                        .then_inc(*done("hg_masked", (layer, n, e)))

            def hgrn_level(layer, n):
                b = LEVELS[n - 1]
                if n == 1:
                    v.wait_ge(*after("hg_cleared", layer))
                v.wait_ge(*after("hg_exp", (layer, n)))
                v.wait_ge(*after("hg_scores", (layer, n - 1)))

                def halves(x):
                    return x.rearrange("p g (r s) -> p (g r) s", s=2 * b)

                d, qs, ks = halves(diff[:, :, :]), halves(z[:, 0:2]), halves(key_k[:, :, :])
                qd, kd = halves(q_dec[:, :, :]), halves(k_dec[:, :, :])
                v.tensor_tensor(qd[:, :, b:], qs[:, :, b:], d[:, :, b:], ALU.mult)
                v.tensor_tensor(kd[:, :, 0:b], ks[:, :, 0:b], d[:, :, 0:b], ALU.mult)\
                    .then_inc(*done("hg_dec", (layer, n)))
                v.wait_ge(*after("hg_dec", (layer, n)))
                if n < len(LEVELS):
                    hgrn_diffs(layer, n + 1)
                else:
                    v.tensor_tensor(diff[:, :, :].rearrange("p g (n f) -> p (g n) f", f=P),
                                    tot[:, :, :].rearrange("p g n -> p (g n)").unsqueeze(2).broadcast_to([P, 8, P]),
                                    gate_b[:, :, :].rearrange("p g (n f) -> p (g n) f", f=P), ALU.subtract)\
                        .then_inc(*done("hg_diff", (layer, "end")))
                hgrn_masked(layer, n - 1)

            def hgrn_chunk(layer):
                v.wait_ge(*after("hg_exp", (layer, "end")))
                v.wait_ge(*after("hg_scores", (layer, len(LEVELS))))
                v.tensor_tensor(k_dec[:, :, :], key_k[:, :, :], diff[:, :, :], ALU.mult)
                v.tensor_tensor(q_dec[:, :, :], z[:, 0:2], gate_b[:, :, :], ALU.mult)\
                    .then_inc(*done("hg_dec", (layer, "end")))
                hgrn_masked(layer, len(LEVELS))

            def hgrn_states(layer):
                for g in range(2):
                    v.wait_ge(*after("hg_kv", (layer, g)))
                    for n in range(3):
                        for e in range(2):
                            s = slice(64 * e, 64 * e + 64)
                            kv = bank[4 + g][s, n * P + 64 * e:n * P + 64 * e + 64]
                            if n == 0:
                                v.tensor_copy(state[s, 0, g, s], kv).then_inc(*done("hg_state", (layer, g, n, e)))
                            else:
                                v.wait_ge(*after("hg_state", (layer, g, n - 1, e)))
                                v.scalar_tensor_tensor(state[s, n, g, s], state[s, n - 1, g, s],
                                                       e_tot[s, g, n:n + 1], kv, ALU.mult, ALU.add)\
                                    .then_inc(*done("hg_state", (layer, g, n, e)))

            def hgrn_out(layer):
                for g in range(2):
                    v.wait_ge(*after("inverse", (layer, "hg", g)))
                    v.wait_ge(*after("hg_o_copied", (layer, g)))
                    v.tensor_tensor(hg_o[:, g], hg_o[:, g], k_dec[:, g], ALU.mult)\
                        .then_inc(*done("hg_normed", (layer, g)))
                    if g == 0:
                        v.wait_ge(*after("hg_out_gate", layer))
                    v.wait_ge(*after("hg_normed", (layer, g)))
                    v.scalar_tensor_tensor(hg_o[:, g], hg_o[:, g], par2[:, layer, P2_HG:P2_HG + 1], z[:, 6 + g],
                                           ALU.mult, ALU.mult).then_inc(*done("mix_out", (layer, g)))

            def attention(layer):
                def rotate(i):
                    zi = z[:, 12 if i == 0 else 13 + i]
                    v.wait_ge(*after("att_rot", (layer, i)))
                    if i:
                        v.wait_ge(*after("att_roped", (layer, i - 1)))
                    v.tensor_tensor(tmp[0][:], zi, cos_t[:], ALU.mult)
                    v.tensor_tensor(tmp[1][:], rot_bank[i], sin_t[:], ALU.mult)\
                        .then_inc(*done("att_rot_terms", (layer, i)))
                    v.wait_ge(*after("att_rot_terms", (layer, i)))
                    v.tensor_tensor(zi, tmp[0][:], tmp[1][:], ALU.add).then_inc(*done("att_roped", (layer, i)))

                def shifts(i):
                    t, w0 = i // 4, P if i % 4 == 0 else 0
                    st, sc = stat[i % 3], scores[i % 3]
                    sink = par2[:, layer, P2_SINK + 2 * t:P2_SINK + 2 * t + 2]
                    v.wait_ge(*after("att_scores", (layer, i)))
                    if i >= 3:
                        v.wait_ge(*after("att_turned", (layer, i - 3)))
                    mask = table[:, C_AMASK + w0:C_AMASK + 2 * P].unsqueeze(1).broadcast_to([P, 2, 2 * P - w0])
                    v.scalar_tensor_tensor(sc[:, :, w0:], banks[:, 2 * (i % 2):2 * (i % 2) + 2, w0:2 * P],
                                           SCALE, mask, ALU.mult, ALU.add).then_inc(*done("att_masked", (layer, i)))
                    v.wait_ge(*after("att_masked", (layer, i)))
                    v.tensor_reduce(st[:, 0], sc[:, :, w0:], AX.X, ALU.max).then_inc(*done("att_max", (layer, i)))
                    v.wait_ge(*after("att_max", (layer, i)))
                    v.tensor_tensor(st[:, 0], st[:, 0], sink, ALU.max).then_inc(*done("att_max2", (layer, i)))
                    v.wait_ge(*after("att_max2", (layer, i)))
                    v.tensor_scalar(st[:, 1], st[:, 0], -1.0, None, ALU.mult)
                    v.tensor_tensor(st[:, 2], sink, st[:, 0], ALU.subtract).then_inc(*done("att_shift", (layer, i)))

                def probabilities(i):
                    w0 = P if i % 4 == 0 else 0
                    st, sc = stat[i % 3], scores[i % 3]
                    v.wait_ge(*after("att_exp", (layer, i)))
                    v.tensor_tensor(st[:, 5], st[:, 3], st[:, 4], ALU.add).then_inc(*done("att_den", (layer, i)))
                    v.wait_ge(*after("att_den", (layer, i)))
                    v.reciprocal(st[:, 6], st[:, 5]).then_inc(*done("att_rden", (layer, i)))
                    v.wait_ge(*after("att_rden", (layer, i)))
                    v.tensor_tensor(sc[:, :, w0:], sc[:, :, w0:], st[:, 6].unsqueeze(2).broadcast_to([P, 2, 2 * P - w0]),
                                    ALU.mult).then_inc(*done("att_probs", (layer, i)))

                rotate(0)
                rotate(1)
                for i in range(16 + 3):
                    if i < 16:
                        shifts(i)
                    if i < 3:
                        rotate(2 + i)
                    if 1 <= i <= 16:
                        probabilities(i - 1)
                    if 3 <= i < 7:
                        mix_low(layer, i - 3, hg_o[:, i - 3] if i < 5 else z[:, 8 + i - 5])
                    if i >= 6 and (i - 6) % 4 == 0:
                        mix_low(layer, 4 + (i - 6) // 4, mix_bank[(i - 6) // 4 % 2][:])

            def gating_center(layer):
                v.wait_ge(*after("ln_mean", layer))
                v.scalar_tensor_tensor(z[:, 10:12], acc[2][:].unsqueeze(1).broadcast_to([P, 2, SEQ]), -1.0 / (2 * P),
                                       z[:, 10:12], ALU.mult, ALU.add).then_inc(*done("ln_x", layer))

            def gating_scale(layer):
                v.wait_ge(ld[f"mix{layer}"], 16)
                tri = table[:, C_TRI:C_TRI + P].unsqueeze(1).broadcast_to([P, 4, P])
                v.tensor_tensor(sg_w[:, :, :], mixpar[:, M2_SGW:M2_COLS].rearrange("p (g t) -> p g t", t=P), tri,
                                ALU.mult).then_inc(*done("sg_w", layer))
                v.wait_ge(*after("inverse", (layer, "ln")))
                for g in range(2):
                    v.scalar_tensor_tensor(z[:, 10 + g], z[:, 10 + g], par2[:, layer, P2_LN + g:P2_LN + g + 1], tmp[2][:],
                                           ALU.mult, ALU.mult).then_inc(*done("ln_out", (layer, g)))

            def gating_out(layer):
                for g in range(2):
                    v.wait_ge(*after("sg_mixed", (layer, g)))
                    bias = mixpar[:, M2_SGB + g * P:M2_SGB + (g + 1) * P].unsqueeze(1).broadcast_to([P, 4, P])
                    v.tensor_tensor(z[:, 10 + g].rearrange("p (n f) -> p n f", f=P),
                                    acc[2 + g][:].rearrange("p (n f) -> p n f", f=P), bias, ALU.add)\
                        .then_inc(*done("sg_biased", (layer, g)))
                    v.wait_ge(*after("sg_biased", (layer, g)))
                    v.tensor_tensor(z[:, 8 + g], z[:, 8 + g], z[:, 10 + g], ALU.mult)\
                        .then_inc(*done("mix_out", (layer, 2 + g)))

            def prepare():
                ready = lambda key: v.wait_ge(*after("prepared", key))
                v.memset(small[:, 0:1], EPS).then_inc(*done("eps", 0))
                v.wait_ge(ld["masks"], 16)
                v.tensor_copy(masks[:, :, :], masks_f[:, :, :]).then_inc(*done("masks", 0))
                v.wait_ge(ld["par2"], 16)
                lg = par2[:, 0, P2_LB:P2_LB + 4]
                v.tensor_tensor(small[:, 4:6], lg[:, 0:2], lg[:, 2:4], ALU.max).then_inc(*done("prepared", "lmax"))
                ready("lmax")
                for l in range(DEPTH):
                    v.tensor_tensor(small[:, 8 + 2 * l:10 + 2 * l], lg[:, 2 * l:2 * l + 2], small[:, 4:6], ALU.subtract)\
                        .then_inc(*done("prepared", ("lsub", l), *(["logits"] if l else [])))
                v.wait_ge(*after("prepared_act", "logits"))
                v.tensor_tensor(small[:, 4:6], small[:, 8:10], small[:, 10:12], ALU.add).then_inc(*done("prepared", "lsum"))
                ready("lsum")
                v.reciprocal(small[:, 6:8], small[:, 4:6]).then_inc(*done("prepared", "linv"))
                ready("linv")
                v.tensor_tensor(small[:, 8:12].rearrange("p (l g) -> p l g", l=2), small[:, 8:12].rearrange("p (l g) -> p l g", l=2),
                                small[:, 6:8].unsqueeze(1).broadcast_to([P, 2, 2]), ALU.mult).then_inc(*done("prepared", "probs"))
                ready("probs")
                v.tensor_tensor(small[:, 12:14], small[:, 8:10], small[:, 8:10], ALU.subtract)
                v.tensor_tensor(small[:, 16:18], small[:, 8:10], small[:, 10:12], ALU.add).then_inc(*done("prepared", "psum"))
                ready("psum")
                v.tensor_tensor(small[:, 14:16], small[:, 16:18], small[:, 8:10], ALU.subtract).then_inc(*done("prepared", "lb"))
                ready("lb")
                bounds = small[:, 12:16].rearrange("p (l g) -> p l g", l=2)
                v.tensor_scalar(lower[:, :, :, 0], bounds, LB_FLOOR, None, ALU.max)
                v.tensor_scalar(lower[:, :, :, 1], bounds, -1.0, 1.0, ALU.mult, ALU.add)
                for l in range(DEPTH):
                    for n in (1, 5):
                        gains = par2[:, l, P2_NORM + 8 * n:P2_NORM + 8 * n + 8]
                        v.tensor_scalar(gains, gains, 0.5, None, ALU.mult).then_inc(*done("prepared", ("half", l, n)))

            def prepare_angles():
                ready = lambda key: v.wait_ge(*after("prepared", key))
                v.wait_ge(ld["table"], 16)
                v.wait_ge(ld["pos"], 16)
                v.tensor_copy(tmp[1][:], tmp[0][:].bitcast(I32)).then_inc(*done("prepared", "pos"))
                ready("pos")
                v.tensor_scalar(tmp[2][:], tmp[1][:], table[:, C_INV:C_INV + 1], None, ALU.mult)\
                    .then_inc(*done("prepared", "angle"))
                ready("angle")
                two_pi = 2 * np.pi
                c1 = 6.28125
                c2 = float(np.float32(np.float16(two_pi - c1)))
                c3 = two_pi - c1 - c2
                for name, dst, turn in (("cos", cos_t, 0.25), ("sin", sin_t, 0.0)):
                    v.tensor_scalar(tmp[1][:], tmp[2][:], 1 / two_pi, turn, ALU.mult, ALU.add)\
                        .then_inc(*done("prepared", (name, 0)))
                    ready((name, 0))
                    v.tensor_scalar(tmp[1][:], tmp[1][:], 12582912.0, None, ALU.add).then_inc(*done("prepared", (name, 1)))
                    ready((name, 1))
                    v.tensor_scalar(tmp[1][:], tmp[1][:], -12582912.0, None, ALU.add).then_inc(*done("prepared", (name, 2)))
                    ready((name, 2))
                    src = tmp[2]
                    for n, c in enumerate((c1, c2, c3)):
                        v.scalar_tensor_tensor(dst[:], tmp[1][:], -c, src[:], ALU.mult, ALU.add)\
                            .then_inc(*done("prepared", (name, 3 + n)))
                        ready((name, 3 + n))
                        src = dst
                    v.tensor_scalar(dst[:], dst[:], turn * two_pi, 3.1415925, ALU.add, ALU.min)\
                        .then_inc(*done("prepared", (name, 6)))
                    ready((name, 6))
                    v.tensor_scalar(dst[:], dst[:], -3.1415925, None, ALU.max)\
                        .then_inc(*done("prepared", (name, 7), *(["angles"] if name == "sin" else [])))

            def first_block_dve():
                v.wait_ge(*after("mod_turned", 0))
                v.tensor_tensor(mod[:, :, :], bank[6][:, 0:2 * ADA_T].rearrange("p (m c) -> p m c", c=2),
                                par1[:, P1_ADA:P1_ADA + ADA_T].unsqueeze(2).broadcast_to([P, ADA_T, 2]), ALU.add)\
                    .then_inc(*done("mod", 0))
                v.wait_ge(*after("mod", 0))
                v.scalar_tensor_tensor(in_scale[:, :, :], mod[:, KT:2 * KT], 1.0,
                                       par1[:, P1_NORM:P1_NORM + KT].unsqueeze(2).broadcast_to([P, KT, 2]),
                                       ALU.add, ALU.mult).then_inc(*done("in_scale", 0))
                v.wait_ge(*after("in_scale", 0))
                v.wait_ge(*after("inverse", "ctx"))

                def lows(k):
                    for c, (src, hi, lo) in enumerate(((x_scaled, xhi, xlo), (ctx_scaled, ctx_hi, ctx_lo))):
                        v.wait_ge(*after("in_high", (k, c)))
                        v.scalar_tensor_tensor(lo[:, k], src[:, k], mod[:, k, c:c + 1], hi[:, k].bitcast(F32),
                                               ALU.add, ALU.subtract).then_inc(*done("in_low", (k, c)))

                for k in range(KT):
                    v.scalar_tensor_tensor(x_scaled[:, k], h[:, k], in_scale[:, k, 0:1], inv_rms[:], ALU.mult, ALU.mult)\
                        .then_inc(*done("in_scaled", (k, 0)))
                    v.scalar_tensor_tensor(ctx_scaled[:, k], ctx_raw[:, k], in_scale[:, k, 1:2], sq_sum[:, 0:CTX],
                                           ALU.mult, ALU.mult).then_inc(*done("in_scaled", (k, 1)))
                    if k:
                        lows(k - 1)
                lows(KT - 1)
                for m in range(B0, U0):
                    convolve(m)
                step_sizes()
                for d in range(2):
                    if d:
                        v.wait_ge(*after("state", (0, GROUPS - 1)))
                    for i in range(2):
                        ins = v.tensor_tensor(ctx_weighted[:, i].rearrange("p (h f) -> p h f", f=64),
                                              ctx_tok[:, i].rearrange("p (h f) -> p h f", f=64),
                                              ctx_w_tok[:, i, d * HEADS:(d + 1) * HEADS].unsqueeze(2)
                                              .broadcast_to([P, HEADS, 64]), ALU.mult)
                    ins.then_inc(*done("ctx_weighted", d))
                for j in range(FT4):
                    v.wait_ge(*after("four_high", j))
                    v.tensor_tensor(four_lo[:, j], bank[4 + j], four_hi[:, j].bitcast(F32), ALU.subtract)\
                        .then_inc(*done("four_low", j))
                for m in range(FT4):
                    t = first_tile["four"] + m
                    v.wait_ge(*after("product", ("four", m)))
                    v.scalar_tensor_tensor(zf[:, m], acc[acc_of[t]][:], par1[:, P1_BF + m:P1_BF + m + 1], zf[:, m],
                                           ALU.add, ALU.mult).then_inc(*done("mix1", m, bank_of=t))
                v.wait_ge(*after("cum_high", 0))
                v.tensor_tensor(cum_lo[:], cum[:, 0:SEQ], cum_hi[:].bitcast(F32), ALU.subtract)\
                    .then_inc(*done("cum_low", 0))
                masked_diagonals(0)
                masked_diagonals(1)
                for hd in range(HEADS):
                    head(hd)
                    if hd + 2 < HEADS:
                        masked_diagonals(hd + 2)
                    if hd % 2 and hd > 1:
                        gate_tile(hd // 2 - 1)
                    if hd % 6 == 5 and hd > 6:
                        group_norm(hd // 6 - 1)
                gate_tile(ST - 1)
                for t in range(MIX_T):
                    if t == 5:
                        group_norm(GROUPS - 1)
                    v.wait_ge(*after("mix1_high", t))
                    v.tensor_tensor(mix1_lo(t), mix1(t), mix1_hi(t).bitcast(F32), ALU.subtract)\
                        .then_inc(*done("mix1_low", t))
                prepare_angles()
                v.wait_ge(*after("prepared_act", "angles"))
                v.wait_ge(ld["x_again"], 16)
                for m in range(KT):
                    t = first_tile["out1"] + m
                    v.wait_ge(*after("product", ("out1", m)))
                    v.scalar_tensor_tensor(h[:, m], acc[acc_of[t]][:], mod[:, 2 * KT + m, 0:1], h[:, m], ALU.mult, ALU.add)\
                        .then_inc(*done("residual", m, bank_of=t))
                    if m:
                        sq_add("res_sq", "first", m - 1)
                sq_add("res_sq", "first", KT - 1)

            def convolve(m):
                t = first_tile["in1a"] + m
                w = par1[:, P1_CONV + 9 * (m - B0):P1_CONV + 9 * (m - B0) + 9]
                buf = conv[m % 2]
                v.wait_ge(*after("product", ("in1a", m)))
                if m >= B0 + 2:
                    v.wait_ge(*after("conv_out" if m - 2 >= C0 else "conv_turned", m - 2))
                src = acc[acc_of[t]][:].rearrange("p (y x) -> p y x", x=GRID_W)
                dst = buf[:, 0:SEQ].rearrange("p (y x) -> p y x", x=GRID_W)
                v.tensor_scalar(dst, src, w[:, 4:5], None, ALU.mult).then_inc(*done("conv_tap", (m, 4)))
                last = 4
                for tap in (0, 1, 2, 3, 5, 6, 7, 8):
                    dy, dx = tap // 3 - 1, tap % 3 - 1
                    ys, xs_ = slice(max(0, -dy), ROWS - max(0, dy)), slice(max(0, -dx), GRID_W - max(0, dx))
                    yi, xi = slice(max(0, dy), ROWS - max(0, -dy)), slice(max(0, dx), GRID_W - max(0, -dx))
                    v.wait_ge(*after("conv_tap", (m, last)))
                    v.scalar_tensor_tensor(dst[:, ys, xs_], src[:, yi, xi], w[:, tap:tap + 1], dst[:, ys, xs_],
                                           ALU.mult, ALU.add)\
                        .then_inc(*(done("conv", m, bank_of=t) if tap == 8 and m >= C0 else
                                    done("conv_tap", (m, tap), bank_of=t if tap == 8 else None)))
                    last = tap
                if m < C0:
                    src, dst = ctx_bank[m % 2][:, 0:CTX], buf[:, SEQ:]
                    v.tensor_scalar(dst, src, w[:, 4:5], None, ALU.mult).then_inc(*done("conv_tap", (m, "c")))
                    v.wait_ge(*after("conv_tap", (m, "c")))
                    v.scalar_tensor_tensor(dst[:, 1:], src[:, 0:CTX - 1], w[:, 3:4], dst[:, 1:], ALU.mult, ALU.add)\
                        .then_inc(*done("conv_tap", (m, "l")))
                    v.wait_ge(*after("conv_tap", (m, "l")))
                    v.scalar_tensor_tensor(dst[:, 0:CTX - 1], src[:, 1:], w[:, 5:6], dst[:, 0:CTX - 1], ALU.mult, ALU.add)\
                        .then_inc(*done("conv", m))

            def step_sizes():
                n = [0]

                def link(ins, *keys):
                    n[0] += 1
                    ins.then_inc(*done("dt_step", n[0], *keys))
                    v.wait_ge(*after("dt_step", n[0]))

                e, q, z2 = dt[1], dt[2], dt[3]
                v.wait_ge(*after("dt_act", "exp"))
                v.tensor_scalar(dt_small[:, 1:2], dt_small[:, 0:1], -1.0, None, ALU.mult)
                link(v.tensor_scalar(q[:], e[:], 2.0, None, ALU.add))
                link(v.reciprocal(q[:], q[:]))
                link(v.tensor_tensor(e[:], e[:], q[:], ALU.mult))
                link(v.tensor_tensor(z2[:], e[:], e[:], ALU.mult))
                link(v.tensor_scalar(q[:], z2[:], 1.0 / 19, None, ALU.mult))
                for k in range(8, 0, -1):
                    link(v.scalar_tensor_tensor(q[:], q[:], 1.0 / (2 * k + 1), z2[:], ALU.add, ALU.mult))
                link(v.scalar_tensor_tensor(q[:], q[:], 1.0, e[:], ALU.add, ALU.mult))
                link(v.tensor_scalar(e[:], dt_raw[:], 0.0, None, ALU.max))
                link(v.scalar_tensor_tensor(e[:], q[:], 2.0, e[:], ALU.mult, ALU.add))
                link(v.tensor_scalar(q[:], e[:], dt_small[:, 1:2], None, ALU.mult))
                for s in (slice(0, SEQ), slice(SEQ, SEQ + CTX)):
                    link(v.tensor_tensor_scan(z2[:, s], q[:, s], q[:, s], 0.0, ALU.add, ALU.bypass))
                    link(v.tensor_tensor_scan(dt_raw[:, s][:, ::-1], q[:, s][:, ::-1], q[:, s][:, ::-1], 0.0,
                                              ALU.add, ALU.bypass))
                sel = table[:, C_SEL:C_SEL + 1]
                link(v.scalar_tensor_tensor(dt_raw[:], dt_raw[:], sel, dt_raw[:], ALU.mult, ALU.subtract))
                link(v.scalar_tensor_tensor(cum[:], z2[:], sel, dt_raw[:], ALU.mult, ALU.subtract))
                link(v.scalar_tensor_tensor(dt_small[:, 3:4], cum[:, SEQ:SEQ + 1], sel, cum[:, SEQ:SEQ + 1],
                                            ALU.mult, ALU.subtract))
                link(v.scalar_tensor_tensor(dt_small[:, 2:3], cum[:, SEQ + CTX - 1:], sel, dt_small[:, 3:4],
                                            ALU.mult, ALU.subtract))
                v.tensor_scalar(e[:, 0:SEQ], e[:, 0:SEQ], 1e-18, None, ALU.max).then_inc(*done("dt_cum", 0))
                v.wait_ge(*after("dt_act", "end"))
                v.tensor_tensor(e[:, SEQ:], e[:, SEQ:], dt[2][:, SEQ:], ALU.mult)
                v.wait_ge(*after("dt_act", "ln"))
                v.tensor_tensor(e[:, 0:SEQ], dt[3][:, 0:SEQ], cum[:, 0:SEQ], ALU.subtract).then_inc(*done("dt_bias", 0))
                v.wait_ge(*after("dt_tok", 0))

            def masked_diagonals(hd):
                v.wait_ge(*after("ssd_rows", hd))
                v.wait_ge(*after("neg_bias", hd))
                for d in range(2):
                    ins = v.tensor_tensor(diag[hd % 2][:, d], bank[2 * (hd % 2) + d].rearrange("p (i f) -> p i f", f=P),
                                          neg_bias[hd % 2][d][:, :, :], ALU.add)
                ins.then_inc(*done("ssd_diag", hd))

            def head(hd):
                e, ed, dg = decay[hd % 2], decay_d[hd % 2], diag[hd % 2]
                for half in range(2):
                    t = slice(2 * half, 2 * half + 2)
                    v.wait_ge(*after("ssd_exp", (hd, half)))
                    v.tensor_tensor(ed[:, t], dg[:, 0, t], dg[:, 1, t], ALU.add).then_inc(*done("ssd_sum", (hd, half)))
                    v.wait_ge(*after("ssd_sum", (hd, half)))
                    if hd % 6 == 0:
                        v.wait_ge(*after("cbt", (hd // 6, 2 * half + 1)))
                    v.tensor_tensor(e[:, t], e[:, t], cbt[:, t], ALU.mult).then_inc(*done("ssd_cb", (hd, half)))
                    v.wait_ge(*after("ssd_cb", (hd, half)))
                    v.scalar_tensor_tensor(ed[:, t], ident.unsqueeze(1).broadcast_to([P, 2, P]),
                                           par1[:, P1_D + hd:P1_D + hd + 1], ed[:, t], ALU.mult, ALU.add)\
                        .then_inc(*done("ssd_m", (hd, half)))

            def gate_tile(t):
                v.wait_ge(*after("ssd_y", 2 * t + 1))
                v.tensor_tensor(zs[:, t], zs[:, t], bank[4 + t % 2], ALU.mult).then_inc(*done("ssd_gated", t))

            def group_norm(g):
                v.wait_ge(*after("inverse", ("ssd", g)))
                for t in range(3 * g, 3 * g + 3):
                    v.scalar_tensor_tensor(zs[:, t], zs[:, t], par1[:, P1_SSD + t:P1_SSD + t + 1], inv_rms[:],
                                           ALU.mult, ALU.mult).then_inc(*done("mix1", FT4 + t))

            prepare()
            first_block_dve()

            def gains(layer, n):
                return par2[:, layer, P2_NORM + 8 * n:P2_NORM + 8 * n + 8]

            before = None
            for layer in range(DEPTH):
                for s in range(4):
                    q = (layer, s)
                    if before is None:
                        boundary("first", None, q, par1[:, P1_FIN:P1_FIN + KT], gains(layer, 2 * s))
                    else:
                        y = y_over_x if before[1] in (0, 2) else y_dyn
                        boundary(before, y, q, gains(before[0], 2 * before[1] + 1), gains(layer, 2 * s))
                    if s == 1:
                        hgrn_clear(layer)
                    v.wait_ge(*after("inverse", ("pre", q)))
                    if s in (0, 2):
                        gu = ("gu", layer, s // 2)
                        for j in range(FT):
                            t = first_tile[gu] + 2 * j
                            v.wait_ge(*after("product", (gu, 2 * j)))
                            v.tensor_tensor(tmp[0][:], acc[acc_of[t]][:], inv_rms[:], ALU.mult)\
                                .then_inc(*done("gate_scaled", (q, j), bank_of=t))
                            v.wait_ge(*after("product", (gu, 2 * j + 1)))
                            v.tensor_tensor(tmp[2][:], acc[acc_of[t + 1]][:], inv_rms[:], ALU.mult)\
                                .then_inc(*done("up_scaled", (q, j), bank_of=t + 1))
                            v.wait_ge(*after("up_scaled", (q, j)))
                            v.wait_ge(*after("silu", (q, j)))
                            v.tensor_tensor(tmp[1][:], tmp[0][:], tmp[2][:], ALU.mult)\
                                .then_inc(*done("act_formed", (q, j)))
                            v.wait_ge(*after("act_high", (q, j)))
                            v.tensor_tensor(act_lo[:, j], tmp[1][:], act_hi[:, j].bitcast(F32), ALU.subtract)\
                                .then_inc(*done("act_low", (q, j)))
                        for m in range(KT):
                            sq_add("y_sq", q, m)
                    elif s == 1:
                        def projected(m):
                            t = first_tile["in2", layer] + m
                            v.wait_ge(*after("product", (("in2", layer), m)))
                            v.tensor_tensor(z[:, m], acc[acc_of[t]][:], inv_rms[:], ALU.mult)\
                                .then_inc(*done("z", (layer, m), bank_of=t))

                        for m in range(4):
                            projected(m)
                        hgrn_gates(layer)
                        projected(4)
                        hgrn_cumulate(layer)
                        projected(5)
                        for n in range(1, len(LEVELS) + 1):
                            hgrn_level(layer, n)
                            projected(5 + n)
                        hgrn_chunk(layer)
                        gating_center(layer)
                        projected(13)
                        gating_scale(layer)
                        projected(14)
                        hgrn_states(layer)
                        projected(15)
                        projected(16)
                        gating_out(layer)
                        hgrn_out(layer)
                        projected(17)
                        attention(layer)
                        for m in range(KT):
                            sq_add("y_sq", q, m)
                    else:
                        for m in range(KT):
                            t = first_tile["gate", layer] + m
                            v.wait_ge(*after("product", (("gate", layer), m)))
                            if m >= 2:
                                v.wait_ge(*after("gate2", (layer, m - 2)))
                            v.tensor_tensor(tmp[m % 2][:], acc[acc_of[t]][:], inv_rms[:], ALU.mult)\
                                .then_inc(*done("gate2_scaled", (layer, m), bank_of=t))
                            if m == 4:
                                v.wait_ge(*after("ple_high", layer))
                                v.tensor_tensor(ple_lo[:, :, :], ple_raw[:, :, :], ple_hi[:, :, :].bitcast(F32),
                                                ALU.subtract).then_inc(*done("ple_low", layer))
                        for m in range(KT):
                            t = first_tile["proj", layer] + m
                            v.wait_ge(*after("product", (("proj", layer), m)))
                            v.wait_ge(*after("gate2", (layer, m)))
                            v.tensor_tensor(y_dyn[:, m], y_dyn[:, m], acc[acc_of[t]][:], ALU.mult)\
                                .then_inc(*done("y_formed", (q, m), bank_of=t))
                            if m:
                                sq_add("y_sq", q, m - 1)
                        sq_add("y_sq", q, KT - 1)
                    before = q
            boundary(before, y_dyn, "last", gains(DEPTH - 1, 7), None)

        @block.tensor
        def _(pe):
            def product(stage, tiles, k_tiles, hi, lo, source, key, after_first=None, side_by_side=False, after_tile=None):
                side = 3 if side_by_side else 1
                order = []
                for k in range(k_tiles):
                    order.append(([*range(side)], k))
                    if side_by_side and k % 2:
                        order.append(([side], k // 2))
                group_end = len(order)
                order += [([side], k) for k in range(k_tiles // 2 if side_by_side else 0, k_tiles)]
                order += [([m], k) for m in range(side + 1, tiles) for k in range(k_tiles)]
                for n, (ms, k) in enumerate(order):
                    x_h, x_l = (hi[:, k], lo[:, k]) if hi is not None else (mix1_hi(k), mix1_lo(k))
                    for m in ms:
                        t = first_tile[stage] + m
                        if k == 0 and t >= 4:
                            pe.wait_ge(*(bank_free(earlier[t]) or (ev.sem("product"), 1)))
                        b = first_block[stage] + m * k_tiles + k
                        u, i = b // UNIT, b % UNIT
                        if i == 0 or k == 0:
                            pe.wait_ge(unit_split, u + 1 - WHOLE_UNITS)
                        if m == 0:
                            pe.wait_ge(*after(source + "_high", key(k)))
                        pe.matmul(acc[acc_of[t]][:], whi[:, u % SLOTS, i], x_h, start=(k == 0), stop=False)
                        pe.matmul(acc[acc_of[t]][:], wlo[:, u % SLOTS, i], x_h, start=False, stop=False)
                    for m in ms:
                        t = first_tile[stage] + m
                        b = first_block[stage] + m * k_tiles + k
                        u, i = b // UNIT, b % UNIT
                        if m == 0:
                            pe.wait_ge(*after(source + "_low", key(k)))
                        mm = pe.matmul(acc[acc_of[t]][:], whi[:, u % SLOTS, i], x_l, start=False, stop=(k == k_tiles - 1))
                        keys = [("unit", u)] if i == UNIT - 1 else []
                        if k == k_tiles - 1:
                            keys.append((stage, m))
                        if keys:
                            mm.then_inc(*done("product", *keys))
                    if n + 1 == group_end and after_first:
                        after_first()
                    if k == k_tiles - 1 and ms[0] >= side and after_tile:
                        after_tile(ms[0])

            def sum_features(key, last, dst=None, srcs=None, lhs=None):
                srcs = srcs or [sq_sum[:]]
                pe.wait_ge(*last)
                for n, s in enumerate(srcs):
                    mm = pe.matmul(norm_bank[:] if dst is None else dst, ones if lhs is None else lhs, s,
                                   start=(n == 0), stop=(n == len(srcs) - 1))
                mm.then_inc(*done("summed", key))

            def sum_squares(key, name, q):
                pe.wait_ge(*after("sq_added", (name, q, KT - 2)))
                pe.matmul(norm_bank[:], ones, sq_sum[:], start=True, stop=False)
                pe.wait_ge(*after(name, (q, KT - 1)))
                pe.matmul(norm_bank[:], ones, tmp[1 + (KT - 1) % 2][:], start=False, stop=True)\
                    .then_inc(*done("summed", key))

            def turn(dst, src):
                for n in range(4):
                    mm = pe.transpose(dst[:, n * P:(n + 1) * P], src[:, n * P:(n + 1) * P], ident)
                return mm

            def hgrn_scores(layer, n):
                if n == 0:
                    pe.wait_ge(*after("hg_gate", (layer, 1)))
                else:
                    pe.wait_ge(*after("hg_dec", (layer, n)))
                    pe.wait_ge(*after("hg_masked", (layer, n - 1, 3)))
                qs, ks = (z[:, 0:2], key_k[:, :, :]) if n == 0 else (q_dec[:, :, :], k_dec[:, :, :])
                for e in range(4):
                    g, s = e // 2, slice(64 * (e % 2), 64 * (e % 2) + 64)
                    for c in range(4):
                        cs = slice(c * P, (c + 1) * P)
                        mm = pe.matmul(bank[4 + e][:, cs], ks[s, g, cs], qs[s, g, cs], start=True, stop=True)
                mm.then_inc(*done("hg_scores", (layer, n)))

            def hgrn_step(layer, m):
                levels = len(LEVELS) + 1
                if 5 <= m < 5 + levels:
                    hgrn_scores(layer, m - 5)
                elif m == 5 + levels:
                    pe.wait_ge(*after("hg_dec", (layer, "end")))
                    pe.wait_ge(*after("hg_masked", (layer, len(LEVELS), 3)))
                    for g in range(2):
                        turn(bank[4 + g], k_dec[:, g]).then_inc(*done("hg_kt", (layer, g)))
                        turn(bank[6 + g], z[:, 4 + g]).then_inc(*done("hg_vt", (layer, g)))
                elif m == 6 + levels:
                    for g in range(2):
                        pe.wait_ge(*after("hg_ktok", (layer, g)))
                        pe.wait_ge(*after("hg_vtok", (layer, g)))
                        for n in range(3):
                            mm = pe.matmul(bank[4 + g][:, n * P:(n + 1) * P], k_tok[:, g, n], v_tok[:, g, n],
                                           start=True, stop=True)
                        mm.then_inc(*done("hg_kv", (layer, g)))
                elif m == 7 + levels:
                    for g in range(2):
                        pe.wait_ge(*after("hg_state", (layer, g, 2, 1)))
                        for n in range(4):
                            cs = slice(n * P, (n + 1) * P)
                            if n:
                                pe.matmul(bank[6 + g][:, cs], state[:, n - 1, g], q_dec[:, g, cs], start=True,
                                          stop=False, skip_group_check=True)
                            for e in range(2):
                                s = slice(64 * e, 64 * e + 64)
                                mm = pe.matmul(bank[6 + g][s, cs], v_tok[:, g, n, s], hg_att[:, 2 * g + e, cs],
                                               start=(n == 0), stop=True, skip_group_check=True)
                        mm.then_inc(*done("hg_o", (layer, g)))
                elif m == 8 + levels:
                    for g in range(2):
                        sum_features((layer, "hg", g), after("hg_o_sq", (layer, g)), bank[4 + g], [diff[:, g]], blk64)

            def attention(layer):
                for i in range(5):
                    zi = 12 if i == 0 else 13 + i
                    pe.wait_ge(*after("z", (layer, zi)))
                    if i == 0:
                        pe.wait_ge(*after("mix_out", (layer, 3)))
                    elif i == 2:
                        pe.wait_ge(*after("inverse", (layer, "hg", 1)))
                    elif i == 4:
                        pe.wait_ge(*after("hg_o_copied", (layer, 1)))
                    pe.matmul(rot_bank[i], rot, z[:, zi], start=True, stop=True).then_inc(*done("att_rot", (layer, i)))
                turn(mix_bank[1], z[:, 13]).then_inc(*done("att_vt", layer))

                def score(i):
                    t, n = divmod(i, 4)
                    if n == 0 or i == 1:
                        pe.wait_ge(*after("att_roped", (layer, t + 1)))
                    if i >= 2:
                        pe.wait_ge(*after("att_masked", (layer, i - 2)))
                    w0 = P if n == 0 else 0
                    for e in range(2):
                        s = slice(64 * e, 64 * e + 64)
                        mm = pe.matmul(acc[2 * (i % 2) + e][:, w0:2 * P], z[s, 14 + t, n * P:(n + 1) * P],
                                       z[s, 12, (n - 1) * P + w0:(n + 1) * P], start=True, stop=True)
                    mm.then_inc(*done("att_scores", (layer, i)))

                def turn_probs(i):
                    pe.wait_ge(*after("att_probs", (layer, i)))
                    if i >= 2:
                        pe.wait_ge(*after("att_pt", (layer, i - 2)))
                    for e in range(2):
                        for k in range(1 if i % 4 == 0 else 0, 2):
                            c = (2 * e + k) * P
                            mm = pe.transpose(turn_bank[i % 2][:, c:c + P], scores[i % 3][:, e, k * P:(k + 1) * P], ident)
                    mm.then_inc(*done("att_turned", (layer, i)))

                def values(i):
                    t, n = divmod(i, 4)
                    pe.wait_ge(*after("att_pt", (layer, i)))
                    if n == 0 and t >= 2:
                        pe.wait_ge(*after("mix_low", (layer, 4 + t - 2)))
                    k0 = 1 if n == 0 else 0
                    for e in range(2):
                        s = slice(64 * e, 64 * e + 64)
                        for k in range(k0, 2):
                            mm = pe.matmul(mix_bank[t % 2][s, n * P:(n + 1) * P], va_tok[:, n - 1 + k, s],
                                           probs_t[i % 2][:, e, k], start=(k == k0), stop=(k == 1))
                    mm.then_inc(*done("att_o", (layer, "part", i), *([(layer, t)] if n == 3 else [])))

                pe.wait_ge(*after("att_vtok", layer))
                score(0)
                score(1)
                for i in range(16 + 1):
                    if i + 2 < 16:
                        score(i + 2)
                    if i < 16:
                        turn_probs(i)
                    if i:
                        values(i - 1)

            def gating_step(layer, m):
                if m == 12:
                    pe.wait_ge(*after("gelu", layer))
                    for g in range(2):
                        mm = pe.matmul(acc[2][:], ones, z[:, 10 + g], start=(g == 0), stop=(g == 1))
                    mm.then_inc(*done("ln_mean", layer))
                elif m == 13:
                    sum_features((layer, "ln"), after("ln_sq", layer), acc[3][:], [ln_sq[:, 0], ln_sq[:, 1]])
                elif m == 15:
                    for g in range(2):
                        pe.wait_ge(*after("ln_out", (layer, g)))
                        turn(acc[2 + g], z[:, 10 + g]).then_inc(*done("sg_vt", (layer, g)))
                elif m == 16:
                    pe.wait_ge(*after("sg_tok", (layer, 1)))
                    for g in range(2):
                        for n in range(4):
                            for e in range(2):
                                s, f = slice(64 * e, 64 * e + 64), (2 * g + e) * 64
                                mm = pe.matmul(acc[2 + g][s, n * P:(n + 1) * P], sg_tok[:, n, f:f + 64],
                                               sg_w[:, 2 * g + e], start=True, stop=True)
                        mm.then_inc(*done("sg_mixed", (layer, g)))

            def first_block_pe():
                pe.wait_ge(*after("c_silu", 0))
                for n in range(ADA_T // 4):
                    for k in range(KT):
                        u = (n * KT + k) // 2
                        if k % 2 == 0:
                            pe.wait_ge(raw_loaded[u % SLOTS], 16 * (u // SLOTS + 1))
                        mm = pe.matmul(mod_bank[n][0:2, :], c_silu[:, k], raw[:, u % SLOTS, k % 2 * 4:k % 2 * 4 + 4],
                                       start=(k == 0), stop=(k == KT - 1))
                        if k % 2:
                            mm.then_inc(*done("product", ("unit", u), *([("ada", n)] if k == KT - 1 else [])))
                    if n == 3:
                        pe.wait_ge(ld["table"], 16)
                        sum_features("x", after("x_sq", "x"), None, [x_sq[:, k] for k in range(KT)])
                    elif n == 4:
                        sum_features("ctx", after("x_sq", "ctx"), mix_bank[0][:, 0:CTX], [ctx_sq[:, k] for k in range(KT)])
                for m in range(ADA_T):
                    pe.wait_ge(*after("mod_rows", m // 4 if m >= 16 else 4))
                    mm = pe.matmul(bank[6][:, 2 * m:2 * m + 2], mod_rows[0:2, m * P:(m + 1) * P], ident[0:2, 0:2],
                                   start=True, stop=True)
                mm.then_inc(*done("mod_turned", 0))
                for m in range(IN1A_T):
                    in_tile("in1a", m, m < C0)
                    if B0 <= m - 2 < C0:
                        turn_conv(m - 2)
                states()
                for m in range(ST):
                    in_tile("in1b", m, False)
                fourier()
                product("four", FT4, FT4, four_hi, four_lo, "four", lambda k: k)
                ssd()
                product("out1", KT, MIX_T, None, None, "mix1", lambda k: k)
                sum_squares("first", "res_sq", "first")

            def in_tile(stage, m, with_ctx):
                t, u = first_tile[stage] + m, first_block[stage] // UNIT + m
                dst, cdst = acc[acc_of[t]][:], ctx_bank[m % 2][:, 0:CTX]
                if counted and t - 4 >= ADA_T:
                    pe.wait_ge(*bank_free(t - 4))
                if with_ctx and m >= 2:
                    pe.wait_ge(*(after("dt_raw", 1) if m == 2 else after("conv", m - 2)))
                elif with_ctx and m == 0:
                    pe.wait_ge(*after("inverse", "ctx"))
                pe.wait_ge(unit_split, u + 1 - WHOLE_UNITS)
                for k in range(KT):
                    if m == 0 and stage == "in1a":
                        pe.wait_ge(*after("in_low", (k, 1)))
                    w_h, w_l = whi[:, u % SLOTS, k], wlo[:, u % SLOTS, k]
                    first, last = k == 0, k == KT - 1
                    pe.matmul(dst, w_h, xhi[:, k], start=first, stop=False)
                    pe.matmul(dst, w_h, xlo[:, k], start=False, stop=False)
                    if with_ctx:
                        pe.matmul(cdst, w_h, ctx_hi[:, k], start=first, stop=False)
                        pe.matmul(cdst, w_h, ctx_lo[:, k], start=False, stop=False)
                        pe.matmul(cdst, w_l, ctx_hi[:, k], start=False, stop=last)
                    mm = pe.matmul(dst, w_l, xhi[:, k], start=False, stop=last)
                mm.then_inc(*done("product", ("unit", u), (stage, m)))

            def turn_conv(m):
                pe.wait_ge(*after("conv_out", m))
                if m > B0:
                    pe.wait_ge(*after("conv_tok", m - 1))
                buf = conv[m % 2]
                if m >= XS0:
                    turn(mix_bank[1], buf)
                for i in range(2):
                    mm = pe.transpose(mix_bank[2][:, i * P:(i + 1) * P], buf[:, SEQ + i * P:SEQ + (i + 1) * P], ident)
                mm.then_inc(*done("conv_turned", m))

            def states():
                pe.wait_ge(*after("dt_bias", 0))
                pe.wait_ge(*after("conv_tok", C0 - 1))
                turn(bank[4], dt[1])
                for i in range(2):
                    mm = pe.transpose(bank[5][:, i * P:(i + 1) * P], dt[1][:, SEQ + i * P:SEQ + (i + 1) * P], ident)
                mm.then_inc(*done("dt_turned", 0))
                for d in range(2):
                    pe.wait_ge(*after("ctx_weighted", d))
                    for g in range(GROUPS):
                        if d:
                            pe.wait_ge(*after("h0", (0, g)))
                        for i in range(2):
                            mm = pe.matmul(bank[4 + g][:, 0:384], ctx_b_tok[:, i, g * P:(g + 1) * P],
                                           ctx_weighted[:, i, g * 384:(g + 1) * 384], start=(i == 0), stop=(i == 1))
                        mm.then_inc(*done("state", (d, g)))

            def fourier():
                pe.wait_ge(ld["dft_c"], 16)
                pe.wait_ge(*after("h0", (1, GROUPS - 1)))
                for i in range(4):
                    if i >= 2:
                        pe.wait_ge(*after("four_tok_out", i - 2))
                    for j in range(FT4):
                        mm = pe.matmul(bank[4 + 2 * (i % 2) + j // 2][:, (j % 2) * 2 * P:(j % 2 + 1) * 2 * P],
                                       u_in[:, j, i * P:(i + 1) * P], dft_c[:, :], start=True, stop=True)
                    mm.then_inc(*done("four_tok", i))
                pe.wait_ge(*after("four_tok_out", 3))
                pe.wait_ge(ld["dft_t"], 16)
                for j in range(FT4):
                    for n in range(8):
                        c, i = n % 2, n // 2
                        mm = pe.matmul(bank[4 + j], four_tok[:, i, j, c], dft_t[:, c, i], start=(n == 0), stop=(n == 7))
                    mm.then_inc(*done("four", j))

            def ssd():
                def rows(hd):
                    if hd >= 2:
                        pe.wait_ge(*after("ssd_row_exp", hd - 2))
                    elif hd == 0:
                        pe.wait_ge(*after("cum_low", 0))
                    for d in range(2):
                        r = d * HEADS + hd
                        one_row = ident_r[:, r:r + 1].broadcast_to([P, P])
                        for n, part in enumerate((cum_hi, cum_lo)):
                            mm = pe.matmul(bank[2 * (hd % 2) + d], one_row, part[:], start=(n == 0), stop=(n == 1))
                    mm.then_inc(*done("ssd_rows", hd))

                def cb(g, tiles):
                    for i in tiles:
                        if i >= 2:
                            pe.wait_ge(*after("cbt", (g, i - 2)))
                        elif i == 0 and g:
                            pe.wait_ge(*after("cbt", (g - 1, 3)))
                            if g >= 2:
                                pe.wait_ge(*after("inverse", ("ssd", g - 2)))
                        pe.matmul(bank[6 + i % 2], b_x[:, g, i * P:(i + 1) * P], c_x[:, g], start=True, stop=True)\
                            .then_inc(*done("cb", (g, i)))

                def y_bank(hd):
                    return bank[4 + hd // 2 % 2][64 * (hd % 2):64 * (hd % 2) + 64, :]

                def y_inner(hd):
                    if hd >= 4 and hd % 2 == 0:
                        pe.wait_ge(*after("ssd_gated", hd // 2 - 2))
                    for half in range(2):
                        pe.wait_ge(*after("ssd_m", (hd, half)))
                        for i in (2 * half, 2 * half + 1):
                            mm = pe.matmul(y_bank(hd), x_tok[:, i, 64 * hd:64 * hd + 64], decay[hd % 2][:, i],
                                           start=(i == 0), stop=False)
                        mm.then_inc(*done("ssd_y_inner", (hd, half)))

                def y_outer(hd):
                    pe.wait_ge(*after("ssd_c", hd))
                    for d in range(2):
                        mm = pe.matmul(y_bank(hd), h0[d][:, 64 * hd:64 * hd + 64], c_dec[hd % 2][:, d],
                                       start=False, stop=(d == 1))
                    mm.then_inc(*done("ssd_y", hd))

                def group_sum(g):
                    sum_features(("ssd", g), after("ssd_sq", (g, 2)), bank[6], [tmp[t][:] for t in range(3)])

                pe.wait_ge(*after("four_low", 3))
                rows(0)
                rows(1)
                cb(0, range(4))
                for hd in range(HEADS):
                    if hd + 2 < HEADS:
                        rows(hd + 2)
                    next_group = (hd + 1) // 6 if hd % 6 == 5 and hd + 1 < HEADS else None
                    if next_group:
                        cb(next_group, range(0, 2))
                    y_inner(hd)
                    if next_group:
                        cb(next_group, range(2, 4))
                    y_outer(hd)
                    if hd % 6 == 2 and hd > 6:
                        group_sum(hd // 6 - 1)
                group_sum(GROUPS - 1)

            first_block_pe()
            for layer in range(DEPTH):
                for s in range(4):
                    q = (layer, s)
                    tile = lambda k: (q, k)
                    pre_sum = lambda: sum_squares(("pre", q), "h_sq", q)
                    if s in (0, 2):
                        product(("gu", layer, s // 2), 2 * FT, KT, xhi, xlo, "x", tile, pre_sum, True)
                        product(("down", layer, s // 2), KT, FT, act_hi, act_lo, "act", tile)
                    elif s == 1:
                        product(("in2", layer), IN_T, KT, xhi, xlo, "x", tile, pre_sum, True,
                                lambda m: (hgrn_step(layer, m), gating_step(layer, m)))
                        attention(layer)
                        product(("out2", layer), KT, KT, xhi, xlo, "mix", lambda k: (layer, k))
                    else:
                        product(("gate", layer), KT, KT, xhi, xlo, "x", tile, pre_sum, True)
                        product(("proj", layer), KT, PLE_T, ple_hi, ple_lo, "ple", lambda k: layer)
                    sum_squares(("post", q), "y_sq", q)
    return ev.values, ev.freed


def blocks_of(w, rows=None):
    k, m = w.shape[0] // P, w.shape[1] // P
    return w.reshape(k, P, m, P).transpose(2, 0, 1, 3).reshape(m * k, P, P)


def columns(x):
    return x.reshape(-1, P).T


def feature_major(x):
    t, f = x.shape
    return np.ascontiguousarray(x.T.reshape(f // P, P, t).transpose(1, 0, 2).reshape(P, -1))


HEAD_ORDER = np.concatenate([np.r_[64 * t:64 * t + 64, 64 * (4 + t):64 * (4 + t) + 64] for t in range(4)])


def lay_out_second(i, into):
    weights = []
    order = np.r_[0:1024, 1792:2304, 1536:1792, 1024 + HEAD_ORDER]
    order_out = np.r_[0:256, 768:1024, 256 + HEAD_ORDER]
    for l in range(DEPTH):
        for s in range(2):
            gu = blocks_of(i[f"ffn{s + 1}_gate_up_2"][l]).reshape(2, FT, KT, P, P)
            weights.append(gu.transpose(1, 0, 2, 3, 4).reshape(-1, P, P))
            weights.append(blocks_of(i[f"ffn{s + 1}_down_2"][l]))
            if s == 0:
                weights.append(blocks_of(i["w_in_2"][l][:, order]))
                weights.append(blocks_of(i["w_out_2"][l][order_out]))
        weights.append(blocks_of(i["ple_gate_2"][l]))
        weights.append(blocks_of(i["ple_proj_2"][l]))
    par = np.zeros((DEPTH, P, P2_COLS), np.float32)
    mix = np.zeros((DEPTH, P, M2_COLS), np.float32)
    for l in range(DEPTH):
        par[l, :, P2_NORM:P2_NORM + 64] = columns(i["norm_gains_2"][l].reshape(-1))
        par[l, :, P2_HG] = np.tile(i["hgrn_norm_gain_2"][l], 2)
        par[l, :, P2_LB:P2_LB + 4] = columns(i["hgrn_lb_logits_2"].reshape(-1))
        par[l, :, P2_LN:P2_LN + 2] = columns(i["sg_ln_gain_2"][l])
        par[l, :, P2_SINK:P2_SINK + 8] = i["attn_sinks_2"][l].reshape(2, 4).T.reshape(-1)[None]
        mix[l, :, :2 * P] = np.repeat(i["sg_spatial_b_2"][l].reshape(2, 2, P).transpose(1, 0, 2), 64, 0).reshape(P, -1)
        mix[l, :, 2 * P:] = i["sg_spatial_w_2"][l].transpose(2, 0, 1).reshape(P, -1)
    into["par2"], into["mixpar"] = par, mix
    into["ple"] = np.stack([feature_major(i["p_2"][l, 0]) for l in range(DEPTH)])
    into["positions"] = i["positions_2"]
    return weights


def lay_out_first(i, into):
    w = i["w_in"][0]
    u, zf, zs, xs, b, c, dt = np.split(w, np.cumsum([D_FOUR, D_FOUR, D_SSD, D_SSD, 512, 512]), axis=1)
    dt = np.concatenate([dt, np.zeros((D, P - DT_ROWS), np.float32)], axis=1)
    ada = blocks_of(i["w_ada"][0]).reshape(ADA_T // 4, 4, KT, P, P).transpose(0, 2, 1, 3, 4).reshape(-1, P, P)
    weights = [ada, blocks_of(np.concatenate([dt, b, xs, c, u, zf, zs], axis=1)),
               blocks_of(i["w_fourier"][0]), blocks_of(i["w_out"][0])]
    par = np.zeros((P, P1_COLS), np.float32)
    par[:, P1_NORM:P1_NORM + KT] = columns(i["norm_w"][0])
    par[:, P1_ADA:P1_ADA + ADA_T] = columns(i["b_ada"][0])
    order = np.r_[D_SSD:D_SSD + 512, 0:D_SSD, D_SSD + 512:D_SSD + 1024]
    taps = i["conv_w"][0].reshape(9, -1)[:, order]
    par[:, P1_CONV:P1_CONV + 180] = taps.reshape(9, 20, P).transpose(2, 1, 0).reshape(P, 180)
    par[:, P1_CB:P1_CB + 20] = columns(i["conv_b"][0][order])
    par[:, P1_SSD:P1_SSD + ST] = columns(i["ssd_norm_w"][0])
    par[:, P1_BF:P1_BF + FT4] = columns(i["b_fourier"][0])
    par[:, P1_FIN:P1_FIN + KT] = columns(i["final_norm_w"])
    par[:, P1_C:P1_C + 2 * KT] = np.stack([columns(i["c"][0]), columns(i["c_ctx"])], 2).reshape(P, -1)
    par[:, P1_D:P1_D + HEADS] = i["d_skip"][0][None]
    par[:DT_ROWS, P1_DTB] = i["dt_bias"][0].reshape(-1)
    par[:DT_ROWS, P1_DTB + 1] = i["a_log"][0].reshape(-1)
    into["par1"] = par
    into["x"], into["ctx"] = feature_major(i["x"][0]), feature_major(i["ctx"][0])
    return weights


def stream_of(weights, units):
    w = np.concatenate(weights)
    pad = units * UNIT - len(w)
    if pad:
        w = np.concatenate([w, np.zeros((pad, P, P), np.float32)])
    return np.ascontiguousarray(w.reshape(units, UNIT, P, P).transpose(0, 2, 1, 3))


def kernel(**inputs):
    import concourse.bacc as bacc
    from concourse.bass_utils import run_bass_kernel_spmd

    i = {name: np.asarray(value) for name, value in inputs.items()}
    arrays = {}
    weights = lay_out_first(i, arrays) + lay_out_second(i, arrays)
    units = stream_plan(STREAM)[2]
    arrays["stream"] = stream_of(weights, units)
    arrays["table"], arrays["masks"], arrays["dft_c"], arrays["dft_t"] = fixed_tables()

    def program(counted):
        nc = bacc.Bacc("TRN2", target_bir_lowering=False, num_devices=1)
        a = {name: nc.dram_tensor(f"in_{name}", v.shape, mybir.dt.from_np(v.dtype), kind="ExternalInput").ap()
             for name, v in arrays.items()}
        out = nc.dram_tensor("out", (P, KT * SEQ), F32, kind="ExternalOutput").ap()
        return nc, build(nc, a, out.rearrange("p (k t) -> p k t", t=SEQ), counted, STREAM)

    _, counted = program(None)
    nc, _ = program(counted)
    r = run_bass_kernel_spmd(nc, [{f"in_{name}": v for name, v in arrays.items()}], core_ids=[0])
    got = r.results[0]["out"].reshape(P, KT, SEQ)
    return np.ascontiguousarray(got.transpose(2, 1, 0).reshape(1, SEQ, D))
```
